# Optimizing a Trainium2 kernel written in Bass

```python
import math
import jax, jax.numpy as jnp
from jax import lax
import numpy as np

D_MODEL = 1024
BATCH = 1
SEQ = 512
DEPTH = 2
DEC_BATCH = 1
DEC_SEQ = 32
PAST_LEN = 128

CHUNK = 64
Q_BLOCK = 128
N_AB = (DEPTH + 1) // 2
N_C = DEPTH // 2
GLA_H = 4
GLA_DK = 64
GLA_DV = 128
GLA_LR = 16
GLA_TAU = 16.0
GDN_H = 4
GDN_DK = 128
GDN_DV = 128
CONV_W = 4
GDN_CONV_DIM = GDN_H * (2 * GDN_DK + GDN_DV)
AB_IN_WIDTHS = (GLA_H * GLA_DK, GLA_H * GLA_DK, GLA_H * GLA_DV, GLA_LR, GLA_H * GLA_DV,
                GDN_CONV_DIM, GDN_H, GDN_H, GDN_H * GDN_DV)
AB_IN = 3608
AB_OUT = GLA_H * GLA_DV + GDN_H * GDN_DV
MLA_H = 16
MLA_NOPE = 64
MLA_ROPE = 32
MLA_V = 64
MLA_Q_RANK = 384
MLA_KV_RANK = 256
MLA_IN = MLA_Q_RANK + MLA_KV_RANK + MLA_ROPE
ROPE_THETA = 10000.0
N_GROUPS = 4
EXPERTS_PER_GROUP = 8
N_EXPERTS = N_GROUPS * EXPERTS_PER_GROUP
TOP_K = 2
D_EXPERT = 512
MOE_BLOCK = 128
EPS = 1e-6

kernel_name = 'hybrid_stream_gla_gdn_mla_hmoe_step'

def rmsnorm(x, w):
    xf = x.astype(jnp.float32)
    y = xf * lax.rsqrt(jnp.mean(xf * xf, axis=-1, keepdims=True) + EPS)
    return (y * w.astype(jnp.float32)).astype(x.dtype)

def l2norm(x):
    return x * lax.rsqrt(jnp.sum(x * x, axis=-1, keepdims=True) + EPS)

def ada_modulation(c, w, b):
    m = (jax.nn.silu(c) @ w + b)[:, None, :]
    return jnp.split(m, 3, axis=-1)

def to_heads(x, n):
    b, l, w = x.shape
    return x.reshape(b, l, n, w // n).transpose(0, 2, 1, 3)

def from_heads(x):
    b, n, l, d = x.shape
    return x.transpose(0, 2, 1, 3).reshape(b, l, n * d)

def rope(x, pos):
    half = x.shape[-1] // 2
    inv = jnp.exp(-math.log(ROPE_THETA) * jnp.arange(half, dtype=jnp.float32) / half)
    ang = pos.astype(jnp.float32)[:, None] * inv[None, :]
    if x.ndim == 4:
        ang = ang[:, None, :]
    cos, sin = jnp.cos(ang), jnp.sin(ang)
    xf = x.astype(jnp.float32)
    x1, x2 = xf[..., :half], xf[..., half:]
    return jnp.concatenate([x1 * cos - x2 * sin, x1 * sin + x2 * cos], axis=-1).astype(x.dtype)

def chunk_scan(step, s0, xs):
    b, h, l = xs[0].shape[:3]
    nc = max(l // CHUNK, 1)
    lc = l // nc

    def split(a):
        return jnp.moveaxis(a.reshape(a.shape[:2] + (nc, lc) + a.shape[3:]), 2, 0)

    s, out = lax.scan(lambda s, x: step(s, *x), s0.astype(jnp.float32), tuple(split(a) for a in xs))
    out = jnp.moveaxis(out, 0, 2)
    return s, out.reshape((b, h, l) + out.shape[4:])

def gla_chunk(S, q, k, v, la):
    L = q.shape[2]
    b = jnp.cumsum(la, axis=2)
    incl = jnp.tril(jnp.ones((L, L), bool))[:, :, None]
    dec = jnp.exp(jnp.where(incl, b[:, :, :, None, :] - b[:, :, None, :, :], -jnp.inf))
    att = jnp.einsum('bhid,bhjd,bhijd->bhij', q, k, dec)
    o = jnp.einsum('bhij,bhjv->bhiv', att, v) + jnp.einsum('bhid,bhdv->bhiv', q * jnp.exp(b), S)
    b_last = b[:, :, -1:, :]
    S_new = jnp.exp(b_last[:, :, 0, :])[..., None] * S + jnp.einsum('bhjd,bhjv->bhdv', k * jnp.exp(b_last - b), v)
    return S_new, o

def gdn_chunk(S, q, k, v, g, beta):
    L = q.shape[2]
    gam = jnp.cumsum(g, axis=-1)
    incl = jnp.tril(jnp.ones((L, L), bool))
    strict = jnp.tril(jnp.ones((L, L), bool), -1)
    dec = jnp.exp(jnp.where(incl, gam[..., :, None] - gam[..., None, :], -jnp.inf))
    kk = jnp.einsum('bhid,bhjd->bhij', k, k)
    a_mat = jnp.eye(L, dtype=jnp.float32) + jnp.where(strict, beta[..., :, None] * kk * dec, 0.0)
    rhs = jnp.concatenate([v * beta[..., None], k * (beta * jnp.exp(gam))[..., None]], axis=-1)
    sol = lax.linalg.triangular_solve(a_mat, rhs, left_side=True, lower=True)
    u, w = sol[..., :GDN_DV], sol[..., GDN_DV:]
    delta = u - jnp.einsum('bhlk,bhkv->bhlv', w, S)
    qk = jnp.einsum('bhid,bhjd->bhij', q, k) * dec
    o = jnp.einsum('bhik,bhkv->bhiv', q * jnp.exp(gam)[..., None], S) + jnp.einsum('bhij,bhjv->bhiv', qk, delta)
    g_last = gam[..., -1:]
    S_new = jnp.exp(g_last)[..., None] * S + jnp.einsum('bhjk,bhjv->bhkv', k * jnp.exp(g_last - gam)[..., None], delta)
    return S_new, o

def ab_mixer(h, gla_s0, gdn_s0, conv_hist, w_in, w_alpha, b_alpha, gla_nw, conv_w, a_log, dt_bias, gdn_nw, w_out):
    B, L, _ = h.shape
    z = h @ w_in
    offs = np.cumsum(AB_IN_WIDTHS)[:-1].tolist()
    gq, gk, gv, glr, gr, qkv, ga, gb, gg = jnp.split(z, offs, axis=-1)
    q = to_heads(gq, GLA_H).astype(jnp.float32) * GLA_DK ** -0.5
    k = to_heads(gk, GLA_H).astype(jnp.float32)
    v = to_heads(gv, GLA_H).astype(jnp.float32)
    la = jax.nn.log_sigmoid((glr @ w_alpha + b_alpha).astype(jnp.float32)) / GLA_TAU
    la = to_heads(la, GLA_H)
    gla_s, o_gla = chunk_scan(gla_chunk, gla_s0, (q, k, v, la))
    o_gla = from_heads(rmsnorm(o_gla.astype(h.dtype), gla_nw)) * jax.nn.silu(gr)
    xc = jnp.concatenate([conv_hist.astype(qkv.dtype), qkv], axis=1)
    new_conv = xc[:, -(CONV_W - 1):, :]
    conv = jax.nn.silu(sum(xc[:, i:i + L, :] * conv_w[i] for i in range(CONV_W)))
    q2, k2, v2 = jnp.split(conv, [GDN_H * GDN_DK, 2 * GDN_H * GDN_DK], axis=-1)
    q2 = l2norm(to_heads(q2, GDN_H).astype(jnp.float32)) * GDN_DK ** -0.5
    k2 = l2norm(to_heads(k2, GDN_H).astype(jnp.float32))
    v2 = to_heads(v2, GDN_H).astype(jnp.float32)
    beta = jax.nn.sigmoid(gb.astype(jnp.float32)).transpose(0, 2, 1)
    g = (-jnp.exp(a_log.astype(jnp.float32)) *
         jax.nn.softplus(ga.astype(jnp.float32) + dt_bias.astype(jnp.float32))).transpose(0, 2, 1)
    gdn_s, o_gdn = chunk_scan(gdn_chunk, gdn_s0, (q2, k2, v2, g, beta))
    o_gdn = from_heads(rmsnorm(o_gdn.astype(h.dtype), gdn_nw)) * jax.nn.silu(gg)
    out = jnp.concatenate([o_gla, o_gdn], axis=-1) @ w_out
    return out, gla_s, gdn_s, new_conv

def mla_attend(q_nope, q_rope, k_nope, k_rope, v, q_pos, k_pos):
    scale = (MLA_NOPE + MLA_ROPE) ** -0.5
    k_chunk = k_pos // CHUNK

    def block(args):
        qn, qr, qp = args
        s = (jnp.einsum('bqhd,bkhd->bhqk', qn, k_nope) + jnp.einsum('bqhd,bkd->bhqk', qr, k_rope)).astype(jnp.float32)
        mask = (qp // CHUNK)[:, None] >= k_chunk[None, :]
        p = jax.nn.softmax(jnp.where(mask, s * scale, -jnp.inf), axis=-1).astype(v.dtype)
        return jnp.einsum('bhqk,bkhd->bqhd', p, v)

    B, L = q_nope.shape[:2]
    if L <= Q_BLOCK:
        return block((q_nope, q_rope, q_pos))
    nb = L // Q_BLOCK

    def to_blocks(a):
        return jnp.moveaxis(a.reshape((B, nb, Q_BLOCK) + a.shape[2:]), 1, 0)

    out = lax.map(block, (to_blocks(q_nope), to_blocks(q_rope), q_pos.reshape(nb, Q_BLOCK)))
    return jnp.moveaxis(out, 0, 1).reshape((B, L) + out.shape[3:])

def mla_mixer(h, q_pos, past_ckv, past_kr, w_in, q_nw, w_uq, kv_nw, w_ukv, w_out):
    B, L, _ = h.shape
    cq, ckv, kr = jnp.split(h @ w_in, [MLA_Q_RANK, MLA_Q_RANK + MLA_KV_RANK], axis=-1)
    q = (rmsnorm(cq, q_nw) @ w_uq).reshape(B, L, MLA_H, MLA_NOPE + MLA_ROPE)
    q_nope, q_rope = q[..., :MLA_NOPE], rope(q[..., MLA_NOPE:], q_pos)
    ckv = rmsnorm(ckv, kv_nw)
    kr = rope(kr, q_pos)
    if past_ckv is None:
        ckv_all, kr_all, k_pos = ckv, kr, q_pos
    else:
        ckv_all = jnp.concatenate([past_ckv.astype(ckv.dtype), ckv], axis=1)
        kr_all = jnp.concatenate([past_kr.astype(kr.dtype), kr], axis=1)
        k_pos = jnp.arange(ckv_all.shape[1], dtype=jnp.int32)
    kv = (ckv_all @ w_ukv).reshape(B, ckv_all.shape[1], MLA_H, MLA_NOPE + MLA_V)
    o = mla_attend(q_nope, q_rope, kv[..., :MLA_NOPE], kr_all, kv[..., MLA_NOPE:], q_pos, k_pos)
    return o.reshape(B, L, MLA_H * MLA_V) @ w_out, ckv, kr

def hier_moe(h, w_group, b_group, w_expert, b_expert, w1, w3, w2):
    T, D = h.shape
    tok = jnp.arange(T, dtype=jnp.int32)
    gl = (h @ w_group).astype(jnp.float32) + b_group.astype(jnp.float32)
    g_sel = jnp.argmax(gl, axis=-1).astype(jnp.int32)
    p_g = jax.nn.softmax(gl, axis=-1)[tok, g_sel]
    el = ((h @ w_expert).astype(jnp.float32) + b_expert.astype(jnp.float32)).reshape(T, N_GROUPS, EXPERTS_PER_GROUP)
    el = el[tok, g_sel]
    top_v, top_i = lax.top_k(el, TOP_K)
    w_tok = p_g[:, None] * jax.nn.softmax(top_v, axis=-1)
    e_id = g_sel[:, None] * EXPERTS_PER_GROUP + top_i.astype(jnp.int32)
    A = T * TOP_K
    e_flat = e_id.reshape(A)
    t_flat = jnp.repeat(tok, TOP_K)
    w_flat = w_tok.reshape(A)
    order = jnp.argsort(e_flat)
    e_sorted = e_flat[order]
    counts = jnp.bincount(e_flat, length=N_EXPERTS)
    padded = (counts + MOE_BLOCK - 1) // MOE_BLOCK * MOE_BLOCK
    start = jnp.cumsum(counts) - counts
    pend = jnp.cumsum(padded)
    pstart = pend - padded
    dest = pstart[e_sorted] + jnp.arange(A, dtype=jnp.int32) - start[e_sorted]
    nb = -(-(A + N_EXPERTS * (MOE_BLOCK - 1)) // MOE_BLOCK)
    P = nb * MOE_BLOCK
    row_tok = jnp.zeros((P,), jnp.int32).at[dest].set(t_flat[order])
    row_w = jnp.zeros((P,), h.dtype).at[dest].set(w_flat[order].astype(h.dtype))
    blk_e = jnp.clip(jnp.searchsorted(pend, jnp.arange(nb, dtype=jnp.int32) * MOE_BLOCK, side='right'),
                     0, N_EXPERTS - 1)
    xg = h[row_tok].reshape(nb, MOE_BLOCK, D)

    def expert_block(args):
        xb, e = args
        return (jax.nn.silu(xb @ w1[e]) * (xb @ w3[e])) @ w2[e]

    yb = lax.map(expert_block, (xg, blk_e)).reshape(P, D)
    return jnp.zeros((T, D), h.dtype).at[row_tok].add(yb * row_w[:, None])

def trunk(x, c, pos0, gla_s, gdn_s, conv_s, past_ckv, past_kr, p):
    B, L, D = x.shape
    q_pos = pos0 + jnp.arange(L, dtype=jnp.int32)
    new_gla, new_gdn, new_conv, new_ckv, new_kr = [], [], [], [], []
    for l in range(DEPTH):
        i = l // 2
        shift, scale, gate = ada_modulation(c, p['ada_w'][l, 0], p['ada_b'][l, 0])
        h = rmsnorm(x, p['norm_w'][l, 0]) * (1 + scale) + shift
        if l % 2 == 0:
            out, s1, s2, cv = ab_mixer(h, gla_s[i], gdn_s[i], conv_s[i], p['ab_w_in'][i], p['gla_w_alpha'][i],
                                       p['gla_b_alpha'][i], p['gla_norm_w'][i], p['gdn_conv_w'][i],
                                       p['gdn_a_log'][i], p['gdn_dt_bias'][i], p['gdn_norm_w'][i], p['ab_w_out'][i])
            new_gla.append(s1)
            new_gdn.append(s2)
            new_conv.append(cv)
        else:
            out, ckv, kr = mla_mixer(h, q_pos, None if past_ckv is None else past_ckv[i],
                                     None if past_kr is None else past_kr[i], p['mla_w_in'][i],
                                     p['mla_q_norm_w'][i], p['mla_w_uq'][i], p['mla_kv_norm_w'][i],
                                     p['mla_w_ukv'][i], p['mla_w_out'][i])
            new_ckv.append(ckv)
            new_kr.append(kr)
        x = x + gate * out
        shift, scale, gate = ada_modulation(c, p['ada_w'][l, 1], p['ada_b'][l, 1])
        h = rmsnorm(x, p['norm_w'][l, 1]) * (1 + scale) + shift
        y = hier_moe(h.reshape(B * L, D), p['moe_w_group'][l], p['moe_b_group'][l], p['moe_w_expert'][l],
                     p['moe_b_expert'][l], p['moe_w1'][l], p['moe_w3'][l], p['moe_w2'][l])
        x = x + gate * y.reshape(B, L, D)
    y = rmsnorm(x, p['final_norm_w'])
    return (y, jnp.stack(new_gla), jnp.stack(new_gdn), jnp.stack(new_conv), jnp.stack(new_ckv), jnp.stack(new_kr))

def setup_inputs(seed: int = 0) -> dict:
    key = jax.random.key(seed)
    ks = iter(jax.random.split(key, 40))

    def nrm(shape, scale):
        return jax.random.normal(next(ks), shape, jnp.float32) * scale

    def gain(shape):
        return 1.0 + nrm(shape, 0.05)

    D = D_MODEL
    dt = jnp.exp(jax.random.uniform(next(ks), (N_AB, GDN_H), jnp.float32, math.log(1e-3), math.log(1e-1)))
    return {
        'x_prompt': nrm((BATCH, SEQ, D), 1.0),
        'x_sample': nrm((DEC_BATCH, DEC_SEQ, D), 1.0),
        'state_gla': nrm((N_AB, DEC_BATCH, GLA_H, GLA_DK, GLA_DV), 0.1),
        'state_gdn': nrm((N_AB, DEC_BATCH, GDN_H, GDN_DK, GDN_DV), 0.1),
        'state_gdn_conv': nrm((N_AB, DEC_BATCH, CONV_W - 1, GDN_CONV_DIM), 1.0),
        'cache_mla_ckv': nrm((N_C, DEC_BATCH, PAST_LEN, MLA_KV_RANK), 1.0),
        'cache_mla_krope': nrm((N_C, DEC_BATCH, PAST_LEN, MLA_ROPE), 1.0),
        'c_prompt': nrm((BATCH, D), 1.0),
        'c_sample': nrm((DEC_BATCH, D), 1.0),
        'ada_w': nrm((DEPTH, 2, D, 3 * D), 0.5 * D ** -0.5),
        'ada_b': nrm((DEPTH, 2, 3 * D), 0.02),
        'norm_w': gain((DEPTH, 2, D)),
        'final_norm_w': gain((D,)),
        'ab_w_in': nrm((N_AB, D, AB_IN), D ** -0.5),
        'gla_w_alpha': nrm((N_AB, GLA_LR, GLA_H * GLA_DK), GLA_LR ** -0.5),
        'gla_b_alpha': nrm((N_AB, GLA_H * GLA_DK), 0.1),
        'gla_norm_w': gain((N_AB, GLA_DV)),
        'gdn_conv_w': nrm((N_AB, CONV_W, GDN_CONV_DIM), CONV_W ** -0.5),
        'gdn_a_log': jnp.log(jax.random.uniform(next(ks), (N_AB, GDN_H), jnp.float32, 1.0, 16.0)),
        'gdn_dt_bias': dt + jnp.log(-jnp.expm1(-dt)),
        'gdn_norm_w': gain((N_AB, GDN_DV)),
        'ab_w_out': nrm((N_AB, AB_OUT, D), AB_OUT ** -0.5),
        'mla_w_in': nrm((N_C, D, MLA_IN), D ** -0.5),
        'mla_q_norm_w': gain((N_C, MLA_Q_RANK)),
        'mla_w_uq': nrm((N_C, MLA_Q_RANK, MLA_H * (MLA_NOPE + MLA_ROPE)), MLA_Q_RANK ** -0.5),
        'mla_kv_norm_w': gain((N_C, MLA_KV_RANK)),
        'mla_w_ukv': nrm((N_C, MLA_KV_RANK, MLA_H * (MLA_NOPE + MLA_V)), MLA_KV_RANK ** -0.5),
        'mla_w_out': nrm((N_C, MLA_H * MLA_V, D), (MLA_H * MLA_V) ** -0.5),
        'moe_w_group': nrm((DEPTH, D, N_GROUPS), D ** -0.5),
        'moe_b_group': nrm((DEPTH, N_GROUPS), 0.01),
        'moe_w_expert': nrm((DEPTH, D, N_EXPERTS), D ** -0.5),
        'moe_b_expert': nrm((DEPTH, N_EXPERTS), 0.01),
        'moe_w1': nrm((DEPTH, N_EXPERTS, D, D_EXPERT), D ** -0.5),
        'moe_w3': nrm((DEPTH, N_EXPERTS, D, D_EXPERT), D ** -0.5),
        'moe_w2': nrm((DEPTH, N_EXPERTS, D_EXPERT, D), D_EXPERT ** -0.5),
    }

def reference(x_prompt, x_sample, state_gla, state_gdn, state_gdn_conv, cache_mla_ckv, cache_mla_krope,
              c_prompt, c_sample, ada_w, ada_b, norm_w, final_norm_w, ab_w_in, gla_w_alpha, gla_b_alpha,
              gla_norm_w, gdn_conv_w, gdn_a_log, gdn_dt_bias, gdn_norm_w, ab_w_out, mla_w_in, mla_q_norm_w,
              mla_w_uq, mla_kv_norm_w, mla_w_ukv, mla_w_out, moe_w_group, moe_b_group, moe_w_expert,
              moe_b_expert, moe_w1, moe_w3, moe_w2):
    p = dict(ada_w=ada_w, ada_b=ada_b, norm_w=norm_w, final_norm_w=final_norm_w, ab_w_in=ab_w_in,
             gla_w_alpha=gla_w_alpha, gla_b_alpha=gla_b_alpha, gla_norm_w=gla_norm_w, gdn_conv_w=gdn_conv_w,
             gdn_a_log=gdn_a_log, gdn_dt_bias=gdn_dt_bias, gdn_norm_w=gdn_norm_w, ab_w_out=ab_w_out,
             mla_w_in=mla_w_in, mla_q_norm_w=mla_q_norm_w, mla_w_uq=mla_w_uq, mla_kv_norm_w=mla_kv_norm_w,
             mla_w_ukv=mla_w_ukv, mla_w_out=mla_w_out, moe_w_group=moe_w_group, moe_b_group=moe_b_group,
             moe_w_expert=moe_w_expert, moe_b_expert=moe_b_expert, moe_w1=moe_w1, moe_w3=moe_w3, moe_w2=moe_w2)
    bp = x_prompt.shape[0]
    y_prompt, gla_p, gdn_p, conv_p, ckv_p, kr_p = trunk(
        x_prompt, c_prompt, 0,
        jnp.zeros((N_AB, bp, GLA_H, GLA_DK, GLA_DV), jnp.float32),
        jnp.zeros((N_AB, bp, GDN_H, GDN_DK, GDN_DV), jnp.float32),
        jnp.zeros((N_AB, bp, CONV_W - 1, GDN_CONV_DIM), x_prompt.dtype),
        None, None, p)
    y_sample, gla_s, gdn_s, conv_s, ckv_s, kr_s = trunk(
        x_sample, c_sample, cache_mla_ckv.shape[2], state_gla, state_gdn, state_gdn_conv,
        cache_mla_ckv, cache_mla_krope, p)
    return (y_prompt, y_sample, gla_p, gdn_p, conv_p, ckv_p, kr_p, gla_s, gdn_s, conv_s, ckv_s, kr_s)


_drawn_inputs = setup_inputs


def setup_inputs(seed=0):
    import zlib

    import numpy as np

    out = dict(_drawn_inputs(seed))
    spreads = {}
    factors = {'state_gla': 4.266,
     'cache_mla_krope': 3.181,
     'gla_norm_w': 3.749,
     'gdn_norm_w': 5.719,
     'mla_q_norm_w': 8.0,
     'moe_b_group': 24.236,
     'moe_b_expert': 23.219}
    for name, (base, spread) in spreads.items():
        noise = np.random.default_rng([zlib.crc32(name.encode()), seed]).standard_normal(out[name].shape)
        drawn = base * np.exp(spread * noise) if base else spread * noise
        out[name] = __import__('jax').numpy.asarray(drawn.astype(out[name].dtype))
    for name, factor in factors.items():
        out[name] = (out[name] * factor).astype(out[name].dtype)
    return out
```

```python
from contextlib import ExitStack
import math

import numpy as np
import concourse.bass as bass
from concourse import mybir

F32 = mybir.dt.float32
I32 = mybir.dt.int32
ALU = mybir.AluOpType
ACT = mybir.ActivationFunctionType
AX = mybir.AxisListType

P = 128
D = 1024
KT = D // P
SEQ, DSEQ, PAST = 512, 32, 128
TOK = SEQ + DSEQ
NT = SEQ // P + 1
EPS = 1e-6
GH, GDK, GDV, GLR = 4, 64, 128, 16
NH, DK, DV = 4, 128, 128
CW = 4
CONV = NH * (2 * DK + DV)
MH, NOPE, ROPE, MV = 16, 64, 32, 64
QR, KVR = 384, 256
NG, EG = 4, 8
NE = NG * EG
DE = 512
LEV = 7
CAP = 64
NOV = 16
SLOTS = (NE + NOV) * CAP
RING = 6
CH = 4096

C_GV, C_LR = 2 * GH * GDK, 2 * GH * GDK + GH * GDV
C_GR = C_LR + GLR
C_QKV = C_GR + GH * GDV
C_GA = C_QKV + CONV
C_GG = C_GA + 2 * NH

K_ID, K_U, K_SU, K_ONE = 0, P, 2 * P, 3 * P
K_MT = 4 * P
K_ML = K_MT + (LEV + 1) * P
K_CS = K_ML + LEV * P
K_EC = K_CS + NT * ROPE
K_DG = K_EC + NE
K_DE = K_DG + NG
K_B = K_DE + EG
K_AM = K_B + NOV
K_END = K_AM + P + 64


def constants():
    c = np.zeros((P, K_END), np.float32)
    i = np.arange(P)
    c[:, K_ID:K_ID + P] = np.eye(P)
    c[:, K_U:K_U + P] = i[:, None] <= i[None, :]
    c[:, K_SU:K_SU + P] = i[:, None] < i[None, :]
    c[:, K_ONE:K_ONE + P] = 1.0
    for l in range(LEV):
        m = 1 << l
        blk = i // m
        mt = (blk[None, :] == blk[:, None] + 1) & (blk[:, None] % 2 == 0)
        c[:, K_MT + l * P:K_MT + (l + 1) * P] = mt
        c[:, K_ML + l * P:K_ML + (l + 1) * P] = mt.T
    c[:, K_MT + LEV * P:K_MT + (LEV + 1) * P] = np.eye(P)
    half = ROPE // 2
    inv = np.exp(np.float32(-math.log(10000.0)) * np.arange(half, dtype=np.float32) / np.float32(half)).astype(np.float32)
    for t in range(NT):
        pos = (i + t * P if t < NT - 1 else PAST + i).astype(np.float32)
        ang = pos[:, None] * inv[None, :]
        c[:, K_CS + t * ROPE:K_CS + t * ROPE + half] = np.cos(ang)
        c[:, K_CS + t * ROPE + half:K_CS + (t + 1) * ROPE] = np.sin(ang)
    c[:, K_EC:K_EC + NE] = np.arange(NE) * CAP
    c[:, K_DG:K_DG + NG] = NG - np.arange(NG)
    c[:, K_DE:K_DE + EG] = EG - np.arange(EG)
    c[:, K_B:K_B + NOV] = np.arange(NOV)
    c[0, K_AM:K_AM + 64] = 1.0
    c[0, K_AM + P:K_AM + P + 64] = -1e30
    return c


def width(t):
    return P if t < NT - 1 else DSEQ


class Chain:

    def __init__(self, eng, sem, at):
        self.eng, self.sem, self.n = eng, sem, at

    def __call__(self, ins):
        self.n += 1
        ins.then_inc(self.sem, 1)
        self.eng.wait_ge(self.sem, self.n)


class Prog:

    def __init__(self, nc, ctx, io):
        self.nc, self.ctx, self.io = nc, ctx, io
        self.cst = ctx.enter_context(nc.sbuf_tensor("cst", [P, K_END], F32))
        self.ring = ctx.enter_context(nc.sbuf_tensor("ring", [P, RING, CH], F32))
        self.eps = ctx.enter_context(nc.sbuf_tensor("eps", [P, 1], F32))
        self.arrived = [ctx.enter_context(nc.semaphore(f"arrived{j}")) for j in range(RING)]
        self.free_when = {}
        self.chains = {e: ctx.enter_context(nc.semaphore(f"chain_{e}")) for e in ("act", "dve", "pool")}
        self.chained = {e: 0 for e in self.chains}
        self.n_load = 0
        self.phase_sems = []
        self.plan = []

    def semaphore(self, name):
        self.phase_sems.append(self.nc.alloc_semaphore(name))
        return self.phase_sems[-1]

    def end_phase(self):
        self.free_when = {n: None for n in self.free_when}
        if len(self.phase_sems) > 120:
            self.nc.clear_and_free_semaphores(self.phase_sems)
            self.nc.all_engine_barrier()
            self.phase_sems = []

    def chain(self, eng, name):
        return Chain(eng, self.chains[name], self.chained[name])

    def done(self, chain, name):
        self.chained[name] = chain.n

    def c(self, at, n, rows=P):
        return self.cst[0:rows, at:at + n]

    def load(self, sp, n):
        src, shape = self.plan[n]
        if n >= RING and self.free_when[n - RING]:
            sp.wait_ge(*self.free_when[n - RING])
        size = shape[1] * shape[2]
        dst = self.ring[0:shape[0], n % RING, 0:size].rearrange("p (k n) -> p k n", k=shape[1])
        sp.dma_start(dst, src).then_inc(self.arrived[n % RING], 16)

    def stream(self, sp, upto):
        while self.n_load < min(upto + RING, len(self.plan)):
            self.load(sp, self.n_load)
            self.n_load += 1

    def chunk(self, pe, n):
        _, shape = self.plan[n]
        pe.wait_ge(self.arrived[n % RING], 16 * (n // RING + 1))
        return self.ring[0:shape[0], n % RING, 0:shape[1] * shape[2]].rearrange("p (k n) -> p k n", k=shape[1])


def kview(w, a, b):
    return w[:, a:b].rearrange("(p k) n -> p k n", k=KT)


def make_plan(g):
    plan = []
    for s in range(4):
        w = g["ada_w"][s // 2, s % 2]
        plan += [(kview(w, 512 * j, 512 * j + 512), (P, KT, 512)) for j in range(6)]
    w = g["ab_w_in"][0]
    cols = [(0, 512), (C_GV, C_LR), (C_LR, C_GR), (C_GA, C_GG), (C_GR, C_QKV),
            (C_QKV, C_QKV + 512), (C_QKV + 512, C_QKV + 1024), (C_QKV + 1024, C_GA), (C_GG, C_GG + 512)]
    plan += [(kview(w, a, b), (P, KT, b - a)) for a, b in cols]
    wo = g["ab_w_out"][0].rearrange("(k p) n -> p k n", p=P)
    plan += [(wo[:, :, 512 * j:512 * j + 512], (P, KT, 512)) for j in range(2)]

    def moe(l):
        for e in range(NE):
            for w in (g["moe_w1"], g["moe_w3"]):
                plan.append((kview(w[l, e], 0, DE), (P, KT, DE)))
            plan.append((g["moe_w2"][l, e].rearrange("(j p) n -> p j n", p=P), (P, DE // P, D)))
    moe(0)
    w = g["mla_w_in"][0]
    plan += [(kview(w, 0, QR), (P, KT, QR)), (kview(w, QR, QR + KVR + ROPE), (P, KT, KVR + ROPE))]
    w = g["mla_w_uq"][0].rearrange("(k p) n -> p k n", p=P)
    plan += [(w[:, :, 768 * j:768 * j + 768], (P, QR // P, 768)) for j in range(2)]
    plan.append((g["mla_w_ukv"][0].rearrange("(k p) n -> p k n", p=P), (P, KVR // P, 2048)))
    wo = g["mla_w_out"][0].rearrange("(k p) n -> p k n", p=P)
    plan += [(wo[:, :, 512 * j:512 * j + 512], (P, KT, 512)) for j in range(2)]
    moe(1)
    return plan


def phase(build):
    def built(g, *args):
        build(g, *args)
        g.end_phase()
    return built


N_ADA, N_AB, N_ABO = 0, 24, 33
N_MOE = [35, 138]
N_MLA = 131


@phase
def phase_modulation(g):
    nc = g.nc
    with ExitStack() as ctx:
        sb = lambda n, s: ctx.enter_context(nc.sbuf_tensor(n, s, F32))
        sem = lambda n: g.semaphore(n)
        cin = sb("c_in", [P, 2, KT])
        sc = sb("silu_c", [P, KT, 2])
        bias = sb("ada_bias", [2, 4 * 3 * D])
        row = sb("mod_row", [2, 4 * 3 * D])
        ps = ctx.enter_context(nc.psum_tensor("mod_ps", [2, 6, 512], F32))
        c_here, silu_done, mod_mm, mod_sum, mod_out = map(sem, ("c_here", "silu_done", "mod_mm", "mod_sum", "mod_out"))
        const_here, zero_set, zero_out = sem("const_here"), sem("zero_set"), sem("zero_out")
        zx = sb("zero_rows", [P, D])
        g.free_when.update({n: (mod_mm, n + 1) for n in range(N_AB)})
        with nc.Block() as block:
            @block.sync
            def _(sp):
                for c, name in enumerate(("c_prompt", "c_sample")):
                    sp.dma_start(cin[:, c, :], g.io[name][0].rearrange("(p k) -> p k", k=KT)).then_inc(c_here, 16)
                for r in range(2):
                    sp.dma_start(bias[r:r + 1, :], g.io["ada_b"].rearrange("(o l) s n -> o (l s n)", o=1)).then_inc(c_here, 16)
                g.stream(sp, 24)
                sp.dma_start(g.cst[:], g.io["cst"]).then_inc(const_here, 16)
                sp.wait_ge(mod_sum, 24)
                sp.dma_start(g.io["mod"].rearrange("s c n -> c s n"),
                             row[:].rearrange("c (s n) -> c s n", s=4)).then_inc(mod_out, 16)
                sp.wait_ge(mod_out, 16)
                sp.wait_ge(const_here, 16)

            @block.scalar
            def _(act):
                act.wait_ge(c_here, 64)
                nc.scalar.activation(sc[:].rearrange("p k c -> p c k"), cin[:], ACT.Silu).then_inc(silu_done, 1)

            @block.tensor
            def _(pe):
                pe.wait_ge(silu_done, 1)
                for n in range(24):
                    w = g.chunk(pe, n)
                    if n >= 6:
                        pe.wait_ge(mod_sum, n - 5)
                    for k in range(KT):
                        last = nc.tensor.matmul(ps[:, n % 6, :], sc[:, k, :], w[:, k, :], start=k == 0, stop=k == KT - 1)
                    last.then_inc(mod_mm, 1)

            @block.vector
            def _(dve):
                for n in range(24):
                    dve.wait_ge(mod_mm, n + 1)
                    nc.vector.tensor_tensor(row[:, 512 * n:512 * n + 512], ps[:, n % 6, :],
                                            bias[:, 512 * n:512 * n + 512], ALU.add).then_inc(mod_sum, 1)

            @block.gpsimd
            def _(pool):
                nc.gpsimd.memset(g.eps[:], EPS)
                nc.gpsimd.memset(zx[:], 0.0).then_inc(zero_set, 1)
                pool.wait_ge(zero_set, 1)
                for name, first in (("xslot", 0), ("yslot", NE * CAP)):
                    rows = g.io[name][first:SLOTS, :]
                    pool.dma_start(rows.rearrange("(b p) d -> p b d", p=P),
                                   zx[:].unsqueeze(1).to_broadcast([P, (SLOTS - first) // P, D])).then_inc(zero_out, 16)
                pool.wait_ge(zero_out, 32)


def x_source(g, s, t):
    if s == 0:
        return g.io["x_prompt"][0, t * P:(t + 1) * P, :] if t < NT - 1 else g.io["x_sample"][0]
    return g.io["xres"][s - 1][t * P:t * P + width(t), :]


def bcast_rows(ap, n=P):
    return ap.partition_broadcast(n)


@phase
def phase_norm(g, s, hT, h, base):
    nc = g.nc
    with ExitStack() as ctx:
        sb = lambda n, sh: ctx.enter_context(nc.sbuf_tensor(f"{n}_{s}", sh, F32))
        sem = lambda n: g.semaphore(f"{n}_{s}")
        xt = sb("xt", [P, NT, D])
        mod = sb("mod", [P, 2, 2, D])
        nw = sb("nw", [P, D])
        junk = sb("junk", [P, D])
        ss = sb("ss", [P, NT])
        rs = sb("rs", [P, NT])
        ht = h if h is not None else xt
        tp = ctx.enter_context(nc.psum_tensor(f"tp_{s}", [P, 2, KT, P], F32))
        x_here = [sem(f"x_here{t}") for t in range(NT)]
        mod_here, rs_done, h_done, tp_done, ht_done = map(
            sem, ("mod_here", "rs_done", "h_done", "tp_done", "ht_done"))
        g.ht_done = ht_done
        with nc.Block() as block:
            @block.sync
            def _(sp):
                for t in range(NT):
                    sp.dma_start(xt[0:width(t), t, :], x_source(g, s, t)).then_inc(x_here[t], 16)
                sp.dma_start(nw[:], bcast_rows(g.io["norm_w"][s // 2, s % 2])).then_inc(mod_here, 16)
                for c in range(2):
                    for m in range(2):
                        sp.dma_start(mod[:, c, m, :], bcast_rows(g.io["mod"][s, c, m * D:(m + 1) * D])).then_inc(mod_here, 16)
                g.stream(sp, base)

            @block.scalar
            def _(act):
                ch = g.chain(act, "act")
                for t in range(NT):
                    w = width(t)
                    act.wait_ge(x_here[t], 16)
                    ch(nc.scalar.activation(junk[0:w, :], xt[0:w, t, :], ACT.Square, accum_out=ss[0:w, t:t + 1]))
                    ch(nc.scalar.activation(rs[0:w, t:t + 1], ss[0:w, t:t + 1], ACT.Ln, scale=1.0 / D, bias=g.eps[0:w, :]))
                    nc.scalar.activation(rs[0:w, t:t + 1], rs[0:w, t:t + 1], ACT.Exp, scale=-0.5).then_inc(rs_done, 1)
                for t in range(NT):
                    w = width(t)
                    act.wait_ge(tp_done, t + 1)
                    nc.scalar.copy(hT[:, :, t * P:t * P + w], tp[:, t % 2, :, 0:w]).then_inc(ht_done, 1)
                g.done(ch, "act")

            @block.vector
            def _(dve):
                ch = g.chain(dve, "dve")
                dve.wait_ge(mod_here, 80)
                for c in range(2):
                    ch(nc.vector.scalar_tensor_tensor(mod[:, c, 1, :], mod[:, c, 1, :], 1.0, nw[:], ALU.add, ALU.mult))
                for t in range(NT):
                    w, c = width(t), int(t == NT - 1)
                    dve.wait_ge(rs_done, t + 1)
                    ch(nc.vector.scalar_tensor_tensor(ht[0:w, t, :], xt[0:w, t, :], rs[0:w, t:t + 1],
                                                      mod[0:w, c, 1, :], ALU.mult, ALU.mult))
                    nc.vector.tensor_tensor(ht[0:w, t, :], ht[0:w, t, :], mod[0:w, c, 0, :], ALU.add).then_inc(h_done, 1)
                g.done(ch, "dve")

            @block.tensor
            def _(pe):
                for t in range(NT):
                    w = width(t)
                    pe.wait_ge(h_done, t + 1)
                    if t >= 2:
                        pe.wait_ge(ht_done, t - 1)
                    for k in range(KT):
                        last = nc.tensor.transpose(tp[:, t % 2, k, 0:w], ht[0:w, t, k:D:KT], g.c(K_ID, w, w))
                    last.then_inc(tp_done, 1)


@phase
def phase_ab_project(g, a, hT):
    nc, io = g.nc, g.io
    base = N_AB
    with ExitStack() as ctx:
        sb = lambda n, sh: ctx.enter_context(nc.sbuf_tensor(n, sh, F32))
        sem = lambda n: g.semaphore(n)
        lrT = sb("lrT", [GLR, TOK])
        wal = sb("w_alpha", [GLR, 2 * P])
        bal = sb("b_alpha", [P, 2])
        laz = sb("la_z", [P, 2, TOK])
        lae = sb("la_e", [P, 2, TOK])
        gp = sb("gate_par", [P, 2, NH])
        gab = sb("gab", [P, NT, 2 * NH])
        ge = sb("gab_e", [P, NT, 2 * NH])
        silu = sb("silu_out", [P, 2, 512])
        cw = sb("conv_w", [P, 12, CW])
        xc = sb("conv_in", [P, 2, TOK + 6])
        cv = sb("conv_sum", [P, 2, TOK + 6])
        hist0 = sb("conv_hist_in", [P, 12, 3])
        hist = sb("conv_hist", [P, 2, 12, 3])
        sq = laz
        z = ctx.enter_context(nc.psum_tensor("ab_z", [P, 2, 2, 512], F32))
        zt = ctx.enter_context(nc.psum_tensor("ab_zt", [P, 2, 512], F32))
        zs = ctx.enter_context(nc.psum_tensor("ab_zs", [P, NT, 2 * NH], F32))
        (par_here, pads_set, fm_done, fm_free, tm_done, tm_free, la_abs, la_ln, gab_done, gab_here, gab_abs, gab_exp,
         xc_ready, conv_done, conv_used, hist_done, hist_out, sq_ready, rn_ready,
         l2_done, ss_done, gab_set) = map(sem, (
             "par_here", "pads_set", "fm_done", "fm_free", "tm_done", "tm_free", "la_abs", "la_ln", "gab_done", "gab_here",
             "gab_abs", "gab_exp", "xc_ready", "conv_done", "conv_used", "hist_done",
             "hist_out", "sq_ready", "rn_ready", "l2_done", "ss_done", "gab_set"))
        g.free_when.update(dict(zip(range(N_AB, N_ABO), (
            (fm_done, 4), (tm_done, 5), (fm_done, 5), (gab_done, 1), (tm_done, 10),
            (fm_done, 11), (fm_done, 15), (fm_done, 19), (tm_done, 15)))))
        silu_used = [sem("silu_used0"), sem("silu_used1")]
        N_FM = 19

        with nc.Block() as block:
            @block.sync
            def _(sp):
                with nc.allow_non_contiguous_dma(reason="small parameters by features"):
                    sp.dma_start(wal[:], io["gla_w_alpha"][0]).then_inc(par_here, 16)
                    sp.dma_start(bal[:], io["gla_b_alpha"][0].rearrange("(j p) -> p j", p=P)).then_inc(par_here, 16)
                    sp.dma_start(gp[:, 0, :], bcast_rows(io["gdn_dt_bias"][0])).then_inc(par_here, 16)
                    sp.dma_start(gp[:, 1, :], bcast_rows(io["gdn_a_log"][0])).then_inc(par_here, 16)
                    for i in range(CW):
                        sp.dma_start(cw[:, :, i], io["gdn_conv_w"][0, i].rearrange("(f p) -> p f", p=P)).then_inc(par_here, 16)
                    for i in range(3):
                        sp.dma_start(hist0[:, :, i], io["state_gdn_conv"][0, 0, i].rearrange("(f p) -> p f", p=P)).then_inc(par_here, 16)
                    g.stream(sp, N_ABO)
                    sp.wait_ge(hist_done, 12)
                    for c, name in enumerate(("conv_prompt", "conv_sample")):
                        for i in range(3):
                            sp.dma_start(io[name][0, 0, i].rearrange("(f p) -> p f", p=P), hist[:, c, :, i]).then_inc(hist_out, 16)
                    sp.wait_ge(hist_out, 96)

            @block.tensor
            def _(pe):
                def fm_tile(i, lhsT, rhs, kt):
                    if i >= 2:
                        pe.wait_ge(fm_free, i - 1)
                    for k in range(kt):
                        m = lhsT(k).free_size()
                        nc.tensor.matmul(z[0:m, i % 2, 0, 0:SEQ], lhsT(k), rhs(k)[:, 0:SEQ], start=k == 0, stop=k == kt - 1)
                        last = nc.tensor.matmul(z[0:m, i % 2, 1, 0:DSEQ], lhsT(k), rhs(k)[:, SEQ:TOK], start=k == 0, stop=k == kt - 1)
                    last.then_inc(fm_done, 1)

                def fm_chunk(n, i):
                    w = g.chunk(pe, N_AB + n)
                    for f in range(-(-w.shape[2] // P)):
                        fm_tile(i + f, lambda k: w[:, k, f * P:min((f + 1) * P, w.shape[2])], lambda k: hT[:, k, :], KT)

                def tm_chunk(n, j):
                    w = g.chunk(pe, N_AB + n)
                    for t in range(NT):
                        if j + t >= 2:
                            pe.wait_ge(tm_free, j + t - 1)
                        for k in range(KT):
                            last = nc.tensor.matmul(zt[0:width(t), (j + t) % 2, :], hT[:, k, t * P:t * P + width(t)], w[:, k, :],
                                                    start=k == 0, stop=k == KT - 1)
                        last.then_inc(tm_done, 1)

                fm_chunk(0, 0)
                tm_chunk(1, 0)
                fm_chunk(2, 4)
                pe.wait_ge(fm_free, 5)
                pe.wait_ge(par_here, 176)
                for j in range(2):
                    fm_tile(5 + j, lambda k: wal[:, j * P:(j + 1) * P], lambda k: lrT[:, :], 1)
                w = g.chunk(pe, N_AB + 3)
                for t in range(NT):
                    for k in range(KT):
                        last = nc.tensor.matmul(zs[0:width(t), t, :], hT[:, k, t * P:t * P + width(t)], w[:, k, :],
                                                start=k == 0, stop=k == KT - 1)
                last.then_inc(gab_done, 1)
                tm_chunk(4, NT)
                for n in range(3):
                    fm_chunk(5 + n, 7 + 4 * n)
                tm_chunk(8, 2 * NT)
                for f in range(8):
                    i = N_FM + f
                    pe.wait_ge(sq_ready, f + 1)
                    pe.wait_ge(fm_free, i - 1)
                    nc.tensor.matmul(z[:, i % 2, 0, 0:SEQ], g.c(K_ONE, P), sq[:, f % 2, 0:SEQ], start=True, stop=True)
                    nc.tensor.matmul(z[:, i % 2, 1, 0:DSEQ], g.c(K_ONE, P), sq[:, f % 2, SEQ:TOK],
                                     start=True, stop=True).then_inc(ss_done, 1)

            @block.scalar
            def _(act):
                ch = g.chain(act, "act")

                def evac_fm(i, prompt, sample, func=ACT.Copy, **kw):
                    m = prompt.shape[0]
                    zp = z[0:m, i % 2, 0, 0:SEQ]
                    if len(prompt.shape) == 3:
                        zp = zp.rearrange("p (a b) -> p a b", b=P)
                    nc.scalar.activation(prompt, zp, func, **kw)
                    nc.scalar.activation(sample, z[0:m, i % 2, 1, 0:DSEQ], func, **kw).then_inc(fm_free, 1)

                def gate(j):
                    t, half, b = j % NT, int(j >= 2 * NT), (j - NT) % 2
                    w = width(t)
                    act.wait_ge(tm_done, j + 1)
                    if j - NT >= 2:
                        act.wait_ge(silu_used[b], 16 * ((j - NT) // 2))
                    nc.scalar.activation(silu[0:w, b, :], zt[0:w, j % 2, :], ACT.Silu).then_inc(tm_free, 1)
                    act.wait_ge(tm_free, j + 1)
                    act.dma_start(io["gates"][t * P:t * P + w, half * 512:half * 512 + 512], silu[0:w, b, :]).then_inc(silu_used[b], 16)

                def conv_silu(f):
                    act.wait_ge(conv_done, f + 1)
                    nc.scalar.activation(a.qkvT[:, f, 0:SEQ], cv[:, f % 2, 0:SEQ], ACT.Silu)
                    nc.scalar.activation(a.qkvT[:, f, SEQ:TOK], cv[:, f % 2, SEQ + 3:TOK + 3], ACT.Silu).then_inc(conv_used, 1)

                def l2(f):
                    i = N_FM + f
                    act.wait_ge(ss_done, f + 1)
                    if f >= 2:
                        act.wait_ge(l2_done, f - 1)
                    nc.scalar.activation(cv[:, f % 2, 0:SEQ], z[:, i % 2, 0, 0:SEQ], ACT.Ln, bias=g.eps[:])
                    nc.scalar.activation(cv[:, f % 2, SEQ:TOK], z[:, i % 2, 1, 0:DSEQ], ACT.Ln, bias=g.eps[:]).then_inc(fm_free, 1)
                    act.wait_ge(fm_free, i + 1)
                    nc.scalar.activation(cv[:, f % 2, 0:TOK], cv[:, f % 2, 0:TOK], ACT.Exp, scale=-0.5).then_inc(rn_ready, 1)

                act.wait_ge(pads_set, 6)
                for i in range(4):
                    act.wait_ge(fm_done, i + 1)
                    evac_fm(i, a.qk2[:, 0:4, i // 2, i % 2, :], a.qk2[:, 4, i // 2, i % 2, 0:DSEQ],
                            scale=GDK ** -0.5 if i < 2 else 1.0)
                for t in range(NT):
                    act.wait_ge(tm_done, t + 1)
                    nc.scalar.copy(a.v[0:width(t), t, :], zt[0:width(t), t % 2, :]).then_inc(tm_free, 1)
                act.wait_ge(fm_done, 5)
                evac_fm(4, lrT[:, 0:SEQ], lrT[:, SEQ:TOK])
                act.wait_ge(par_here, 176)
                for j in range(2):
                    act.wait_ge(fm_done, 6 + j)
                    evac_fm(5 + j, laz[:, j, 0:SEQ], laz[:, j, SEQ:TOK], ACT.Identity, bias=bal[:, j:j + 1])
                act.wait_ge(gab_done, 1)
                nc.scalar.copy(gab[:, 0:4, :], zs[:, 0:4, :])
                nc.scalar.copy(gab[0:DSEQ, 4, :], zs[0:DSEQ, 4, :]).then_inc(gab_here, 1)
                act.wait_ge(la_abs, 1)
                ch(nc.scalar.activation(lae[:], lae[:], ACT.Exp, scale=-1.0))
                nc.scalar.activation(lae[:], lae[:], ACT.Ln, bias=1.0).then_inc(la_ln, 1)
                act.wait_ge(gab_abs, 2)
                ch(nc.scalar.activation(ge[:], ge[:], ACT.Exp, scale=-1.0))
                ch(nc.scalar.activation(gp[:, 1, :], gp[:, 1, :], ACT.Exp))
                nc.scalar.activation(ge[:, :, 0:NH], ge[:, :, 0:NH], ACT.Ln, bias=1.0).then_inc(gab_exp, 1)
                for j in range(NT, 2 * NT):
                    gate(j)
                for f in range(12):
                    act.wait_ge(fm_done, 8 + f)
                    if f >= 2:
                        act.wait_ge(hist_done, f - 1)
                        act.wait_ge(conv_done, f - 1)
                    evac_fm(7 + f, xc[:, f % 2, 3:3 + SEQ], xc[:, f % 2, SEQ + 6:TOK + 6])
                    if f:
                        conv_silu(f - 1)
                conv_silu(11)
                for j in range(2 * NT, 3 * NT):
                    gate(j)
                act.wait_ge(conv_used, 12)
                for f in range(8):
                    if f >= 2:
                        act.wait_ge(ss_done, f - 1)
                    nc.scalar.activation(sq[:, f % 2, :], a.qkvT[:, f, 0:TOK], ACT.Square).then_inc(sq_ready, 1)
                    if f:
                        l2(f - 1)
                l2(7)
                for b in range(2):
                    act.wait_ge(silu_used[b], 16 * NT)
                g.done(ch, "act")

            @block.gpsimd
            def _(pool):
                for ap in (a.qk2[:, 4, :, :, DSEQ:P], a.v[:, 4, :], a.b2[:, 4, :, :], a.qkvT[:, :, TOK:NT * P], gab[:]):
                    nc.gpsimd.memset(ap, 0.0).then_inc(pads_set, 1)
                nc.gpsimd.memset(xc[:, :, 0:3], 0.0).then_inc(pads_set, 1)
                pool.wait_ge(par_here, 176)
                for f in range(12):
                    if f >= 2:
                        pool.wait_ge(conv_done, f - 1)
                    nc.gpsimd.tensor_copy(xc[:, f % 2, SEQ + 3:SEQ + 6], hist0[:, f, :]).then_inc(xc_ready, 1)
                    pool.wait_ge(fm_free, 8 + f)
                    nc.gpsimd.tensor_copy(hist[:, 0, f, :], xc[:, f % 2, SEQ:SEQ + 3])
                    nc.gpsimd.tensor_copy(hist[:, 1, f, :], xc[:, f % 2, TOK + 3:TOK + 6]).then_inc(hist_done, 1)

            @block.vector
            def _(dve):
                ch = g.chain(dve, "dve")
                dve.wait_ge(fm_free, 7)
                nc.vector.scalar_tensor_tensor(lae[:], laz[:], -1.0, laz[:], ALU.mult, ALU.max).then_inc(la_abs, 1)
                dve.wait_ge(gab_here, 1)
                dve.wait_ge(par_here, 176)
                ch(nc.vector.tensor_tensor(gab[:, :, 0:NH], gab[:, :, 0:NH], gp[:, 0:1, :].to_broadcast([P, NT, NH]), ALU.add))
                nc.vector.scalar_tensor_tensor(ge[:, :, 0:NH], gab[:, :, 0:NH], -1.0, gab[:, :, 0:NH], ALU.mult, ALU.max).then_inc(gab_abs, 1)
                nc.vector.tensor_copy(ge[:, :, NH:], gab[:, :, NH:]).then_inc(gab_abs, 1)
                dve.wait_ge(la_ln, 1)
                ch(nc.vector.scalar_tensor_tensor(laz[:], laz[:], 0.0, lae[:], ALU.min, ALU.subtract))
                for j in range(2):
                    nc.vector.tensor_scalar(a.b2[:, 0:4, j, :], laz[:, j, 0:SEQ].rearrange("p (t n) -> p t n", n=P), 1.0 / 16.0, None, ALU.mult)
                    ch(nc.vector.tensor_scalar(a.b2[:, 4, j, 0:DSEQ], laz[:, j, SEQ:TOK], 1.0 / 16.0, None, ALU.mult))
                for t in range(NT):
                    for j in range(2):
                        ch(nc.vector.tensor_tensor_scan(lae[:, 0, 0:P], g.c(K_ONE, P), a.b2[:, t, j, :], 0.0, ALU.mult, ALU.add))
                        ch(nc.vector.tensor_copy(a.b2[:, t, j, :], lae[:, 0, 0:P]))
                dve.wait_ge(gab_exp, 1)
                ch(nc.vector.scalar_tensor_tensor(gab[:, :, 0:NH], gab[:, :, 0:NH], 0.0, ge[:, :, 0:NH], ALU.max, ALU.add))
                ch(nc.vector.scalar_tensor_tensor(a.gb[:, :, 0:NH], gab[:, :, 0:NH], -1.0, gp[:, 1:2, :].to_broadcast([P, NT, NH]), ALU.mult, ALU.mult))
                ch(nc.vector.memset(a.gb[32:64, NT - 1, 0:NH], 0.0))
                ch(nc.vector.memset(a.gb[64:P, NT - 1, 0:NH], 0.0))
                ch(nc.vector.tensor_scalar(ge[:, :, NH:], ge[:, :, NH:], 1.0, None, ALU.add))
                ch(nc.vector.reciprocal(a.gb[:, :, NH:], ge[:, :, NH:]))
                n = TOK + 3
                for f in range(12):
                    dve.wait_ge(fm_free, 8 + f)
                    dve.wait_ge(xc_ready, f + 1)
                    if f >= 2:
                        dve.wait_ge(conv_used, f - 1)
                    x, o = xc[:, f % 2, :], cv[:, f % 2, 0:n]
                    ch(nc.vector.tensor_scalar(o, x[:, 0:n], cw[:, f, 0:1], None, ALU.mult))
                    for i in range(1, CW):
                        ins = nc.vector.scalar_tensor_tensor(o, x[:, i:i + n], cw[:, f, i:i + 1], o, ALU.mult, ALU.add)
                        if i < CW - 1:
                            ch(ins)
                    ins.then_inc(conv_done, 1)
                for f in range(8):
                    dve.wait_ge(rn_ready, f + 1)
                    q = a.qkvT[:, f, 0:TOK]
                    nc.vector.scalar_tensor_tensor(q, q, DK ** -0.5 if f < 4 else 1.0, cv[:, f % 2, 0:TOK],
                                                   ALU.mult, ALU.mult).then_inc(l2_done, 1)
                g.done(ch, "dve")


@phase
def phase_gla(g, a, o):
    nc, io = g.nc, g.io
    with ExitStack() as ctx:
        sb = lambda n, sh: ctx.enter_context(nc.sbuf_tensor("gla_" + n, sh, F32))
        sem = lambda n: g.semaphore("gla_" + n)
        em = sb("em", [P, 2, LEV, 2 * P])
        qe = sb("qe", [P, 2, P])
        ke = sb("ke", [P, 2, P])
        ket = sb("ket", [P, 2, P])
        mk = o[:, 0:2, GH * P:].rearrange("p a (l n) -> p a l n", n=P)
        at = sb("at", [P, GH, P])
        st = sb("st", [P, 3, 2, P])
        el = sb("el", [P, 2, 1])
        ps = ctx.enter_context(nc.psum_tensor("gla_ps", [P, 2, LEV + 1, P], F32))
        pk = ctx.enter_context(nc.psum_tensor("gla_pk", [P, 2, P], F32))
        po = ctx.enter_context(nc.psum_tensor("gla_po", [P, 2, 4, P], F32))
        pst = ctx.enter_context(nc.psum_tensor("gla_pst", [P, 2, P], F32))
        (st_here, x_ready, e_ready, m_ready, s_done, at_ready, kt_done, kt_ready, o_done, o_used, st_done,
         st_ready, out_done) = map(sem, ("st_here", "x_ready", "e_ready", "m_ready", "s_done", "at_ready", "kt_done",
                                         "kt_ready", "o_done", "o_used", "st_done", "st_ready", "out_done"))
        s_in = lambda t: t % 2 if t < NT - 1 else 2
        s_out = lambda t: (t + 1) % 2

        with nc.Block() as block:
            @block.sync
            def _(sp):
                sp.dma_start(st[:, 2, :, :], io["state_gla"][0, 0].rearrange("(j h) d v -> (h d) j v", j=2)).then_inc(st_here, 16)
                g.stream(sp, N_ABO)
                for t, name in ((NT - 2, "gla_prompt"), (NT - 1, "gla_sample")):
                    sp.wait_ge(st_ready, t + 1)
                    sp.dma_start(io[name][0, 0].rearrange("(j h) d v -> (h d) j v", j=2), st[:, s_out(t), :, :]).then_inc(out_done, 16)
                sp.wait_ge(out_done, 32)

            @block.vector
            def _(dve):
                ch = g.chain(dve, "dve")

                def exponents(t):
                    if t >= 2:
                        dve.wait_ge(s_done, GH * (t - 1))
                    for l in range(LEV):
                        m = 1 << l
                        b = a.b2[:, t].rearrange("p j (n x m) -> p (j n) x m", x=2, m=m)
                        e = em[:, t % 2, l].rearrange("p (n x m) -> p n x m", x=2, m=m)
                        mid = b[:, :, 0, m - 1:m].to_broadcast([P, P // m, m])
                        nc.vector.tensor_tensor(e[:, :, 1, :], b[:, :, 1, :], mid, ALU.subtract)
                        nc.vector.tensor_tensor(e[:, :, 0, :], mid, b[:, :, 0, :], ALU.subtract)
                    if t:
                        dve.wait_ge(kt_done, t)
                    last = a.b2[:, t, :, P - 1:P]
                    nc.vector.tensor_tensor(ke[:], last.to_broadcast([P, 2, P]), a.b2[:, t], ALU.subtract).then_inc(x_ready, 1)

                def decayed(t):
                    dve.wait_ge(e_ready, t + 1)
                    for l in range(LEV):
                        m = 1 << l
                        q = a.qk2[:, t, 0].rearrange("p j (n x m) -> p (j n) x m", x=2, m=m)
                        k = a.qk2[:, t, 1].rearrange("p j (n x m) -> p (j n) x m", x=2, m=m)
                        e = em[:, t % 2, l].rearrange("p (n x m) -> p n x m", x=2, m=m)
                        nc.vector.tensor_tensor(e[:, :, 1, :], e[:, :, 1, :], q[:, :, 1, :], ALU.mult)
                        nc.vector.tensor_tensor(e[:, :, 0, :], e[:, :, 0, :], k[:, :, 0, :], ALU.mult)
                    nc.vector.tensor_tensor(qe[:], qe[:], a.qk2[:, t, 0], ALU.mult)
                    nc.vector.tensor_tensor(ke[:], ke[:], a.qk2[:, t, 1], ALU.mult).then_inc(m_ready, 1)

                ch(nc.vector.memset(st[:, 0, :, :], 0.0))
                exponents(0)
                for t in range(NT):
                    decayed(t)
                    for h in range(GH):
                        u = GH * t + h
                        dve.wait_ge(s_done, u + 1)
                        if u:
                            dve.wait_ge(at_ready, u)
                        ch(nc.vector.tensor_tensor(mk, ps[:, u % 2].rearrange("p (a l) n -> p a l n", a=2),
                                                   g.c(K_MT, (LEV + 1) * P).rearrange("p (a l n) -> p a l n", a=2, n=P), ALU.mult))
                        if t:
                            dve.wait_ge(o_done, t)
                        nc.vector.tensor_reduce(at[:, h, :], mk.rearrange("p a l n -> p n a l"), AX.XY, ALU.add).then_inc(at_ready, 1)
                    if t + 1 < NT:
                        exponents(t + 1)
                    dve.wait_ge(st_done, t + 1)
                    if t == NT - 1:
                        dve.wait_ge(st_here, 16)
                    for j in range(2):
                        ins = nc.vector.scalar_tensor_tensor(st[:, s_out(t), j, :], st[:, s_in(t), j, :], el[:, j, :],
                                                             pst[:, j, :], ALU.mult, ALU.add)
                    ins.then_inc(st_ready, 1)
                g.done(ch, "dve")

            @block.scalar
            def _(act):
                for t in range(NT):
                    act.wait_ge(x_ready, t + 1)
                    nc.scalar.activation(em[:, t % 2], em[:, t % 2], ACT.Exp)
                    if t:
                        act.wait_ge(o_done, t)
                        act.wait_ge(st_ready, t)
                    nc.scalar.activation(qe[:], a.b2[:, t], ACT.Exp)
                    nc.scalar.activation(el[:], a.b2[:, t, :, P - 1:P], ACT.Exp)
                    nc.scalar.activation(ke[:], ke[:], ACT.Exp).then_inc(e_ready, 1)
                    act.wait_ge(kt_done, t + 1)
                    if t:
                        act.wait_ge(st_done, t)
                    nc.scalar.copy(ket[:], pk[:]).then_inc(kt_ready, 1)
                    act.wait_ge(o_done, t + 1)
                    nc.scalar.copy(o[:, t, 0:GH * P].rearrange("p (j b n) -> p b j n", b=2, n=P), po[:, :, 0:2, :]).then_inc(o_used, 1)

            @block.tensor
            def _(pe):
                for t in range(NT):
                    pe.wait_ge(m_ready, t + 1)
                    for j in range(2):
                        last = nc.tensor.transpose(pk[:, j, :], ke[:, j, :], g.c(K_ID, P))
                    last.then_inc(kt_done, 1)
                    for h in range(GH):
                        u = GH * t + h
                        r, j = slice(64 * (h % 2), 64 * (h % 2) + 64), h // 2
                        if u >= 2:
                            pe.wait_ge(at_ready, u - 1)
                        for l in range(LEV):
                            m = em[r, t % 2, l, j * P:(j + 1) * P]
                            nc.tensor.matmul(ps[:, u % 2, l, :], m, m, start=True, stop=True)
                        nc.tensor.matmul(ps[:, u % 2, LEV, :], a.qk2[r, t, 1, j, :], a.qk2[r, t, 0, j, :],
                                         start=True, stop=True).then_inc(s_done, 1)
                    pe.wait_ge(kt_ready, t + 1)
                    if t:
                        pe.wait_ge(st_ready, t)
                        pe.wait_ge(o_used, t)
                    for h in range(GH):
                        r = slice(64 * (h % 2), 64 * (h % 2) + 64)
                        last = nc.tensor.matmul(pst[r, h // 2, :], ket[:, h // 2, r], a.v[:, t, h * P:(h + 1) * P], start=True, stop=True)
                    last.then_inc(st_done, 1)
                    if t == NT - 1:
                        pe.wait_ge(st_here, 16)
                    if t == 0:
                        pe.wait_ge(at_ready, 1)
                    for h in range(GH):
                        r = slice(64 * (h % 2), 64 * (h % 2) + 64)
                        pe.wait_ge(at_ready, GH * t + h + 1)
                        nc.tensor.matmul(po[:, h % 2, h // 2, :], at[:, h, :], a.v[:, t, h * P:(h + 1) * P], start=True, stop=False)
                        last = nc.tensor.matmul(po[:, h % 2, h // 2, :], qe[r, h // 2, :], st[r, s_in(t), h // 2, :], start=False, stop=True)
                    last.then_inc(o_done, 1)


@phase
def phase_gdn_inverse(g, a):
    nc, io = g.nc, g.io
    kT = a.qkvT[:, NH:2 * NH, :]
    with ExitStack() as ctx:
        sb = lambda n, sh: ctx.enter_context(nc.sbuf_tensor("inv_" + n, sh, F32))
        sem = lambda n: g.semaphore("inv_" + n)
        lm = sb("lm", [P, NT, NH, P])
        x = sb("x", [P, NT, NH, P])
        ll = sb("ll", [P, 2, NH, P])
        tt = sb("tt", [P, 2, NH, P])
        lr_done, gam_ready, dl_ready, dl_exp, lm_ready = map(sem, ("lr_done", "gam_ready", "dl_ready", "dl_exp", "lm_ready"))
        with ExitStack() as c2:
            pr = c2.enter_context(nc.psum_tensor("inv_pr", [P, 2, NH, P], F32))
            pkk = c2.enter_context(nc.psum_tensor("inv_pkk", [P, 2, NH, P], F32))
            pg = c2.enter_context(nc.psum_tensor("inv_pg", [P, 2, 512], F32))
            with nc.Block() as block:
                @block.tensor
                def _(pe):
                    for t in range(NT):
                        b = t % 2
                        if t >= 2:
                            pe.wait_ge(lm_ready, t - 1)
                        nc.tensor.matmul(pg[:, b, 0:NH], g.c(K_U, P), a.gb[:, t, 0:NH], start=True, stop=True)
                        for h in range(NH):
                            tok = slice(t * P, t * P + P)
                            nc.tensor.matmul(pr[:, b, h, :], a.gb[:, t, h:h + 1].to_broadcast([P, P]), g.c(K_U, P), start=True, stop=True)
                            last = nc.tensor.matmul(pkk[:, b, h, :], kT[:, h, tok], kT[:, h, tok], start=True, stop=True)
                        last.then_inc(lr_done, 1)

                @block.scalar
                def _(act):
                    for t in range(NT):
                        act.wait_ge(lr_done, t + 1)
                        nc.scalar.copy(a.gam[:, t, :], pg[:, t % 2, 0:NH]).then_inc(gam_ready, 1)
                        act.wait_ge(dl_ready, t + 1)
                        nc.scalar.activation(lm[:, t], lm[:, t], ACT.Exp, scale=-1.0).then_inc(dl_exp, 1)

                @block.vector
                def _(dve):
                    for t in range(NT):
                        dve.wait_ge(gam_ready, t + 1)
                        for h in range(NH):
                            ins = nc.vector.tensor_scalar(lm[:, t, h, :], pr[:, t % 2, h, :], a.gam[:, t, h:h + 1], 0.0, ALU.subtract, ALU.max)
                        ins.then_inc(dl_ready, 1)
                        dve.wait_ge(dl_exp, t + 1)
                        for h in range(NH):
                            ins = nc.vector.scalar_tensor_tensor(lm[:, t, h, :], pkk[:, t % 2, h, :], a.gb[:, t, NH + h:NH + h + 1],
                                                                 lm[:, t, h, :], ALU.mult, ALU.mult)
                        ins.then_inc(lm_ready, 1)
        ptt = ctx.enter_context(nc.psum_tensor("inv_ptt", [P, 2, NH, P], F32))
        pp = ctx.enter_context(nc.psum_tensor("inv_pp", [P, 2, NH, P], F32))
        ppt = ctx.enter_context(nc.psum_tensor("inv_ppt", [P, 2, NH, P], F32))
        ll_ready, tt_done, tt_ready, p_done, x_ready = map(sem, ("ll_ready", "tt_done", "tt_ready", "p_done", "x_ready"))
        steps = LEV * NT
        ident = g.c(K_ID, P)
        with nc.Block() as block:
            @block.gpsimd
            def _(pool):
                for i in range(steps):
                    l, t = divmod(i, NT)
                    if i >= 2:
                        pool.wait_ge(tt_done, i - 1)
                    mask = g.c(K_ML + l * P, P).unsqueeze(1).to_broadcast([P, NH, P])
                    nc.gpsimd.tensor_tensor(ll[:, i % 2], lm[:, t], mask, ALU.mult).then_inc(ll_ready, 1)

            @block.tensor
            def _(pe):
                def product_t(i):
                    l, t = divmod(i, NT)
                    pe.wait_ge(ll_ready, i + 1)
                    if l:
                        pe.wait_ge(x_ready, i - NT + 1)
                    if i >= 2:
                        pe.wait_ge(tt_ready, i - 1)
                    for h in range(NH):
                        last = nc.tensor.matmul(ptt[:, i % 2, h, :], ll[:, i % 2, h, :], a.xt[:, t, h, :] if l else ident, start=True, stop=True)
                    last.then_inc(tt_done, 1)

                def correction(i):
                    l, t = divmod(i, NT)
                    pe.wait_ge(tt_ready, i + 1)
                    if i >= 2:
                        pe.wait_ge(x_ready, i - 1)
                    for h in range(NH):
                        if l < LEV - 1:
                            nc.tensor.matmul(pp[:, i % 2, h, :], tt[:, i % 2, h, :], x[:, t, h, :] if l else ident, start=True, stop=True)
                        last = nc.tensor.matmul(ppt[:, i % 2, h, :], x[:, t, h, :] if l else ident, tt[:, i % 2, h, :], start=True, stop=True)
                    last.then_inc(p_done, 1)

                for i in range(steps):
                    product_t(i)
                    if i:
                        correction(i - 1)
                correction(steps - 1)

            @block.scalar
            def _(act):
                for i in range(steps):
                    act.wait_ge(tt_done, i + 1)
                    if i >= 2:
                        act.wait_ge(p_done, i - 1)
                    nc.scalar.copy(tt[:, i % 2], ptt[:, i % 2]).then_inc(tt_ready, 1)

            @block.vector
            def _(dve):
                eye = ident.unsqueeze(1).to_broadcast([P, NH, P])
                for i in range(steps):
                    l, t = divmod(i, NT)
                    dve.wait_ge(p_done, i + 1)
                    if l < LEV - 1:
                        nc.vector.tensor_tensor(x[:, t], x[:, t] if l else eye, pp[:, i % 2], ALU.subtract)
                    nc.vector.tensor_tensor(a.xt[:, t], a.xt[:, t] if l else eye, ppt[:, i % 2], ALU.subtract).then_inc(x_ready, 1)


@phase
def phase_gdn(g, a, o):
    nc, io = g.nc, g.io
    qT, kT, vT = (a.qkvT[:, NH * i:NH * i + NH, :] for i in range(3))
    with ExitStack() as ctx:
        sb = lambda n, sh: ctx.enter_context(nc.sbuf_tensor("gdn_" + n, sh, F32))
        sem = lambda n: g.semaphore("gdn_" + n)
        eg = sb("eg", [P, 2, 2, NH])
        ge = sb("ge", [P, 2, NH, P])
        du = sb("du", [P, NH, P])
        kn = sb("kn", [P, NH, P])
        vb = sb("vb", [P, NH, P])
        kb = sb("kb", [P, NH, P])
        kd = sb("kd", [P, 2, NH, P])
        u = sb("u", [P, 2, NH, P])
        wT = sb("wT", [P, 2, NH, P])
        qk = sb("qk", [P, 2, NH, P])
        qg = sb("qg", [P, 2, NH, P])
        st = sb("st", [P, 3, NH, P])
        pr, pu, pw, pqk, pws, po, pst = (ctx.enter_context(nc.psum_tensor(f"gdn_p{i}", [P, NH, P], F32)) for i in range(7))
        (st_here, a_done, ad_act, prep_done, b_done, uw_ready, ws_done, d_ready, o_done, o_used, st_ready, du_min, du_exp,
         out_done, kn_ready) = map(sem, ("st_here", "a_done", "ad_act", "prep_done", "b_done", "uw_ready", "ws_done", "d_ready",
                                         "o_done", "o_used", "st_ready", "du_min", "du_exp", "out_done", "kn_ready"))
        s_in = lambda t: t % 2 if t < NT - 1 else 2
        s_out = lambda t: (t + 1) % 2
        with nc.Block() as block:
            @block.sync
            def _(sp):
                sp.dma_start(st[:, 2], io["state_gdn"][0, 0].rearrange("h d v -> d h v")).then_inc(st_here, 16)
                for t, name in ((NT - 2, "gdn_prompt"), (NT - 1, "gdn_sample")):
                    sp.wait_ge(st_ready, t + 2)
                    sp.dma_start(io[name][0, 0].rearrange("h d v -> d h v"), st[:, s_out(t)]).then_inc(out_done, 16)
                sp.wait_ge(out_done, 32)

            @block.tensor
            def _(pe):
                def prepare_a(t):
                    tok = slice(t * P, t * P + P)
                    if t:
                        pe.wait_ge(uw_ready, t)
                        pe.wait_ge(prep_done, t)
                    for h in range(NH):
                        nc.tensor.matmul(pr[:, h, :], a.gb[:, t, h:h + 1].to_broadcast([P, P]), g.c(K_U, P), start=True, stop=True)
                        nc.tensor.transpose(pu[:, h, :], kT[:, h, tok], g.c(K_ID, P))
                        nc.tensor.transpose(pw[:, h, :], vT[:, h, tok], g.c(K_ID, P))
                        last = nc.tensor.matmul(pqk[:, h, :], kT[:, h, tok], qT[:, h, tok], start=True, stop=True)
                    last.then_inc(a_done, 1)

                def prepare_b(t):
                    pe.wait_ge(prep_done, t + 1)
                    for h in range(NH):
                        nc.tensor.matmul(pu[:, h, :], a.xt[:, t, h, :], vb[:, h, :], start=True, stop=True)
                        last = nc.tensor.matmul(pw[:, h, :], kb[:, h, :], a.xt[:, t, h, :], start=True, stop=True)
                    last.then_inc(b_done, 1)

                prepare_a(0)
                prepare_b(0)
                for t in range(NT):
                    if t + 1 < NT:
                        prepare_a(t + 1)
                    pe.wait_ge(uw_ready, t + 1)
                    pe.wait_ge(st_ready, t + 1)
                    if t == NT - 1:
                        pe.wait_ge(st_here, 16)
                    for h in range(NH):
                        last = nc.tensor.matmul(pws[:, h, :], wT[:, t % 2, h, :], st[:, s_in(t), h, :], start=True, stop=True)
                    last.then_inc(ws_done, 1)
                    if t + 1 < NT:
                        prepare_b(t + 1)
                    pe.wait_ge(d_ready, t + 1)
                    if t:
                        pe.wait_ge(o_used, t)
                    for h in range(NH):
                        nc.tensor.matmul(pst[:, h, :], kd[:, t % 2, h, :], u[:, t % 2, h, :], start=True, stop=True)
                    for h in range(NH):
                        nc.tensor.matmul(po[:, h, :], qk[:, t % 2, h, :], u[:, t % 2, h, :], start=True, stop=False)
                        last = nc.tensor.matmul(po[:, h, :], qg[:, t % 2, h, :], st[:, s_in(t), h, :], start=False, stop=True)
                    last.then_inc(o_done, 1)

            @block.scalar
            def _(act):
                def prepare_a(t):
                    b = t % 2
                    act.wait_ge(a_done, t + 1)
                    if t:
                        act.wait_ge(prep_done, t)
                    if t >= 2:
                        act.wait_ge(st_ready, t)
                    nc.scalar.activation(eg[:, b, 0, :], a.gam[:, t, :], ACT.Exp)
                    nc.scalar.copy(kn[:], pu[:]).then_inc(kn_ready, 1)
                    act.wait_ge(du_min, t + 1)
                    nc.scalar.activation(ge[:, b], pr[:], ACT.Exp)
                    nc.scalar.activation(du[:], du[:], ACT.Exp).then_inc(du_exp, 1)

                def prepare_b(t):
                    act.wait_ge(b_done, t + 1)
                    nc.scalar.copy(u[:, t % 2], pu[:])
                    nc.scalar.copy(wT[:, t % 2], pw[:]).then_inc(uw_ready, 1)

                prepare_a(0)
                prepare_b(0)
                for t in range(NT):
                    if t + 1 < NT:
                        prepare_a(t + 1)
                        if t:
                            act.wait_ge(o_done, t)
                        prepare_b(t + 1)
                    act.wait_ge(o_done, t + 1)
                    nc.scalar.copy(o[:, t, NH * P:2 * NH * P].rearrange("p (h n) -> p h n", n=P), po[:]).then_inc(o_used, 1)

            @block.vector
            def _(dve):
                ch = g.chain(dve, "dve")

                def prepare(t):
                    b = t % 2
                    dve.wait_ge(a_done, t + 1)
                    for h in range(NH):
                        ins = nc.vector.tensor_scalar(du[:, h, :], pr[:, h, :], a.gam[:, t, h:h + 1], 0.0, ALU.subtract, ALU.min)
                    ins.then_inc(du_min, 1)
                    beta = a.gb[:, t, NH:2 * NH]
                    if t:
                        dve.wait_ge(b_done, t)
                    for h in range(NH):
                        nc.vector.tensor_scalar(vb[:, h, :], pw[:, h, :], beta[:, h:h + 1], None, ALU.mult)
                    dve.wait_ge(kn_ready, t + 1)
                    ch(nc.vector.tensor_tensor(eg[:, b, 1, :], eg[:, b, 0, :], beta, ALU.mult))
                    for h in range(NH):
                        nc.vector.tensor_scalar(kb[:, h, :], kn[:, h, :], eg[:, b, 1, h:h + 1], None, ALU.mult)
                    dve.wait_ge(du_exp, t + 1)
                    if t >= 2:
                        dve.wait_ge(o_done, t - 1)
                    for h in range(NH):
                        nc.vector.tensor_scalar(kd[:, b, h, :], kn[:, h, :], du[:, h, P - 1:P], None, ALU.mult)
                    nc.vector.tensor_tensor(qg[:, b], qT[:, :, t * P:t * P + P], ge[:, b], ALU.mult)
                    ch(nc.vector.tensor_tensor(qk[:, b], du[:], pqk[:], ALU.mult))
                    nc.vector.tensor_tensor(qk[:, b], qk[:, b], g.c(K_U, P).unsqueeze(1).to_broadcast([P, NH, P]), ALU.mult).then_inc(prep_done, 1)

                nc.vector.memset(st[:, 0], 0.0).then_inc(st_ready, 1)
                prepare(0)
                for t in range(NT):
                    if t + 1 < NT:
                        prepare(t + 1)
                    dve.wait_ge(ws_done, t + 1)
                    nc.vector.tensor_tensor(u[:, t % 2], u[:, t % 2], pws[:], ALU.subtract).then_inc(d_ready, 1)
                    dve.wait_ge(o_done, t + 1)
                    if t == NT - 1:
                        dve.wait_ge(st_here, 16)
                    for h in range(NH):
                        ins = nc.vector.scalar_tensor_tensor(st[:, s_out(t), h, :], st[:, s_in(t), h, :], ge[:, t % 2, h, P - 1:P],
                                                             pst[:, h, :], ALU.mult, ALU.add)
                    ins.then_inc(st_ready, 1)
                g.done(ch, "dve")


@phase
def phase_out(g, s, o, base, gated):
    nc, io = g.nc, g.io
    with ExitStack() as ctx:
        sb = lambda n, sh: ctx.enter_context(nc.sbuf_tensor(f"out{s}_{n}", sh, F32))
        sem = lambda n: g.semaphore(f"out{s}_{n}")
        xt = sb("x", [P, NT, D])
        gate = sb("gate", [P, 2, D])
        oT = sb("oT", [P, 2, KT, P])
        y = sb("y", [P, 2, D])
        if gated:
            gr = sb("gr", [P, 2, D])
            nw = sb("nw", [P, 2, P])
            sq = sb("sq", [P, D])
            ms = sb("ms", [P, 2, KT])
        tp = ctx.enter_context(nc.psum_tensor(f"out{s}_tp", [P, 2, KT, P], F32))
        py = ctx.enter_context(nc.psum_tensor(f"out{s}_py", [P, 2, 2, 512], F32))
        (par_here, o_ready, tp_done, oT_ready, y_done, y_ready, x_out, sq_done, ms_ready, rs_ready) = map(sem, (
            "par_here", "o_ready", "tp_done", "oT_ready", "y_done", "y_ready", "x_out", "sq_done", "ms_ready", "rs_ready"))
        x_here = [sem(f"x_here{t}") for t in range(NT)]
        gr_here = [sem(f"gr_here{b}") for b in range(2)]
        g.free_when.update({base: (y_done, NT), base + 1: (y_done, NT)})
        with nc.Block() as block:
            @block.sync
            def _(sp):
                if gated:
                    for i, name in enumerate(("gla_norm_w", "gdn_norm_w")):
                        sp.dma_start(nw[:, i, :], bcast_rows(io[name][0])).then_inc(par_here, 16)
                    for t in range(2):
                        sp.dma_start(gr[:, t, :], io["gates"][t * P:t * P + P, :]).then_inc(gr_here[t], 16)
                for c in range(2):
                    sp.dma_start(gate[:, c, :], bcast_rows(io["mod"][s, c, 2 * D:3 * D])).then_inc(par_here, 16)
                for t in range(NT):
                    sp.dma_start(xt[0:width(t), t, :], x_source(g, s, t)).then_inc(x_here[t], 16)
                if gated:
                    for t in range(2, NT):
                        sp.wait_ge(o_ready, t - 1)
                        w = width(t)
                        sp.dma_start(gr[0:w, t % 2, :], io["gates"][t * P:t * P + w, :]).then_inc(gr_here[t % 2], 16)
                for t in range(NT):
                    sp.wait_ge(y_ready, t + 1)
                    sp.dma_start(io["xres"][s][t * P:t * P + width(t), :], xt[0:width(t), t, :]).then_inc(x_out, 16)
                sp.wait_ge(x_out, 16 * NT)
                g.stream(sp, base + 2)

            @block.vector
            def _(dve):
                ch = g.chain(dve, "dve")
                dve.wait_ge(par_here, 64 if gated else 32)

                def normalise(t):
                    w = width(t)
                    heads = lambda ap: ap.rearrange("p (h n) -> p h n", n=P)
                    dve.wait_ge(sq_done, t + 1)
                    nc.vector.tensor_reduce(ms[0:w, t % 2, :], heads(sq[0:w, :]), AX.X, ALU.add).then_inc(ms_ready, 1)
                    dve.wait_ge(rs_ready, t + 1)
                    ot = o[0:w, t, :]
                    ch(nc.vector.tensor_tensor(heads(ot), heads(ot), ms[0:w, t % 2, :].unsqueeze(2).to_broadcast([w, KT, P]), ALU.mult))
                    o4 = ot.rearrange("p (a h n) -> p a h n", a=2, n=P)
                    ch(nc.vector.tensor_tensor(o4, o4, nw[0:w].unsqueeze(2).to_broadcast([w, 2, 4, P]), ALU.mult))
                    dve.wait_ge(gr_here[t % 2], 16 * (t // 2 + 1))
                    nc.vector.tensor_tensor(ot, ot, gr[0:w, t % 2, :], ALU.mult).then_inc(o_ready, 1)

                def add(t):
                    w, c = width(t), int(t == NT - 1)
                    dve.wait_ge(y_done, t + 1)
                    dve.wait_ge(x_here[t], 16)
                    if t >= 2:
                        dve.wait_ge(y_ready, t - 1)
                    ch(nc.vector.tensor_tensor(y[0:w, t % 2, :], py[0:w, t % 2].rearrange("p a n -> p (a n)"), gate[0:w, c, :], ALU.mult))
                    nc.vector.tensor_tensor(xt[0:w, t, :], xt[0:w, t, :], y[0:w, t % 2, :], ALU.add).then_inc(y_ready, 1)

                for t in range(NT):
                    if gated:
                        normalise(t)
                    if t:
                        add(t - 1)
                add(NT - 1)
                g.done(ch, "dve")

            @block.scalar
            def _(act):
                ch = g.chain(act, "act")

                def squares(t):
                    w = width(t)
                    if t:
                        act.wait_ge(ms_ready, t)
                    nc.scalar.activation(sq[0:w, :], o[0:w, t, :], ACT.Square).then_inc(sq_done, 1)
                    act.wait_ge(ms_ready, t + 1)
                    m = ms[0:w, t % 2, :]
                    ch(nc.scalar.activation(m, m, ACT.Ln, scale=1.0 / P, bias=g.eps[0:w, :]))
                    nc.scalar.activation(m, m, ACT.Exp, scale=-0.5).then_inc(rs_ready, 1)

                for t in range(NT):
                    if gated:
                        squares(t)
                    w = width(t)
                    act.wait_ge(tp_done, t + 1)
                    if t >= 2:
                        act.wait_ge(y_done, t - 1)
                    nc.scalar.copy(oT[:, t % 2, :, 0:w], tp[:, t % 2, :, 0:w]).then_inc(oT_ready, 1)
                g.done(ch, "act")

            @block.tensor
            def _(pe):
                wo = [g.chunk(pe, base + i) for i in range(2)]
                for t in range(NT):
                    w = width(t)
                    if gated:
                        pe.wait_ge(o_ready, t + 1)
                    if t >= 2:
                        pe.wait_ge(oT_ready, t - 1)
                    for k in range(KT):
                        last = nc.tensor.transpose(tp[:, t % 2, k, 0:w], o[0:w, t, k * P:(k + 1) * P], g.c(K_ID, w, w))
                    last.then_inc(tp_done, 1)
                    pe.wait_ge(oT_ready, t + 1)
                    if t >= 2:
                        pe.wait_ge(y_ready, t - 1)
                    for i in range(2):
                        for k in range(KT):
                            last = nc.tensor.matmul(py[0:w, t % 2, i, :], oT[:, t % 2, k, 0:w], wo[i][:, k, :], start=k == 0, stop=k == KT - 1)
                    last.then_inc(y_done, 1)


class Routes:

    def __init__(self, nc, ctx, l):
        sb = lambda n, sh, dt=F32: ctx.enter_context(nc.sbuf_tensor(f"{n}_{l}", sh, dt))
        self.slot = sb("slot", [P, 2, NT], I32)
        self.w = sb("route_w", [P, 2, NT])
        self.more = sb("more", [P, NOV + 1], I32)


@phase
def phase_route(g, l, hT, h, rt):
    nc, io = g.nc, g.io
    NL = NG + NE
    with ExitStack() as ctx:
        sb = lambda n, sh: ctx.enter_context(nc.sbuf_tensor(f"rt{l}_{n}", sh, F32))
        sem = lambda n: g.semaphore(f"rt{l}_{n}")
        wr = sb("w", [P, KT, NL])
        bias = sb("bias", [P, 1, NL])
        lg = sb("lg", [P, NT, NL])
        g1, g2 = sb("g1", [P, NT, NG]), sb("g2", [P, NT, NG])
        e1, e2, e3, e4 = (sb(f"e{i}", [P, NT, EG]) for i in range(1, 5))
        a1, a2, a3, a4, a5 = (sb(f"a{i}", [P, NT, 1]) for i in range(1, 6))
        o1, o2, o3, t1 = (sb(f"o{i}", [P, NT, NE]) for i in range(1, 5))
        c1, c2, c3, c4 = (sb(f"c{i}", [P, NE]) for i in range(1, 5))
        sl = sb("sl", [P, 2, NT])
        bk = sb("bk", [P, NOV, NE])
        bk2 = sb("bk2", [P, NOV + 1])
        pl = ctx.enter_context(nc.psum_tensor(f"rt{l}_pl", [P, NT, 64], F32))
        pc = ctx.enter_context(nc.psum_tensor(f"rt{l}_pc", [P, NT + 1, NE], F32))
        w_here, lg_done, ex_in, ex_out, oh_ready, pc_done, slots_ready, x_out = map(sem, (
            "w_here", "lg_done", "ex_in", "ex_out", "oh_ready", "pc_done", "slots_ready", "x_out"))
        with nc.Block() as block:
            @block.sync
            def _(sp):
                with nc.allow_non_contiguous_dma(reason="router weights"):
                    sp.dma_start(wr[:, :, 0:NG], io["moe_w_group"][l].rearrange("(p k) n -> p k n", k=KT)).then_inc(w_here, 16)
                    sp.dma_start(wr[:, :, NG:NL], io["moe_w_expert"][l].rearrange("(p k) n -> p k n", k=KT)).then_inc(w_here, 16)
                    sp.dma_start(bias[:, 0, 0:NG], bcast_rows(io["moe_b_group"][l])).then_inc(w_here, 16)
                    sp.dma_start(bias[:, 0, NG:NL], bcast_rows(io["moe_b_expert"][l])).then_inc(w_here, 16)

            @block.tensor
            def _(pe):
                pe.wait_ge(w_here, 64)
                for t in range(NT):
                    for k in range(KT):
                        last = nc.tensor.matmul(pl[0:width(t), t, 0:NL], hT[:, k, t * P:t * P + width(t)], wr[:, k, :],
                                                start=k == 0, stop=k == KT - 1)
                last.then_inc(lg_done, 1)
                pe.wait_ge(oh_ready, 1)
                for t in range(NT):
                    nc.tensor.matmul(pc[:, t, :], g.c(K_SU, P), o3[:, t, :], start=True, stop=t == 0)
                    for b in range(t):
                        nc.tensor.matmul(pc[:, t, :], g.c(K_ONE, P), o3[:, b, :], start=False, stop=b == t - 1)
                for b in range(NT):
                    last = nc.tensor.matmul(pc[:, NT, :], g.c(K_ONE, P), o3[:, b, :], start=b == 0, stop=b == NT - 1)
                last.then_inc(pc_done, 1)

            @block.scalar
            def _(act):
                for i, buf in enumerate((g2, a4)):
                    act.wait_ge(ex_in, i + 1)
                    nc.scalar.activation(buf[:], buf[:], ACT.Exp).then_inc(ex_out, 1)

            @block.vector
            def _(dve):
                ch = g.chain(dve, "dve")
                v = nc.vector
                bc = lambda ap, n: ap[:].to_broadcast([P, NT, n])
                const = lambda at, n: g.c(at, n).unsqueeze(1).to_broadcast([P, NT, n])

                def first_max(out, x, tmp, mx, order, n):
                    ch(v.tensor_reduce(mx[:], x, AX.X, ALU.max))
                    ch(v.tensor_tensor(tmp[:], x, bc(mx, n), ALU.is_equal))
                    ch(v.tensor_tensor(tmp[:], tmp[:], const(order, n), ALU.mult))
                    ch(v.tensor_reduce(a5[:], tmp[:], AX.X, ALU.max))
                    ch(v.tensor_tensor(out[:], tmp[:], bc(a5, n), ALU.is_equal))

                ch(v.memset(lg[:], 0.0))
                dve.wait_ge(lg_done, 1)
                bias_t = bias[:].to_broadcast([P, NT - 1, NL])
                ch(v.tensor_tensor(lg[:, 0:NT - 1, :], pl[:, 0:NT - 1, 0:NL], bias_t, ALU.add))
                ch(v.tensor_tensor(lg[0:DSEQ, NT - 1, :], pl[0:DSEQ, NT - 1, 0:NL], bias[0:DSEQ, 0, :], ALU.add))
                G, E = lg[:, :, 0:NG], lg[:, :, NG:NL].rearrange("p t (a b) -> p t a b", a=NG)
                first_max(g1, G, g2, a1, K_DG, NG)
                v.tensor_tensor(g2[:], G, bc(a1, NG), ALU.subtract).then_inc(ex_in, 1)
                dve.wait_ge(ex_out, 1)
                ch(v.tensor_reduce(a2[:], g2[:], AX.X, ALU.add))
                oh4 = g1[:].unsqueeze(3).to_broadcast([P, NT, NG, EG])
                T1 = t1[:].rearrange("p t (a b) -> p t a b", a=NG)
                ch(v.tensor_tensor(T1, E, oh4, ALU.mult))
                ch(v.tensor_reduce(e1[:], T1.rearrange("p t a b -> p t b a"), AX.X, ALU.add))
                first_max(e2, e1[:], e4, a1, K_DE, EG)
                ch(v.scalar_tensor_tensor(e1[:], e2[:], -1e30, e1[:], ALU.mult, ALU.add))
                first_max(e3, e1[:], e4, a3, K_DE, EG)
                v.tensor_tensor(a4[:], a3[:], a1[:], ALU.subtract).then_inc(ex_in, 1)
                for out, sel in ((o1, e2), (o2, e3)):
                    ch(v.tensor_tensor(out[:].rearrange("p t (a b) -> p t a b", a=NG), oh4,
                                       sel[:].unsqueeze(2).to_broadcast([P, NT, NG, EG]), ALU.mult))
                ch(v.tensor_tensor(o3[:], o1[:], o2[:], ALU.add))
                ch(v.memset(o3[32:64, NT - 1, :], 0.0))
                v.memset(o3[64:P, NT - 1, :], 0.0).then_inc(oh_ready, 1)
                dve.wait_ge(ex_out, 2)
                ch(v.scalar_tensor_tensor(a3[:], a4[:], 1.0, a2[:], ALU.add, ALU.mult))
                W = lambda i: rt.w[:, i, :].unsqueeze(2)
                ch(v.reciprocal(W(0), a3[:]))
                ch(v.tensor_tensor(W(1), W(0), a4[:], ALU.mult))
                dve.wait_ge(pc_done, 1)
                ch(v.tensor_copy(c1[:], pc[:, NT, :]))
                ch(v.tensor_scalar(c2[:], c1[:], float(CAP), None, ALU.is_gt))
                for m in range(2, -(-TOK // CAP)):
                    ch(v.scalar_tensor_tensor(c2[:], c1[:], float(m * CAP), c2[:], ALU.is_gt, ALU.add))
                ch(v.tensor_tensor_scan(c3[:], g.c(K_ONE, NE), c2[:], 0.0, ALU.mult, ALU.add))
                ch(v.tensor_tensor(c4[:], c3[:], c2[:], ALU.subtract))
                ch(v.tensor_scalar(c4[:], c4[:], float(NE - 1), float(CAP), ALU.add, ALU.mult))
                ch(v.tensor_tensor(c1[:], g.c(K_EC, NE), c4[:], ALU.subtract))
                row = lambda c: c[:].unsqueeze(1).to_broadcast([P, NT, NE])
                rank = pc[:, 0:NT, :]
                ch(v.tensor_scalar(t1[:], rank, float(CAP), None, ALU.is_lt))
                ch(v.tensor_tensor(t1[:], t1[:], row(c1), ALU.mult))
                ch(v.tensor_tensor(t1[:], t1[:], rank, ALU.add))
                ch(v.tensor_tensor(t1[:], t1[:], row(c4), ALU.add))
                for i, oh in enumerate((o1, o2)):
                    ch(v.tensor_tensor(oh[:], oh[:], t1[:], ALU.mult))
                    ch(v.tensor_reduce(sl[:, i, :].unsqueeze(2), oh[:], AX.X, ALU.add))
                v.tensor_copy(rt.slot[:], sl[:]).then_inc(slots_ready, 1)
                ch(v.tensor_tensor(bk[:], c3[:].unsqueeze(1).to_broadcast([P, NOV, NE]),
                                   g.c(K_B, NOV).unsqueeze(2).to_broadcast([P, NOV, NE]), ALU.is_le))
                ch(v.tensor_reduce(bk2[:, 0:NOV].unsqueeze(2), bk[:], AX.X, ALU.add))
                ch(v.tensor_scalar(bk2[:, 0:NOV], bk2[:, 0:NOV], float(NE - 1), None, ALU.min))
                ch(v.tensor_copy(bk2[:, NOV:], c3[:, NE - 1:NE]))
                ch(v.tensor_copy(rt.more[:], bk2[:]))
                g.done(ch, "dve")

            @block.gpsimd
            def _(pool):
                pool.wait_ge(slots_ready, 1)
                for t in range(NT):
                    for i in range(2):
                        pool.indirect_dma_start(
                            out=io["xslot"], out_offset=bass.IndirectOffsetOnAxis(ap=rt.slot[0:width(t), i, t:t + 1], axis=0),
                            in_=h[0:width(t), t, :], in_offset=None).then_inc(x_out, 16)
                pool.wait_ge(x_out, 32 * NT)


class ExpertBuffers:
    def __init__(self, g, ctx, name):
        nc = g.nc
        sb = lambda n, sh: ctx.enter_context(nc.sbuf_tensor(f"{name}_{n}", sh, F32))
        ps = lambda n, sh: ctx.enter_context(nc.psum_tensor(f"{name}_{n}", sh, F32))
        sem = lambda n: g.semaphore(f"{name}_{n}")
        self.x = sb("x", [CAP, 2, D])
        self.xT = sb("xT", [P, 2, KT, CAP])
        self.s = sb("s", [P, DE // P, CAP])
        self.gT = sb("gT", [P, 2, DE // P, CAP])
        self.y = sb("y", [CAP, 2, D])
        self.px = ps("px", [P, KT, CAP])
        self.p1 = ps("p1", [P, 512])
        self.p3 = ps("p3", [P, 512])
        self.py = ps("py", [CAP, 2, 2, 512])
        self.p1v = self.p1[:, 0:DE // P * CAP].rearrange("p (j c) -> p j c", c=CAP)
        self.p3v = self.p3[:, 0:DE // P * CAP].rearrange("p (j c) -> p j c", c=CAP)
        self.x_here = [sem(f"x_here{b}") for b in range(2)]
        self.y_out = [sem(f"y_out{b}") for b in range(2)]
        (self.t_done, self.xT_ready, self.h1_done, self.h3_done, self.s_ready, self.g_ready, self.y_done,
         self.y_used, self.pe_turn, self.act_turn) = map(sem, (
             "t_done", "xT_ready", "h1_done", "h3_done", "s_ready", "g_ready", "y_done", "y_used", "pe_turn", "act_turn"))
        self.nc = nc

    def transposes(self, b, ident):
        for k in range(KT):
            last = self.nc.tensor.transpose(self.px[:, k, :], self.x[:, b, k:D:KT], ident)
        last.then_inc(self.t_done, 1)

    def up(self, w, out, b, done):
        for j in range(DE // P):
            for k in range(KT):
                last = self.nc.tensor.matmul(out[:, j, :], w[:, k, j * P:(j + 1) * P], self.xT[:, b, k, :], start=k == 0, stop=k == KT - 1)
        last.then_inc(done, 1)

    def down(self, w, b):
        for i in range(2):
            for j in range(DE // P):
                last = self.nc.tensor.matmul(self.py[:, b, i, :], self.gT[:, b, j, :], w[:, j, 512 * i:512 * i + 512],
                                             start=j == 0, stop=j == DE // P - 1)
        last.then_inc(self.y_done, 1)


def ring_views(g, slots):
    shapes = (KT, KT, DE // P)
    return [g.ring[:, s, :].rearrange("p (k n) -> p k n", k=k) for s, k in zip(slots, shapes)]


@phase
def phase_experts(g, l):
    nc, io = g.nc, g.io
    base = N_MOE[l]
    slot = lambda j, i: (base + 3 * j + i) % RING
    laps = lambda j, i: (base + 3 * j + i) // RING + 1
    weights = (io["moe_w1"][l], io["moe_w3"][l], io["moe_w2"][l])
    with ExitStack() as ctx:
        m = ExpertBuffers(g, ctx, f"ex{l}")
        ident = g.c(K_ID, CAP, CAP)
        rows = lambda ap, e: ap[bass.ds(e * CAP, CAP), :]
        g.free_when.update({base + 3 * e + i: ((m.h1_done, m.h3_done, m.y_done)[i], e + 1) for e in range(NE) for i in range(3)})
        with nc.Block() as block:
            @block.sync
            def _(sp):
                def load_x(e, b):
                    sp.dma_start(m.x[:, b, :], rows(io["xslot"], e)).then_inc(m.x_here[b], 16)

                load_x(0, 0)
                load_x(1, 1)
                with sp.Fori(0, NE // 2 - 1) as i:
                    for j in range(2):
                        e = 2 * i + j
                        sp.wait_ge(m.t_done, e + 1)
                        load_x(e + 2, j)
                        for k, (w, done) in enumerate(zip(weights, (m.h1_done, m.h3_done, m.y_done))):
                            sp.wait_ge(done, e + 1)
                            src = w[bass.ds(e + 2, 1)].rearrange("o a n -> (o a) n")
                            src = src.rearrange("(p k) n -> p (k n)", k=KT) if k < 2 else src.rearrange("(k p) n -> p k n", p=P)
                            dst = g.ring[:, slot(j, k), :]
                            sp.dma_start(dst if k < 2 else dst.rearrange("p (k n) -> p k n", n=D), src).then_inc(g.arrived[slot(j, k)], 16)
                g.n_load = base + 3 * NE
                sp.wait_ge(m.t_done, NE - 1)
                load_x(NE, 0)

            @block.tensor
            def _(pe):
                pe.wait_ge(m.x_here[0], 16)
                m.transposes(0, ident)
                with pe.Fori(0, NE // 2) as i:
                    for j in range(2):
                        e = 2 * i + j
                        w1, w3, w2 = ring_views(g, [slot(j, k) for k in range(3)])
                        pe.wait_ge(m.xT_ready, e + 1)
                        pe.wait_ge(g.arrived[slot(j, 0)], 16 * i + 16 * laps(j, 0))
                        pe.wait_ge(m.s_ready, e + 1)
                        m.up(w1, m.p1v, j, m.h1_done)
                        pe.wait_ge(g.arrived[slot(j, 1)], 16 * i + 16 * laps(j, 1))
                        pe.wait_ge(m.g_ready, e + 1)
                        m.up(w3, m.p3v, j, m.h3_done)
                        pe.wait_ge(m.x_here[1 - j], 16 * i + (32 if j else 16))
                        pe.sem_inc(m.pe_turn, 1)
                        m.transposes(1 - j, ident)
                        pe.wait_ge(g.arrived[slot(j, 2)], 16 * i + 16 * laps(j, 2))
                        pe.wait_ge(m.g_ready, e + 2)
                        pe.wait_ge(m.y_used, e + 1)
                        m.down(w2, j)

            @block.scalar
            def _(act):
                nc.scalar.preload_act_table(ACT.Silu)
                act.sem_inc(m.s_ready, 1)
                act.sem_inc(m.y_used, 2)
                for b in range(2):
                    act.sem_inc(m.y_out[b], 16)
                with act.Fori(0, NE // 2) as i:
                    for j in range(2):
                        e = 2 * i + j
                        act.wait_ge(m.h1_done, e + 1)
                        nc.scalar.activation(m.s[:], m.p1v, ACT.Silu).then_inc(m.s_ready, 1)
                        act.wait_ge(m.y_done, e + 1)
                        act.wait_ge(m.y_out[j], 16 * i + 16)
                        nc.scalar.copy(m.y[:, j, :].rearrange("p (a n) -> p a n", a=2), m.py[:, j]).then_inc(m.y_used, 1)
                        act.wait_ge(m.y_used, e + 3)
                        act.dma_start(rows(io["yslot"], e), m.y[:, j, :]).then_inc(m.y_out[j], 16)
                for b in range(2):
                    act.wait_ge(m.y_out[b], 16 * (NE // 2 + 1))

            @block.vector
            def _(dve):
                dve.sem_inc(m.g_ready, 1)
                dve.wait_ge(m.t_done, 1)
                nc.vector.tensor_copy(m.xT[:, 0], m.px[:]).then_inc(m.xT_ready, 1)
                with dve.Fori(0, NE // 2) as i:
                    for j in range(2):
                        e = 2 * i + j
                        dve.wait_ge(m.s_ready, e + 2)
                        dve.wait_ge(m.h3_done, e + 1)
                        nc.vector.tensor_tensor(m.gT[:, j], m.s[:], m.p3v, ALU.mult).then_inc(m.g_ready, 1)
                        dve.wait_ge(m.t_done, e + 2)
                        nc.vector.tensor_copy(m.xT[:, 1 - j], m.px[:]).then_inc(m.xT_ready, 1)


@phase
def phase_more(g, l, rt):
    nc, io = g.nc, g.io
    weights = (io["moe_w1"][l], io["moe_w3"][l], io["moe_w2"][l])
    with ExitStack() as ctx:
        m = ExpertBuffers(g, ctx, f"mo{l}")
        here = [g.semaphore(f"mo{l}_here{s}") for s in range(RING)]
        ident = g.c(K_ID, CAP, CAP)
        rows = lambda ap, b: ap[bass.ds((b + NE) * CAP, CAP), :]
        more = rt.more

        def blocks(eng, body):
            n = eng.value_load(more[0:1, NOV:NOV + 1], min_val=0, max_val=NOV)
            with eng.Fori(0, NOV // 2) as i:
                for j in range(2):
                    with eng.If(n > 2 * i + j):
                        body(i, j, 2 * i + j)

        with nc.Block() as block:
            @block.sync
            def _(sp):
                def body(i, j, b):
                    e = sp.value_load(more[0:1, bass.ds(b, 1)], min_val=0, max_val=NE - 1)
                    sp.wait_ge(m.t_done, b + 1)
                    sp.dma_start(m.x[:, j, :], rows(io["xslot"], b)).then_inc(m.x_here[j], 16)
                    for k, (w, done) in enumerate(zip(weights, (m.h1_done, m.h3_done, m.y_done))):
                        sp.wait_ge(done, b + 1)
                        src = w[bass.ds(e, 1)].rearrange("o a n -> (o a) n")
                        src = src.rearrange("(p k) n -> p (k n)", k=KT) if k < 2 else src.rearrange("(k p) n -> p k n", p=P)
                        dst = g.ring[:, 3 * j + k, :]
                        sp.dma_start(dst if k < 2 else dst.rearrange("p (k n) -> p k n", n=D), src).then_inc(here[3 * j + k], 16)
                blocks(sp, body)

            @block.tensor
            def _(pe):
                for s in (m.t_done, m.h1_done, m.h3_done, m.y_done):
                    pe.sem_inc(s, 2)

                def body(i, j, b):
                    w1, w3, w2 = ring_views(g, [3 * j + k for k in range(3)])
                    pe.wait_ge(m.x_here[j], 16 * i + 16)
                    pe.wait_ge(m.xT_ready, b + 1)
                    pe.sem_inc(m.pe_turn, 1)
                    m.transposes(j, ident)
                    pe.wait_ge(m.xT_ready, b + 2)
                    pe.wait_ge(here[3 * j], 16 * i + 16)
                    pe.wait_ge(m.s_ready, b + 1)
                    m.up(w1, m.p1v, j, m.h1_done)
                    pe.wait_ge(here[3 * j + 1], 16 * i + 16)
                    pe.wait_ge(m.g_ready, b + 1)
                    m.up(w3, m.p3v, j, m.h3_done)
                    pe.wait_ge(here[3 * j + 2], 16 * i + 16)
                    pe.wait_ge(m.g_ready, b + 2)
                    pe.wait_ge(m.y_used, b + 1)
                    m.down(w2, j)
                blocks(pe, body)

            @block.scalar
            def _(act):
                nc.scalar.preload_act_table(ACT.Silu)
                act.sem_inc(m.s_ready, 1)
                act.sem_inc(m.y_used, 2)
                for b in range(2):
                    act.sem_inc(m.y_out[b], 16)

                def body(i, j, b):
                    act.wait_ge(m.h1_done, b + 3)
                    nc.scalar.activation(m.s[:], m.p1v, ACT.Silu).then_inc(m.s_ready, 1)
                    act.wait_ge(m.y_done, b + 3)
                    act.wait_ge(m.y_out[j], 16 * i + 16)
                    nc.scalar.copy(m.y[:, j, :].rearrange("p (a n) -> p a n", a=2), m.py[:, j]).then_inc(m.y_used, 1)
                    act.wait_ge(m.y_used, b + 3)
                    act.dma_start(rows(io["yslot"], b), m.y[:, j, :]).then_inc(m.y_out[j], 16)
                    act.wait_ge(m.y_out[j], 16 * i + 32)
                    act.sem_inc(m.act_turn, 1)
                blocks(act, body)

            @block.vector
            def _(dve):
                dve.sem_inc(m.g_ready, 1)
                dve.sem_inc(m.xT_ready, 1)

                def body(i, j, b):
                    dve.wait_ge(m.t_done, b + 3)
                    nc.vector.tensor_copy(m.xT[:, j], m.px[:]).then_inc(m.xT_ready, 1)
                    dve.wait_ge(m.s_ready, b + 2)
                    dve.wait_ge(m.h3_done, b + 3)
                    nc.vector.tensor_tensor(m.gT[:, j], m.s[:], m.p3v, ALU.mult).then_inc(m.g_ready, 1)
                blocks(dve, body)


@phase
def phase_combine(g, s, rt, last):
    nc, io = g.nc, g.io
    with ExitStack() as ctx:
        sb = lambda n, sh: ctx.enter_context(nc.sbuf_tensor(f"cb{s}_{n}", sh, F32))
        sem = lambda n: g.semaphore(f"cb{s}_{n}")
        xt = sb("x", [P, NT, D])
        y = sb("y", [P, 2, 2, D])
        gate = sb("gate", [P, 3, D])
        ss = sb("ss", [P, NT])
        junk = sb("junk", [P, D]) if last else None
        y_here = [[sem(f"y_here{b}{i}") for i in range(2)] for b in range(2)]
        x_here = [sem(f"x_here{t}") for t in range(NT)]
        gate_here, y_used, x_ready, x_out, rs_ready = map(sem, ("gate_here", "y_used", "x_ready", "x_out", "rs_ready"))
        with nc.Block() as block:
            @block.gpsimd
            def _(pool):
                for t in range(NT):
                    if t >= 2:
                        pool.wait_ge(y_used if last else x_ready, t - 1)
                    for i in range(2):
                        pool.indirect_dma_start(
                            out=y[0:width(t), t % 2, i, :], out_offset=None, in_=io["yslot"],
                            in_offset=bass.IndirectOffsetOnAxis(ap=rt.slot[0:width(t), i, t:t + 1], axis=0)).then_inc(y_here[t % 2][i], 16)

            @block.sync
            def _(sp):
                for t in range(NT):
                    sp.dma_start(xt[0:width(t), t, :], x_source(g, s, t)).then_inc(x_here[t], 16)
                for c in range(2):
                    sp.dma_start(gate[:, c, :], bcast_rows(io["mod"][s, c, 2 * D:3 * D])).then_inc(gate_here, 16)
                if last:
                    sp.dma_start(gate[:, 2, :], bcast_rows(io["final_norm_w"])).then_inc(gate_here, 16)
                for t in range(NT):
                    w = width(t)
                    sp.wait_ge(x_ready, t + 1)
                    if not last:
                        dst = io["xres"][s][t * P:t * P + w, :]
                    elif t < NT - 1:
                        dst = io["y_prompt"][0, t * P:t * P + P, :]
                    else:
                        dst = io["y_sample"][0]
                    sp.dma_start(dst, xt[0:w, t, :]).then_inc(x_out, 16)
                sp.wait_ge(x_out, 16 * NT)

            @block.scalar
            def _(act):
                if last:
                    ch = g.chain(act, "act")
                    for t in range(NT):
                        w = width(t)
                        act.wait_ge(y_used, t + 1)
                        ch(nc.scalar.activation(junk[0:w, :], xt[0:w, t, :], ACT.Square, accum_out=ss[0:w, t:t + 1]))
                        ch(nc.scalar.activation(ss[0:w, t:t + 1], ss[0:w, t:t + 1], ACT.Ln, scale=1.0 / D, bias=g.eps[0:w, :]))
                        nc.scalar.activation(ss[0:w, t:t + 1], ss[0:w, t:t + 1], ACT.Exp, scale=-0.5).then_inc(rs_ready, 1)
                    g.done(ch, "act")

            @block.vector
            def _(dve):
                ch = g.chain(dve, "dve")
                dve.wait_ge(gate_here, 48 if last else 32)

                def finish(t):
                    w = width(t)
                    dve.wait_ge(rs_ready, t + 1)
                    nc.vector.scalar_tensor_tensor(xt[0:w, t, :], xt[0:w, t, :], ss[0:w, t:t + 1], gate[0:w, 2, :],
                                                   ALU.mult, ALU.mult).then_inc(x_ready, 1)

                for t in range(NT):
                    w, c = width(t), int(t == NT - 1)
                    y1, y2 = y[0:w, t % 2, 0, :], y[0:w, t % 2, 1, :]
                    for i in range(2):
                        dve.wait_ge(y_here[t % 2][i], 16 * (t // 2 + 1))
                    ch(nc.vector.tensor_scalar(y1, y1, rt.w[0:w, 0, t:t + 1], None, ALU.mult))
                    ch(nc.vector.scalar_tensor_tensor(y1, y2, rt.w[0:w, 1, t:t + 1], y1, ALU.mult, ALU.add))
                    ch(nc.vector.tensor_tensor(y1, y1, gate[0:w, c, :], ALU.mult))
                    dve.wait_ge(x_here[t], 16)
                    nc.vector.tensor_tensor(xt[0:w, t, :], xt[0:w, t, :], y1, ALU.add).then_inc(y_used if last else x_ready, 1)
                    if last and t:
                        finish(t - 1)
                if last:
                    finish(NT - 1)
                g.done(ch, "dve")


KEYS = SEQ + PAST + DSEQ
NK = NT + 1
HALF = MH // 2
QW = NOPE + ROPE


def key_cols(j):
    return slice(j * P, j * P + (P if j < NK - 1 else DSEQ))


@phase
def phase_mla_project(g, m, hT):
    nc, io = g.nc, g.io
    base = N_MLA
    with ExitStack() as ctx:
        sb = lambda n, sh: ctx.enter_context(nc.sbuf_tensor("mp_" + n, sh, F32))
        sem = lambda n: g.semaphore("mp_" + n)
        qnw, kvnw = sb("qnw", [P, QR]), sb("kvnw", [P, KVR])
        cq = sb("cq", [P, 2, QR])
        kv = sb("kv", [P, NK, KVR + ROPE])
        junk = sb("junk", [P, QR])
        ss = sb("ss", [P, NT, 2])
        rt = sb("rt", [P, 4, ROPE // 2])
        pq, pk, pv = (ctx.enter_context(nc.psum_tensor(f"mp_p{i}", [P, 2, 512], F32)) for i in range(3))
        tp = ctx.enter_context(nc.psum_tensor("mp_tp", [P, 8, P], F32))
        par_here, cache_here, in_done, rs_ready, lat_ready, tp_done, lat_T, out_done = map(sem, (
            "par_here", "cache_here", "in_done", "rs_ready", "lat_ready", "tp_done", "lat_T", "out_done"))
        v_done, v_used = [sem(f"v_done{i}") for i in range(2)], [sem(f"v_used{i}") for i in range(2)]
        kj = lambda t: t if t < NT - 1 else NK - 1
        g.free_when.update({base: (in_done, NT), base + 1: (in_done, NT)})
        with nc.Block() as block:
            @block.sync
            def _(sp):
                sp.dma_start(qnw[:], bcast_rows(io["mla_q_norm_w"][0])).then_inc(par_here, 16)
                sp.dma_start(kvnw[:], bcast_rows(io["mla_kv_norm_w"][0])).then_inc(par_here, 16)
                sp.dma_start(kv[:, NT - 1, 0:KVR], io["cache_mla_ckv"][0, 0]).then_inc(cache_here, 16)
                sp.dma_start(kv[:, NT - 1, KVR:], io["cache_mla_krope"][0, 0]).then_inc(cache_here, 16)
                g.stream(sp, base + 2)
                for t in range(NT):
                    w = width(t)
                    sp.wait_ge(lat_ready, t + 1)
                    for name, cols in (("ckv", slice(0, KVR)), ("krope", slice(KVR, KVR + ROPE))):
                        dst = io[name + "_prompt"][0, 0, t * P:t * P + P, :] if t < NT - 1 else io[name + "_sample"][0, 0]
                        sp.dma_start(dst, kv[0:w, kj(t), cols]).then_inc(out_done, 16)
                sp.wait_ge(out_done, 32 * NT)

            @block.tensor
            def _(pe):
                wq, wk = g.chunk(pe, base), g.chunk(pe, base + 1)

                def project(t):
                    w = width(t)
                    if t >= 2:
                        pe.wait_ge(lat_ready, t - 1)
                    for out, wx, n in ((pq, wq, QR), (pk, wk, KVR + ROPE)):
                        for k in range(KT):
                            last = nc.tensor.matmul(out[0:w, t % 2, 0:n], hT[:, k, t * P:t * P + w], wx[:, k, :], start=k == 0, stop=k == KT - 1)
                    last.then_inc(in_done, 1)

                def transposes(w, j, b, turn):
                    if turn:
                        pe.wait_ge(lat_T, turn)
                    if b is not None:
                        for k in range(QR // P):
                            nc.tensor.transpose(tp[:, k, 0:w], cq[0:w, b, k * P:(k + 1) * P], g.c(K_ID, w, w))
                    for k in range(KVR // P):
                        nc.tensor.transpose(tp[:, 3 + k, 0:w], kv[0:w, j, k * P:(k + 1) * P], g.c(K_ID, w, w))
                    nc.tensor.transpose(tp[0:QW, 5, 0:w], kv[0:w, j, KVR + ROPE - QW:], g.c(K_ID, w, w)).then_inc(tp_done, 1)

                project(0)
                for t in range(NT):
                    if t + 1 < NT:
                        project(t + 1)
                    pe.wait_ge(lat_ready, t + 1)
                    transposes(width(t), kj(t), t % 2, t)
                pe.wait_ge(cache_here, 32)
                transposes(P, NT - 1, None, NT)
                pe.wait_ge(lat_T, NT + 1)
                wv = g.chunk(pe, base + 4).rearrange("p k (h c) -> p k h c", h=MH)
                for j in range(NK):
                    w = key_cols(j).stop - key_cols(j).start
                    for i in range(2):
                        if j:
                            pe.wait_ge(v_used[i], j)
                        for k in range(KVR // P):
                            last = nc.tensor.matmul(pv[0:w, i, :], m.ckvT[:, k, key_cols(j)], wv[:, k, i * HALF:(i + 1) * HALF, NOPE:],
                                                    start=k == 0, stop=k == KVR // P - 1)
                        last.then_inc(v_done[i], 1)

            @block.scalar
            def _(act):
                ch = g.chain(act, "act")
                def factors(t):
                    w = width(t)
                    act.wait_ge(in_done, t + 1)
                    for i, (src, n) in enumerate(((pq[0:w, t % 2, 0:QR], QR), (pk[0:w, t % 2, 0:KVR], KVR))):
                        ch(nc.scalar.activation(junk[0:w, 0:n], src, ACT.Square, accum_out=ss[0:w, t, i:i + 1]))
                        ch(nc.scalar.activation(ss[0:w, t, i:i + 1], ss[0:w, t, i:i + 1], ACT.Ln, scale=1.0 / n, bias=g.eps[0:w, :]))
                    nc.scalar.activation(ss[0:w, t, :], ss[0:w, t, :], ACT.Exp, scale=-0.5).then_inc(rs_ready, 1)

                def keep(w, t, j, turn):
                    act.wait_ge(tp_done, turn + 1)
                    if t is not None:
                        nc.scalar.copy(m.cqT[:, :, t * P:t * P + w], tp[:, 0:3, 0:w])
                    nc.scalar.copy(m.ckvT[:, :, key_cols(j)], tp[:, 3:5, 0:w])
                    nc.scalar.copy(m.kT[NOPE:QW, 0, key_cols(j)], tp[NOPE:QW, 5, 0:w])
                    nc.scalar.copy(m.kT[NOPE:QW, 1, key_cols(j)], tp[NOPE:QW, 5, 0:w]).then_inc(lat_T, 1)

                factors(0)
                for t in range(NT):
                    if t + 1 < NT:
                        factors(t + 1)
                    keep(width(t), t, kj(t), t)
                keep(P, None, NT - 1, NT)
                for j in range(NK):
                    w = key_cols(j).stop - key_cols(j).start
                    act.wait_ge(v_done[0], j + 1)
                    nc.scalar.copy(m.v[0:w, j, 0:512], pv[0:w, 0, :]).then_inc(v_used[0], 1)
                g.done(ch, "act")

            @block.vector
            def _(dve):
                ch = g.chain(dve, "dve")
                v = nc.vector
                dve.wait_ge(par_here, 32)
                for t in range(NT):
                    w, b, j = width(t), t % 2, kj(t)
                    dve.wait_ge(rs_ready, t + 1)
                    if t >= 2:
                        dve.wait_ge(tp_done, t - 1)
                    v.scalar_tensor_tensor(cq[0:w, b, :], pq[0:w, b, 0:QR], ss[0:w, t, 0:1], qnw[0:w, :], ALU.mult, ALU.mult)
                    v.scalar_tensor_tensor(kv[0:w, j, 0:KVR], pk[0:w, b, 0:KVR], ss[0:w, t, 1:2], kvnw[0:w, :], ALU.mult, ALU.mult)
                    x1, x2 = pk[0:w, b, KVR:KVR + 16], pk[0:w, b, KVR + 16:KVR + 32]
                    cos, sin = g.c(K_CS + t * ROPE, 16, w), g.c(K_CS + t * ROPE + 16, 16, w)
                    for i, (x, y) in enumerate(((x1, cos), (x2, sin), (x1, sin), (x2, cos))):
                        last = v.tensor_tensor(rt[0:w, i, :], x, y, ALU.mult)
                    ch(last)
                    v.tensor_tensor(kv[0:w, j, KVR:KVR + 16], rt[0:w, 0, :], rt[0:w, 1, :], ALU.subtract)
                    ch(v.tensor_tensor(kv[0:w, j, KVR + 16:], rt[0:w, 2, :], rt[0:w, 3, :], ALU.add))
                    dve.sem_inc(lat_ready, 1)
                for j in range(NK):
                    w = key_cols(j).stop - key_cols(j).start
                    dve.wait_ge(v_done[1], j + 1)
                    v.tensor_copy(m.v[0:w, j, 512:1024], pv[0:w, 1, :]).then_inc(v_used[1], 1)
                g.done(ch, "dve")


@phase
def phase_mla_queries(g, m, hf):
    nc = g.nc
    n = N_MLA + 2 + hf
    with ExitStack() as ctx:
        sem = lambda n: g.semaphore(f"mq{hf}_" + n)
        rt = ctx.enter_context(nc.sbuf_tensor(f"mq{hf}_rt", [P, 4, HALF, ROPE // 2], F32))
        ps = ctx.enter_context(nc.psum_tensor(f"mq{hf}_ps", [P, 2, 2, 512], F32))
        q_done, q_here = map(sem, ("q_done", "q_here"))
        hw = HALF // 2 * QW
        g.free_when[n] = (q_done, NT)
        with nc.Block() as block:
            @block.sync
            def _(sp):
                g.stream(sp, n + 1)

            @block.tensor
            def _(pe):
                wq = g.chunk(pe, n)
                for t in range(NT):
                    w = width(t)
                    if t >= 2:
                        pe.wait_ge(q_here, t - 1)
                    for i in range(2):
                        for k in range(QR // P):
                            last = nc.tensor.matmul(ps[0:w, t % 2, i, 0:hw], m.cqT[:, k, t * P:t * P + w], wq[:, k, i * hw:(i + 1) * hw],
                                                    start=k == 0, stop=k == QR // P - 1)
                    last.then_inc(q_done, 1)

            @block.scalar
            def _(act):
                for t in range(NT):
                    w = width(t)
                    act.wait_ge(q_done, t + 1)
                    nc.scalar.copy(m.q[0:w, t, :].rearrange("p (i n) -> p i n", i=2), ps[0:w, t % 2, :, 0:hw]).then_inc(q_here, 1)

            @block.vector
            def _(dve):
                ch = g.chain(dve, "dve")
                for t in range(NT):
                    w = width(t)
                    dve.wait_ge(q_here, t + 1)
                    qh = m.q[0:w, t, :].rearrange("p (h c) -> p h c", h=HALF)
                    x1, x2 = qh[:, :, NOPE:NOPE + 16], qh[:, :, NOPE + 16:]
                    cos, sin = (g.c(K_CS + t * ROPE + i, 16, w).unsqueeze(1).to_broadcast([w, HALF, 16]) for i in (0, 16))
                    for i, (x, y) in enumerate(((x1, cos), (x2, sin), (x1, sin), (x2, cos))):
                        last = nc.vector.tensor_tensor(rt[0:w, i], x, y, ALU.mult)
                    ch(last)
                    nc.vector.tensor_tensor(x1, rt[0:w, 0], rt[0:w, 1], ALU.subtract)
                    ch(nc.vector.tensor_tensor(x2, rt[0:w, 2], rt[0:w, 3], ALU.add))
                g.done(ch, "dve")


@phase
def phase_mla_attend(g, m, hf, o):
    nc = g.nc
    scale = QW ** -0.5
    steps = HALF * NT
    with ExitStack() as ctx:
        sb = lambda n, sh: ctx.enter_context(nc.sbuf_tensor(f"ma{hf}_{n}", sh, F32))
        sem = lambda n: g.semaphore(f"ma{hf}_{n}")
        qT = sb("qT", [QW, 2, TOK])
        p = sb("p", [P, 2, SEQ])
        pT = sb("pT", [P, 2, NT - 1, P])
        mx, nm, sm = sb("mx", [P, steps]), sb("nm", [P, steps]), sb("sm", [P, steps])
        pre = ctx.enter_context(nc.psum_tensor(f"ma{hf}_pre", [P, 2, 512], F32))
        ps = ctx.enter_context(nc.psum_tensor(f"ma{hf}_ps", [P, 2, 512], F32))
        pt = ctx.enter_context(nc.psum_tensor(f"ma{hf}_pt", [P, 2, NT - 1, P], F32))
        po = ctx.enter_context(nc.psum_tensor(f"ma{hf}_po", [P, 2, 512], F32))
        (k_done, k_ready, qT_done, qT_ready, s_done, m_ready, p_ready, t_done, pT_ready, o_done, o_ready) = map(sem, (
            "k_done", "k_ready", "qT_done", "qT_ready", "s_done", "m_ready", "p_ready", "t_done", "pT_ready", "o_done", "o_ready"))
        if hf:
            g.free_when[N_MLA + 4] = (k_done, HALF)
        keys = lambda t: slice(0, (t + 1) * P) if t < NT - 1 else slice(SEQ, KEYS)
        tiles = lambda t: list(range(t + 1)) if t < NT - 1 else [NT - 1, NT]
        cut = lambda j: key_cols(j).stop - key_cols(j).start
        with nc.Block() as block:
            @block.sync
            def _(sp):
                g.stream(sp, N_MLA + 3 + 2 * hf)

            @block.tensor
            def _(pe):
                wk = g.chunk(pe, N_MLA + 4)

                def keys_of(h):
                    if h:
                        pe.wait_ge(qT_ready, h)
                    for k in range(KVR // P):
                        lhsT = wk[:, k, (hf * HALF + h) * P:(hf * HALF + h) * P + NOPE]
                        nc.tensor.matmul(pre[0:NOPE, 0, :], lhsT, m.ckvT[:, k, 0:SEQ], start=k == 0, stop=k == KVR // P - 1)
                        last = nc.tensor.matmul(pre[0:NOPE, 1, 0:KEYS - SEQ], lhsT, m.ckvT[:, k, SEQ:KEYS], start=k == 0, stop=k == KVR // P - 1)
                    last.then_inc(k_done, 1)

                def queries_of(h):
                    pe.wait_ge(k_ready, h + 1)
                    for t in range(NT):
                        w = width(t)
                        out = pre[0:QW, 0, t * P:t * P + P] if t < NT - 1 else pre[0:QW, 1, 0:w]
                        last = nc.tensor.transpose(out, m.q[0:w, t, h * QW:(h + 1) * QW], g.c(K_ID, w, w))
                    last.then_inc(qT_done, 1)

                def scores(i):
                    h, t = divmod(i, NT)
                    w, n = width(t), keys(t).stop - keys(t).start
                    if t == 0:
                        pe.wait_ge(k_ready, h + 1)
                        pe.wait_ge(qT_ready, h + 1)
                    if i >= 2:
                        pe.wait_ge(p_ready, i - 1)
                    last = nc.tensor.matmul(ps[0:w, i % 2, 0:n], qT[:, h % 2, t * P:t * P + w], m.kT[:, h % 2, keys(t)],
                                            start=True, stop=t == NT - 1)
                    if t < NT - 1:
                        last = nc.tensor.matmul(ps[:, i % 2, n - 64:n], g.c(K_AM, P, 1), g.c(K_AM + P, 64, 1), start=False, stop=True)
                    last.then_inc(s_done, 1)

                def transposes(i):
                    t = i % NT
                    w = width(t)
                    pe.wait_ge(p_ready, i + 1)
                    if i >= 2:
                        pe.wait_ge(pT_ready, i - 1)
                    for a, j in enumerate(tiles(t)):
                        last = nc.tensor.transpose(pt[0:cut(j), i % 2, a, 0:w], p[0:w, i % 2, a * P:a * P + cut(j)], g.c(K_ID, w, w))
                    last.then_inc(t_done, 1)

                def values(i):
                    h, t = divmod(i, NT)
                    w, js = width(t), tiles(t)
                    c = (hf * HALF + h) * MV
                    pe.wait_ge(pT_ready, i + 1)
                    if i >= 2:
                        pe.wait_ge(o_ready, i - 1)
                    for a, j in enumerate(js):
                        last = nc.tensor.matmul(po[0:w, i % 2, 0:MV], pT[0:cut(j), i % 2, a, 0:w], m.v[0:cut(j), j, c:c + MV],
                                                start=a == 0, stop=a == len(js) - 1)
                    last.then_inc(o_done, 1)

                keys_of(0)
                queries_of(0)
                scores(0)
                for i in range(steps):
                    h, t = divmod(i, NT)
                    if i + 1 < steps:
                        scores(i + 1)
                    if t == 1 and h + 1 < HALF:
                        keys_of(h + 1)
                    if t == 2 and h + 1 < HALF:
                        queries_of(h + 1)
                    transposes(i)
                    if i:
                        values(i - 1)
                values(steps - 1)

            @block.scalar
            def _(act):
                def exps(i):
                    t = i % NT
                    w, n = width(t), keys(t).stop - keys(t).start
                    act.wait_ge(m_ready, i + 1)
                    if i >= 2:
                        act.wait_ge(t_done, i - 1)
                    nc.scalar.activation(p[0:w, i % 2, 0:n], ps[0:w, i % 2, 0:n], ACT.Exp, scale=scale,
                                         bias=nm[0:w, i:i + 1], accum_out=sm[0:w, i:i + 1]).then_inc(p_ready, 1)

                def keep_queries(h):
                    act.wait_ge(qT_done, h + 1)
                    nc.scalar.copy(qT[:, h % 2, 0:SEQ], pre[0:QW, 0, :])
                    nc.scalar.copy(qT[:, h % 2, SEQ:TOK], pre[0:QW, 1, 0:DSEQ]).then_inc(qT_ready, 1)

                keep_queries(0)
                exps(0)
                for i in range(steps):
                    h, t = divmod(i, NT)
                    if i + 1 < steps:
                        exps(i + 1)
                    if t == 2 and h + 1 < HALF:
                        keep_queries(h + 1)
                    act.wait_ge(t_done, i + 1)
                    if i >= 2:
                        act.wait_ge(o_done, i - 1)
                    if t < NT - 1:
                        nc.scalar.copy(pT[:, i % 2, 0:t + 1, :], pt[:, i % 2, 0:t + 1, :]).then_inc(pT_ready, 1)
                    else:
                        nc.scalar.copy(pT[:, i % 2, 0, 0:DSEQ], pt[:, i % 2, 0, 0:DSEQ])
                        nc.scalar.copy(pT[0:DSEQ, i % 2, 1, 0:DSEQ], pt[0:DSEQ, i % 2, 1, 0:DSEQ]).then_inc(pT_ready, 1)

            @block.vector
            def _(dve):
                ch = g.chain(dve, "dve")

                def maxima(i):
                    t = i % NT
                    w, n = width(t), keys(t).stop - keys(t).start
                    dve.wait_ge(s_done, i + 1)
                    ch(nc.vector.tensor_reduce(mx[0:w, i:i + 1], ps[0:w, i % 2, 0:n], AX.X, ALU.max))
                    nc.vector.tensor_scalar(nm[0:w, i:i + 1], mx[0:w, i:i + 1], -scale, None, ALU.mult).then_inc(m_ready, 1)

                def keep_keys(h):
                    dve.wait_ge(k_done, h + 1)
                    if h >= 2:
                        dve.wait_ge(s_done, NT * (h - 1))
                    nc.vector.tensor_copy(m.kT[0:NOPE, h % 2, 0:SEQ], pre[0:NOPE, 0, :])
                    nc.vector.tensor_copy(m.kT[0:NOPE, h % 2, SEQ:KEYS], pre[0:NOPE, 1, 0:KEYS - SEQ]).then_inc(k_ready, 1)

                def outputs(i):
                    h, t = divmod(i, NT)
                    w, c = width(t), (hf * HALF + h) * MV
                    ch(nc.vector.reciprocal(mx[0:w, i:i + 1], sm[0:w, i:i + 1]))
                    dve.wait_ge(o_done, i + 1)
                    nc.vector.tensor_scalar(o[0:w, t, c:c + MV], po[0:w, i % 2, 0:MV], mx[0:w, i:i + 1], None, ALU.mult).then_inc(o_ready, 1)

                keep_keys(0)
                maxima(0)
                for i in range(steps):
                    h, t = divmod(i, NT)
                    if i + 1 < steps:
                        maxima(i + 1)
                    if t == 1 and h + 1 < HALF:
                        keep_keys(h + 1)
                    if i:
                        outputs(i - 1)
                outputs(steps - 1)
                g.done(ch, "dve")


class Heads:
    pass


def layer_ab(g):
    nc = g.nc
    with ExitStack() as ctx:
        wide = ctx.enter_context(nc.sbuf_tensor("wide_ab", [P, NT * D], F32))
        hT = wide[:, 0:KT * TOK].rearrange("p (k n) -> p k n", k=KT)
        o = wide[:].rearrange("p (t n) -> p t n", t=NT)
        phase_norm(g, 0, hT, None, N_AB)
        with ExitStack() as c2:
            sb = lambda n, sh: c2.enter_context(nc.sbuf_tensor(n, sh, F32))
            a = Heads()
            a.gb = sb("gdn_gb", [P, NT, 2 * NH])
            a.gam = sb("gdn_gam", [P, NT, NH])
            a.qkvT = sb("gdn_qkvT", [P, 3 * NH, NT * P])
            with ExitStack() as c3:
                sb = lambda n, sh: c3.enter_context(nc.sbuf_tensor(n, sh, F32))
                a.qk2 = sb("gla_qk", [P, NT, 2, 2, P])
                a.b2 = sb("gla_b", [P, NT, 2, P])
                a.v = sb("gla_v", [P, NT, GH * GDV])
                phase_ab_project(g, a, hT)
                phase_gla(g, a, o)
            a.xt = c2.enter_context(nc.sbuf_tensor("gdn_xt", [P, NT, NH, P], F32))
            phase_gdn_inverse(g, a)
            phase_gdn(g, a, o)
        phase_out(g, 0, o, N_ABO, True)


def layer_mla(g):
    nc = g.nc
    with ExitStack() as ctx:
        wide = ctx.enter_context(nc.sbuf_tensor("wide_mla", [P, NT * D], F32))
        hT = wide[:, 0:KT * TOK].rearrange("p (k n) -> p k n", k=KT)
        o = wide[:].rearrange("p (t n) -> p t n", t=NT)
        phase_norm(g, 2, hT, None, N_MLA)
        with ExitStack() as c2:
            sb = lambda n, sh: c2.enter_context(nc.sbuf_tensor("mla_" + n, sh, F32))
            m = Heads()
            m.cqT = sb("cqT", [P, QR // P, TOK])
            m.ckvT = sb("ckvT", [P, KVR // P, KEYS])
            m.kT = sb("kT", [QW, 2, KEYS])
            m.v = sb("v", [P, NK, MH * MV])
            phase_mla_project(g, m, hT)
            m.q = sb("q", [P, NT, HALF * QW])
            for hf in range(2):
                phase_mla_queries(g, m, hf)
                phase_mla_attend(g, m, hf, o)
        phase_out(g, 2, o, N_MLA + 5, False)


def layer_moe(g, l):
    nc = g.nc
    s = 2 * l + 1
    with ExitStack() as ctx:
        rt = Routes(nc, ctx, l)
        with ExitStack() as c2:
            hT = c2.enter_context(nc.sbuf_tensor(f"hT_{s}", [P, KT, TOK], F32))
            h = c2.enter_context(nc.sbuf_tensor(f"h_{s}", [P, NT, D], F32))
            phase_norm(g, s, hT, h, N_MOE[l])
            phase_route(g, l, hT, h, rt)
        phase_experts(g, l)
        phase_more(g, l, rt)
        phase_combine(g, s, rt, l == 1)


OUTS = [("y_prompt", (1, SEQ, D)), ("y_sample", (1, DSEQ, D)),
        ("gla_prompt", (1, 1, GH, GDK, GDV)), ("gdn_prompt", (1, 1, NH, DK, DV)),
        ("conv_prompt", (1, 1, CW - 1, CONV)), ("ckv_prompt", (1, 1, SEQ, KVR)), ("krope_prompt", (1, 1, SEQ, ROPE)),
        ("gla_sample", (1, 1, GH, GDK, GDV)), ("gdn_sample", (1, 1, NH, DK, DV)),
        ("conv_sample", (1, 1, CW - 1, CONV)), ("ckv_sample", (1, 1, DSEQ, KVR)), ("krope_sample", (1, 1, DSEQ, ROPE))]
SCRATCH = [("mod", (4, 2, 3 * D)), ("xslot", (SLOTS, D)), ("yslot", (SLOTS, D)), ("gates", (TOK, D)),
           ("xres", (3, TOK, D))]


def build(nc, io):
    with ExitStack() as ctx:
        g = Prog(nc, ctx, io)
        g.plan = make_plan(io)
        phase_modulation(g)
        layer_ab(g)
        layer_moe(g, 0)
        layer_mla(g)
        layer_moe(g, 1)


def kernel(**inputs):
    import concourse.bacc as bacc
    from concourse.bass_utils import run_bass_kernel_spmd

    nc = bacc.Bacc("TRN2", target_bir_lowering=False, num_devices=1)
    data = {name: np.ascontiguousarray(a) for name, a in inputs.items()}
    data["cst"] = constants()
    io = {name: nc.dram_tensor("in_" + name, a.shape, F32, kind="ExternalInput").ap() for name, a in data.items()}
    for names, kind in ((OUTS, "ExternalOutput"), (SCRATCH, "Internal")):
        for name, shape in names:
            io[name] = nc.dram_tensor("out_" + name if kind == "ExternalOutput" else name, shape, F32, kind=kind).ap()
    build(nc, io)
    r = run_bass_kernel_spmd(nc, [{"in_" + name: a for name, a in data.items()}], core_ids=[0])
    return tuple(r.results[0]["out_" + name] for name, _ in OUTS)
```

```python
from contextlib import ExitStack
import math

import numpy as np
import concourse.bass as bass
from concourse import mybir

F32 = mybir.dt.float32
F32R = mybir.dt.float32r
I32 = mybir.dt.int32
ALU = mybir.AluOpType
ACT = mybir.ActivationFunctionType
AX = mybir.AxisListType

P = 128
D = 1024
KT = D // P
SEQ, DSEQ, PAST = 512, 32, 128
TOK = SEQ + DSEQ
NT = SEQ // P + 1
EPS = 1e-6
GH, GDK, GDV, GLR = 4, 64, 128, 16
NH, DK, DV = 4, 128, 128
CW = 4
CONV = NH * (2 * DK + DV)
MH, NOPE, ROPE, MV = 16, 64, 32, 64
QR, KVR = 384, 256
NG, EG = 4, 8
NE = NG * EG
NL = NG + NE
DE = 512
LEV = 7
CAP = P
NOV = 2 * TOK // CAP
NB = NE + NOV
NOBODY = 8192
RING = 3
CH = 4096

C_GV, C_LR = 2 * GH * GDK, 2 * GH * GDK + GH * GDV
C_GR = C_LR + GLR
C_QKV = C_GR + GH * GDV
C_GA = C_QKV + CONV
C_GG = C_GA + 2 * NH

K_ID, K_U, K_SU, K_ONE = 0, P, 2 * P, 3 * P
K_MT = 4 * P
K_ML = K_MT + (LEV + 1) * P
K_CS = K_ML + LEV * P
K_EC = K_CS + NT * ROPE
K_DG = K_EC + NE
K_DE = K_DG + NG
K_B = K_DE + EG
K_AM = K_B + NOV
K_IO = K_AM + P + 64
K_IB = K_IO + P
K_ID1 = K_IB + NB
K_END = K_ID1 + 2 * NT


def constants():
    c = np.zeros((P, K_END), np.float32)
    i = np.arange(P)
    c[:, K_ID:K_ID + P] = np.eye(P)
    c[:, K_U:K_U + P] = i[:, None] <= i[None, :]
    c[:, K_SU:K_SU + P] = i[:, None] < i[None, :]
    c[:, K_ONE:K_ONE + P] = 1.0
    for l in range(LEV):
        m = 1 << l
        blk = i // m
        mt = (blk[None, :] == blk[:, None] + 1) & (blk[:, None] % 2 == 0)
        c[:, K_MT + l * P:K_MT + (l + 1) * P] = mt
        c[:, K_ML + l * P:K_ML + (l + 1) * P] = mt.T
    c[:, K_MT + LEV * P:K_MT + (LEV + 1) * P] = np.eye(P)
    half = ROPE // 2
    inv = np.exp(np.float32(-math.log(10000.0)) * np.arange(half, dtype=np.float32) / np.float32(half)).astype(np.float32)
    for t in range(NT):
        pos = (i + t * P if t < NT - 1 else PAST + i).astype(np.float32)
        ang = pos[:, None] * inv[None, :]
        c[:, K_CS + t * ROPE:K_CS + t * ROPE + half] = np.cos(ang)
        c[:, K_CS + t * ROPE + half:K_CS + (t + 1) * ROPE] = np.sin(ang)
    c[:, K_EC:K_EC + NE] = np.arange(NE) * CAP
    c[:, K_DG:K_DG + NG] = NG - np.arange(NG)
    c[:, K_DE:K_DE + EG] = EG - np.arange(EG)
    c[:, K_B:K_B + NOV] = np.arange(NOV)
    c[0, K_AM:K_AM + 64] = 1.0
    c[0, K_AM + P:K_AM + P + 64] = -1e30
    c[:, K_IO:K_IO + P] = i
    c[:, K_IB:K_IB + NB] = np.arange(NB) * CAP
    for choice in range(2):
        for t in range(NT):
            c[:width(t), K_ID1 + choice * NT + t] = 1 + choice * TOK + t * P + i[:width(t)]
    return c


def width(t):
    return P if t < NT - 1 else DSEQ


class Chain:

    def __init__(self, eng, sem, at):
        self.eng, self.sem, self.n = eng, sem, at

    def __call__(self, ins):
        self.n += 1
        ins.then_inc(self.sem, 1)
        self.eng.wait_ge(self.sem, self.n)


class Prog:

    def __init__(self, nc, ctx, io):
        self.nc, self.ctx, self.io = nc, ctx, io
        self.cst = ctx.enter_context(nc.sbuf_tensor("cst", [P, K_END], F32))
        self.ring = ctx.enter_context(nc.sbuf_tensor("ring", [P, RING, CH], F32))
        self.eps = ctx.enter_context(nc.sbuf_tensor("eps", [P, 1], F32))
        self.arrived = [ctx.enter_context(nc.semaphore(f"arrived{j}")) for j in range(RING)]
        self.free_when = {}
        self.chains = {e: ctx.enter_context(nc.semaphore(f"chain_{e}")) for e in ("act", "dve", "pool")}
        self.chained = {e: 0 for e in self.chains}
        self.n_load = 0
        self.phase_sems = []
        self.plan = []

    def semaphore(self, name):
        self.phase_sems.append(self.nc.alloc_semaphore(name))
        return self.phase_sems[-1]

    def end_phase(self):
        self.free_when = {n: None for n in self.free_when}
        if len(self.phase_sems) > 120:
            self.nc.clear_and_free_semaphores(self.phase_sems)
            self.nc.all_engine_barrier()
            self.phase_sems = []

    def chain(self, eng, name):
        return Chain(eng, self.chains[name], self.chained[name])

    def done(self, chain, name):
        self.chained[name] = chain.n

    def c(self, at, n, rows=P):
        return self.cst[0:rows, at:at + n]

    def load(self, sp, n):
        src, shape = self.plan[n]
        if n >= RING and self.free_when[n - RING]:
            sp.wait_ge(*self.free_when[n - RING])
        size = shape[1] * shape[2]
        dst = self.ring[0:shape[0], n % RING, 0:size].rearrange("p (k n) -> p k n", k=shape[1])
        sp.dma_start(dst, src).then_inc(self.arrived[n % RING], 16)

    def stream(self, sp, upto):
        while self.n_load < min(upto + RING, len(self.plan)):
            self.load(sp, self.n_load)
            self.n_load += 1

    def chunk(self, pe, n):
        _, shape = self.plan[n]
        pe.wait_ge(self.arrived[n % RING], 16 * (n // RING + 1))
        return self.ring[0:shape[0], n % RING, 0:shape[1] * shape[2]].rearrange("p (k n) -> p k n", k=shape[1])


def product(nc, out, terms, first=True, last=True):
    for n, (lh, ll, rh, rl) in enumerate(terms):
        for m, (a, b) in enumerate(((lh, rh), (ll, rh), (lh, rl))):
            ins = nc.tensor.matmul(out, a, b, start=first and n + m == 0, stop=last and n == len(terms) - 1 and m == 2)
    return ins


class Splits:

    def __init__(self, g, ctx, name, units, bufs=2):
        self.g, self.units, self.bufs = g, units, bufs
        self.wh, self.wl = (ctx.enter_context(g.nc.sbuf_tensor(f"{name}_{n}", [P, bufs, CH // 2], F32R)) for n in ("wh", "wl"))
        self.hi_ready, self.lo_ready = g.semaphore(name + "_hi_ready"), g.semaphore(name + "_lo_ready")
        for u, unit in enumerate(units):
            g.free_when[unit[0]] = (self.lo_ready, u + 1)

    def views(self, u):
        n, a, b, _ = self.units[u]
        _, shape = self.g.plan[n]
        part = lambda w: w[:, u % self.bufs, 0:shape[1] * (b - a)].rearrange("p (k n) -> p k n", k=shape[1])
        w = self.g.ring[:, n % RING, 0:shape[1] * shape[2]].rearrange("p (k n) -> p k n", k=shape[1])
        return w[:, :, a:b], part(self.wh), part(self.wl)

    def hi(self, act, u):
        w, h, _ = self.views(u)
        n = self.units[u][0]
        act.wait_ge(self.g.arrived[n % RING], 16 * (n // RING + 1))
        if u >= self.bufs:
            act.wait_ge(*self.units[u - self.bufs][3])
        self.g.nc.scalar.copy(h, w).then_inc(self.hi_ready, 1)

    def lo(self, dve, u):
        w, h, l = self.views(u)
        dve.wait_ge(self.hi_ready, u + 1)
        self.g.nc.vector.tensor_tensor(l, w, h.bitcast(F32), ALU.subtract).then_inc(self.lo_ready, 1)

    def get(self, pe, u):
        pe.wait_ge(self.lo_ready, u + 1)
        return self.views(u)[1:]


def kview(w, a, b):
    return w[:, a:b].rearrange("(p k) n -> p k n", k=KT)


def make_plan(g):
    plan = []
    for s in range(4):
        w = g["ada_w"][s // 2, s % 2]
        plan += [(kview(w, 512 * j, 512 * j + 512), (P, KT, 512)) for j in range(6)]
    w = g["ab_w_in"][0]
    cols = [(0, 512), (C_GV, C_LR), (C_LR, C_GR), (C_GA, C_GG), (C_GR, C_QKV),
            (C_QKV, C_QKV + 512), (C_QKV + 512, C_QKV + 1024), (C_QKV + 1024, C_GA), (C_GG, C_GG + 512)]
    plan += [(kview(w, a, b), (P, KT, b - a)) for a, b in cols]
    wo = g["ab_w_out"][0].rearrange("(k p) n -> p k n", p=P)
    plan += [(wo[:, :, 512 * j:512 * j + 512], (P, KT, 512)) for j in range(2)]

    def moe(l):
        for e in range(NE):
            for w in (g["moe_w1"], g["moe_w3"]):
                plan.append((kview(w[l, e], 0, DE), (P, KT, DE)))
            plan.append((g["moe_w2"][l, e].rearrange("(j p) n -> p j n", p=P), (P, DE // P, D)))
    moe(0)
    w = g["mla_w_in"][0]
    plan += [(kview(w, 0, QR), (P, KT, QR)), (kview(w, QR, QR + KVR + ROPE), (P, KT, KVR + ROPE))]
    w = g["mla_w_uq"][0].rearrange("(k p) n -> p k n", p=P)
    plan += [(w[:, :, 768 * j:768 * j + 768], (P, QR // P, 768)) for j in range(2)]
    plan.append((g["mla_w_ukv"][0].rearrange("(k p) n -> p k n", p=P), (P, KVR // P, 2048)))
    wo = g["mla_w_out"][0].rearrange("(k p) n -> p k n", p=P)
    plan += [(wo[:, :, 512 * j:512 * j + 512], (P, KT, 512)) for j in range(2)]
    moe(1)
    return plan


def phase(build):
    def built(g, *args):
        build(g, *args)
        g.end_phase()
    return built


N_AB, N_ABO = 24, 33
N_MOE = [35, 138]
N_MLA = 131


@phase
def phase_modulation(g):
    nc = g.nc
    with ExitStack() as ctx:
        sb = lambda n, s, dt=F32: ctx.enter_context(nc.sbuf_tensor(n, s, dt))
        sem = lambda n: g.semaphore(n)
        cin = sb("c_in", [P, 2, KT])
        sc = sb("silu_c", [P, KT, 2])
        sh, sl = sb("silu_hi", [P, KT, 2], F32R), sb("silu_lo", [P, KT, 2], F32R)
        row = sb("mod_row", [2, 4 * 3 * D])
        ps = ctx.enter_context(nc.psum_tensor("mod_ps", [2, 8, 512], F32))
        c_here, silu_done, c_hi, c_lo, mod_mm, mod_sum, mod_out, const_here, bias_here = map(sem, (
            "c_here", "silu_done", "c_hi", "c_lo", "mod_mm", "mod_sum", "mod_out", "const_here", "bias_here"))
        units = 2 * N_AB
        split = Splits(g, ctx, "mod", [(u // 2, 256 * (u % 2), 256 * (u % 2) + 256, (mod_mm, u + 1)) for u in range(units)], 4)
        with nc.Block() as block:
            @block.sync
            def _(sp):
                for c, name in enumerate(("c_prompt", "c_sample")):
                    sp.dma_start(cin[:, c, :], g.io[name][0].rearrange("(p k) -> p k", k=KT)).then_inc(c_here, 16)
                for n in range(RING):
                    g.load(sp, n)
                g.n_load = RING
                for r in range(2):
                    sp.dma_start(row[r:r + 1, :], g.io["ada_b"].rearrange("(o l) s n -> o (l s n)", o=1)).then_inc(bias_here, 16)
                g.stream(sp, N_AB)
                sp.dma_start(g.cst[:], g.io["cst"]).then_inc(const_here, 16)
                sp.wait_ge(mod_sum, units)
                sp.dma_start(g.io["mod"].rearrange("s c n -> c s n"),
                             row[:].rearrange("c (s n) -> c s n", s=4)).then_inc(mod_out, 16)
                sp.wait_ge(mod_out, 16)
                sp.wait_ge(const_here, 16)

            @block.scalar
            def _(act):
                act.wait_ge(c_here, 32)
                nc.scalar.activation(sc[:].rearrange("p k c -> p c k"), cin[:], ACT.Silu).then_inc(silu_done, 1)
                act.wait_ge(silu_done, 1)
                nc.scalar.copy(sh[:], sc[:]).then_inc(c_hi, 1)
                for u in range(units):
                    split.hi(act, u)

            @block.tensor
            def _(pe):
                pe.wait_ge(c_lo, 1)
                for u in range(units):
                    wh, wl = split.get(pe, u)
                    if u >= 8:
                        pe.wait_ge(mod_sum, u - 7)
                    product(nc, ps[:, u % 8, 0:256], [(sh[:, k, :], sl[:, k, :], wh[:, k, :], wl[:, k, :])
                                                      for k in range(KT)]).then_inc(mod_mm, 1)

            @block.vector
            def _(dve):
                dve.wait_ge(c_hi, 1)
                nc.vector.tensor_tensor(sl[:], sc[:], sh[:].bitcast(F32), ALU.subtract).then_inc(c_lo, 1)
                for u in range(units + 3):
                    if u < units:
                        split.lo(dve, u)
                    if u == 3:
                        dve.wait_ge(bias_here, 32)
                    if u >= 3:
                        cols = slice(256 * (u - 3), 256 * (u - 2))
                        dve.wait_ge(mod_mm, u - 2)
                        nc.vector.tensor_tensor(row[:, cols], ps[:, (u - 3) % 8, 0:256], row[:, cols], ALU.add).then_inc(mod_sum, 1)

            @block.gpsimd
            def _(pool):
                nc.gpsimd.memset(g.eps[:], EPS)


def x_source(g, s, t):
    if s == 0:
        return g.io["x_prompt"][0, t * P:(t + 1) * P, :] if t < NT - 1 else g.io["x_sample"][0]
    return g.io["xres"][s - 1][t * P:t * P + width(t), :]


def bcast_rows(ap, n=P):
    return ap.partition_broadcast(n)


@phase
def phase_norm(g, s, hT, lo, h, x, base, logits=None):
    nc = g.nc
    with ExitStack() as ctx:
        sb = lambda n, sh: ctx.enter_context(nc.sbuf_tensor(f"{n}_{s}", sh, F32))
        sem = lambda n: g.semaphore(f"{n}_{s}")
        xt = sb("xt", [P, NT, D]) if x is None else x
        mod = sb("mod", [P, 2, 2, D])
        nw = sb("nw", [P, D])
        junk = sb("junk", [P, D])
        ss = sb("ss", [P, NT])
        rs = sb("rs", [P, NT])
        ht = h if h is not None else xt
        tp = ctx.enter_context(nc.psum_tensor(f"tp_{s}", [P, 2, KT, P], F32))
        x_here = [sem(f"x_here{t}") for t in range(NT)]
        ss_set, rs_done, h_done, tp_done, ht_done, lo_done = map(
            sem, ("ss_set", "rs_done", "h_done", "tp_done", "ht_done", "lo_done"))
        scale_here, shift_here = ([sem(f"{n}_here{c}") for c in range(2)] for n in ("scale", "shift"))
        if logits is not None:
            l = s // 2
            wr, bias = sb("wr", [P, KT, NL]), sb("rbias", [P, NL])
            pl = ctx.enter_context(nc.psum_tensor(f"pl_{s}", [P, NT, 64], F32))
            wr_here, lg_done, h_out = map(sem, ("wr_here", "lg_done", "h_out"))
        batches = ((0, 1), (2, 3, 4))
        with nc.Block() as block:
            @block.sync
            def _(sp):
                mod_row = lambda c, m: bcast_rows(g.io["mod"][s, c, m * D:(m + 1) * D])
                sp.dma_start(nw[:], bcast_rows(g.io["norm_w"][s // 2, s % 2])).then_inc(scale_here[0], 16)
                sp.dma_start(mod[:, 0, 1, :], mod_row(0, 1)).then_inc(scale_here[0], 16)
                for t in range(NT):
                    if x is None:
                        sp.dma_start(xt[0:width(t), t, :], x_source(g, s, t)).then_inc(x_here[t], 16)
                    if t == 0:
                        sp.dma_start(mod[:, 0, 0, :], mod_row(0, 0)).then_inc(shift_here[0], 16)
                sp.dma_start(mod[:, 1, 1, :], mod_row(1, 1)).then_inc(scale_here[1], 16)
                sp.dma_start(mod[:, 1, 0, :], mod_row(1, 0)).then_inc(shift_here[1], 16)
                if logits is not None:
                    with nc.allow_non_contiguous_dma(reason="router weights"):
                        for at, n, name in ((0, NG, "group"), (NG, NE, "expert")):
                            w = g.io["moe_w_" + name][l].rearrange("(p k) n -> p k n", k=KT)
                            sp.dma_start(wr[:, :, at:at + n], w).then_inc(wr_here, 16)
                            sp.dma_start(bias[:, at:at + n], bcast_rows(g.io["moe_b_" + name][l])).then_inc(wr_here, 16)
                g.stream(sp, base)
                if logits is not None:
                    for t in range(NT):
                        sp.wait_ge(h_done, t + 1)
                        sp.dma_start(g.io["hrow"][t * P:t * P + width(t), :], h[0:width(t), t, :]).then_inc(h_out, 16)
                    sp.wait_ge(h_out, 16 * NT)

            @block.scalar
            def _(act):
                ch = g.chain(act, "act")
                act.wait_ge(ss_set, 1)
                for tiles in batches:
                    cols = slice(tiles[0], tiles[-1] + 1)
                    for t in tiles:
                        w = width(t)
                        if x is None:
                            act.wait_ge(x_here[t], 16)
                        ch(nc.scalar.activation(junk[0:w, :], xt[0:w, t, :], ACT.Square, accum_out=ss[0:w, t:t + 1]))
                    ch(nc.scalar.activation(rs[:, cols], ss[:, cols], ACT.Ln, scale=1.0 / D, bias=g.eps[:]))
                    nc.scalar.activation(rs[:, cols], rs[:, cols], ACT.Exp, scale=-0.5).then_inc(rs_done, 1)
                for t in range(NT):
                    w = width(t)
                    act.wait_ge(tp_done, t + 1)
                    nc.scalar.copy(hT[:, :, t * P:t * P + w], tp[:, t % 2, :, 0:w]).then_inc(ht_done, 1)
                g.done(ch, "act")

            @block.vector
            def _(dve):
                ch = g.chain(dve, "dve")

                def take_lo(t):
                    tok = slice(t * P, t * P + width(t))
                    dve.wait_ge(ht_done, t + 1)
                    nc.vector.tensor_tensor(lo[:, :, tok], tp[:, t % 2, :, 0:width(t)], hT[:, :, tok].bitcast(F32), ALU.subtract).then_inc(lo_done, 1)

                nc.vector.memset(ss[:], 1.0).then_inc(ss_set, 1)
                dve.wait_ge(scale_here[0], 32)
                for t in range(NT):
                    w, c = width(t), int(t == NT - 1)
                    if t in (0, NT - 1):
                        if c:
                            dve.wait_ge(scale_here[1], 16)
                        ch(nc.vector.scalar_tensor_tensor(mod[:, c, 1, :], mod[:, c, 1, :], 1.0, nw[:], ALU.add, ALU.mult))
                    dve.wait_ge(rs_done, 1 if t in batches[0] else 2)
                    ch(nc.vector.scalar_tensor_tensor(ht[0:w, t, :], xt[0:w, t, :], rs[0:w, t:t + 1],
                                                      mod[0:w, c, 1, :], ALU.mult, ALU.mult))
                    dve.wait_ge(shift_here[c], 16)
                    nc.vector.tensor_tensor(ht[0:w, t, :], ht[0:w, t, :], mod[0:w, c, 0, :], ALU.add).then_inc(h_done, 1)
                    if lo is not None and t:
                        take_lo(t - 1)
                if lo is not None:
                    take_lo(NT - 1)
                if logits is not None:
                    ch(nc.vector.memset(logits[:], 0.0))
                    dve.wait_ge(lg_done, 1)
                    dve.wait_ge(wr_here, 64)
                    nc.vector.tensor_tensor(logits[:, 0:NT - 1, :], pl[:, 0:NT - 1, 0:NL],
                                            bias[:].unsqueeze(1).to_broadcast([P, NT - 1, NL]), ALU.add)
                    ch(nc.vector.tensor_tensor(logits[0:DSEQ, NT - 1, :], pl[0:DSEQ, NT - 1, 0:NL], bias[0:DSEQ, :], ALU.add))
                g.done(ch, "dve")

            @block.tensor
            def _(pe):
                def route(t):
                    pe.wait_ge(ht_done, t + 1)
                    for k in range(KT):
                        last = nc.tensor.matmul(pl[0:width(t), t, 0:NL], hT[:, k, t * P:t * P + width(t)], wr[:, k, :],
                                                start=k == 0, stop=k == KT - 1)
                    return last

                for t in range(NT):
                    w = width(t)
                    pe.wait_ge(h_done, t + 1)
                    if t >= 2:
                        pe.wait_ge(ht_done if lo is None else lo_done, t - 1)
                    for k in range(KT):
                        last = nc.tensor.transpose(tp[:, t % 2, k, 0:w], ht[0:w, t, k:D:KT], g.c(K_ID, w, w))
                    last.then_inc(tp_done, 1)
                    if logits is not None and t:
                        if t == 1:
                            pe.wait_ge(wr_here, 64)
                        route(t - 1)
                if logits is not None:
                    route(NT - 1).then_inc(lg_done, 1)


@phase
def phase_ab_project(g, a, hh, hl):
    nc, io = g.nc, g.io
    base = N_AB
    with ExitStack() as ctx:
        sb = lambda n, sh: ctx.enter_context(nc.sbuf_tensor(n, sh, F32))
        sem = lambda n: g.semaphore(n)
        lrT = sb("lrT", [GLR, TOK])
        wal = sb("w_alpha", [GLR, 2 * P])
        bal = sb("b_alpha", [P, 2])
        laz = sb("la_z", [P, 2, TOK])
        lae = sb("la_e", [P, 2, TOK])
        gp = sb("gate_par", [P, 2, NH])
        gab = sb("gab", [P, NT, 2 * NH])
        ge = sb("gab_e", [P, NT, 2 * NH])
        silu = sb("silu_out", [P, 2, 256])
        cw = sb("conv_w", [P, 12, CW])
        xc = sb("conv_in", [P, 2, TOK + 6])
        cv = sb("conv_sum", [P, 2, TOK + 6])
        hist0 = sb("conv_hist_in", [P, 12, 3])
        hist = sb("conv_hist", [P, 2, 12, 3])
        sq = laz
        z = ctx.enter_context(nc.psum_tensor("ab_z", [P, 2, 2, 512], F32))
        zt = ctx.enter_context(nc.psum_tensor("ab_zt", [P, 2, 512], F32))
        zs = ctx.enter_context(nc.psum_tensor("ab_zs", [P, NT, 2 * NH], F32))
        (par_here, pads_set, fm_done, fm_free, tm_done, tm_free, la_abs, la_ln, gab_done, gab_here, gab_abs, gab_exp,
         xc_ready, conv_done, conv_used, hist_done, hist_out, sq_ready, rn_ready,
         l2_done) = map(sem, (
             "par_here", "pads_set", "fm_done", "fm_free", "tm_done", "tm_free", "la_abs", "la_ln", "gab_done", "gab_here",
             "gab_abs", "gab_exp", "xc_ready", "conv_done", "conv_used", "hist_done",
             "hist_out", "sq_ready", "rn_ready", "l2_done"))
        split = Splits(g, ctx, "ab", [
            (base, 0, 256, (fm_done, 2)), (base, 256, 512, (fm_done, 4)),
            (base + 1, 0, 256, (tm_done, 5)), (base + 1, 256, 512, (tm_done, 10)),
            (base + 2, 0, GLR, (fm_done, 5)), (base + 3, 0, 2 * NH, (gab_done, 1)),
            (base + 4, 0, 256, (tm_done, 15)), (base + 4, 256, 512, (tm_done, 20))]
            + [(base + 5 + u // 2, 256 * (u % 2), 256 * (u % 2) + 256, (fm_done, 9 + 2 * u)) for u in range(6)]
            + [(base + 8, 0, 256, (tm_done, 25)), (base + 8, 256, 512, (tm_done, 30))])
        silu_used = [sem("silu_used0"), sem("silu_used1")]
        N_FM = 19

        with nc.Block() as block:
            @block.sync
            def _(sp):
                with nc.allow_non_contiguous_dma(reason="small parameters by features"):
                    sp.dma_start(wal[:], io["gla_w_alpha"][0]).then_inc(par_here, 16)
                    sp.dma_start(bal[:], io["gla_b_alpha"][0].rearrange("(j p) -> p j", p=P)).then_inc(par_here, 16)
                    sp.dma_start(gp[:, 0, :], bcast_rows(io["gdn_dt_bias"][0])).then_inc(par_here, 16)
                    sp.dma_start(gp[:, 1, :], bcast_rows(io["gdn_a_log"][0])).then_inc(par_here, 16)
                    for i in range(CW):
                        sp.dma_start(cw[:, :, i], io["gdn_conv_w"][0, i].rearrange("(f p) -> p f", p=P)).then_inc(par_here, 16)
                    for i in range(3):
                        sp.dma_start(hist0[:, :, i], io["state_gdn_conv"][0, 0, i].rearrange("(f p) -> p f", p=P)).then_inc(par_here, 16)
                    g.stream(sp, N_ABO)
                    sp.wait_ge(hist_done, 12)
                    for c, name in enumerate(("conv_prompt", "conv_sample")):
                        for i in range(3):
                            sp.dma_start(io[name][0, 0, i].rearrange("(f p) -> p f", p=P), hist[:, c, :, i]).then_inc(hist_out, 16)
                    sp.wait_ge(hist_out, 96)

            @block.tensor
            def _(pe):
                def halves(i, m, product):
                    if i >= 2:
                        pe.wait_ge(fm_free, i - 1)
                    product(z[0:m, i % 2, 0, 0:256], slice(0, 256))
                    product(z[0:m, i % 2, 1, 0:TOK - 256], slice(256, TOK)).then_inc(fm_done, 1)

                def fm_unit(u, i):
                    wh, wl = split.get(pe, u)
                    n = wh.shape[2]
                    for f in range(-(-n // P)):
                        cols = slice(f * P, min((f + 1) * P, n))
                        halves(i + f, cols.stop - cols.start, lambda out, tok: product(
                            nc, out, [(wh[:, k, cols], wl[:, k, cols], hh[:, k, tok], hl[:, k, tok]) for k in range(KT)]))

                def tm_unit(u, out, j):
                    wh, wl = split.get(pe, u)
                    for t in range(NT):
                        tok = slice(t * P, t * P + width(t))
                        if j is not None and j + t >= 2:
                            pe.wait_ge(tm_free, j + t - 1)
                        last = product(nc, out(t), [(hh[:, k, tok], hl[:, k, tok], wh[:, k, :], wl[:, k, :]) for k in range(KT)])
                        if j is not None:
                            last.then_inc(tm_done, 1)
                    return last

                tm = lambda u, j: tm_unit(u, lambda t: zt[0:width(t), (j + t) % 2, 0:256], j)
                fm_unit(0, 0)
                fm_unit(1, 2)
                tm(2, 0)
                tm(3, NT)
                fm_unit(4, 4)
                pe.wait_ge(fm_free, 5)
                pe.wait_ge(par_here, 176)
                for j in range(2):
                    halves(5 + j, P, lambda out, tok: nc.tensor.matmul(out, wal[:, j * P:(j + 1) * P], lrT[:, tok], start=True, stop=True))
                tm_unit(5, lambda t: zs[0:width(t), t, :], None).then_inc(gab_done, 1)
                tm(6, 2 * NT)
                tm(7, 3 * NT)
                for u in range(6):
                    fm_unit(8 + u, 7 + 2 * u)
                tm(14, 4 * NT)
                tm(15, 5 * NT)
                for f in range(8):
                    i = N_FM + f
                    pe.wait_ge(sq_ready, f + 1)
                    halves(i, P, lambda out, tok: nc.tensor.matmul(out, g.c(K_ONE, P), sq[:, f % 2, tok], start=True, stop=True))

            @block.scalar
            def _(act):
                ch = g.chain(act, "act")

                def evac_fm(i, prompt, sample, func=ACT.Copy, **kw):
                    m = prompt.shape[0]
                    zp = z[0:m, i % 2, :, 0:256]
                    if len(prompt.shape) == 3:
                        zp = zp.rearrange("p h (a b) -> p h a b", b=P)
                        prompt = prompt.rearrange("p (h a) b -> p h a b", h=2)
                    else:
                        prompt = prompt.rearrange("p (h n) -> p h n", h=2)
                    nc.scalar.activation(prompt, zp, func, **kw)
                    nc.scalar.activation(sample, z[0:m, i % 2, 1, 256:TOK - 256], func, **kw).then_inc(fm_free, 1)

                def gate(j):
                    t, part, b = j % NT, j // NT - 2, j % 2
                    w = width(t)
                    act.wait_ge(tm_done, j + 1)
                    if j - 2 * NT >= 2:
                        act.wait_ge(silu_used[b], 16 * ((j - 2 * NT) // 2))
                    nc.scalar.activation(silu[0:w, b, :], zt[0:w, j % 2, 0:256], ACT.Silu).then_inc(tm_free, 1)
                    act.wait_ge(tm_free, j + 1)
                    act.dma_start(io["gates"][t * P:t * P + w, part * 256:part * 256 + 256], silu[0:w, b, :]).then_inc(silu_used[b], 16)

                def conv_silu(f):
                    act.wait_ge(conv_done, f + 1)
                    nc.scalar.activation(a.qkvT[:, f, 0:SEQ], cv[:, f % 2, 0:SEQ], ACT.Silu)
                    nc.scalar.activation(a.qkvT[:, f, SEQ:TOK], cv[:, f % 2, SEQ + 3:TOK + 3], ACT.Silu).then_inc(conv_used, 1)

                def l2(f):
                    i = N_FM + f
                    act.wait_ge(fm_done, i + 1)
                    if f >= 2:
                        act.wait_ge(l2_done, f - 1)
                    nc.scalar.activation(cv[:, f % 2, 0:256], z[:, i % 2, 0, 0:256], ACT.Ln, bias=g.eps[:])
                    nc.scalar.activation(cv[:, f % 2, 256:TOK], z[:, i % 2, 1, 0:TOK - 256], ACT.Ln, bias=g.eps[:]).then_inc(fm_free, 1)
                    act.wait_ge(fm_free, i + 1)
                    nc.scalar.activation(cv[:, f % 2, 0:TOK], cv[:, f % 2, 0:TOK], ACT.Exp, scale=-0.5).then_inc(rn_ready, 1)

                def values(u):
                    for j in range(u * NT, u * NT + NT):
                        t = j % NT
                        act.wait_ge(tm_done, j + 1)
                        nc.scalar.copy(a.v[0:width(t), t, u * 256:u * 256 + 256], zt[0:width(t), j % 2, 0:256]).then_inc(tm_free, 1)

                split.hi(act, 0)
                split.hi(act, 1)
                act.wait_ge(pads_set, 6)
                for i in range(4):
                    act.wait_ge(fm_done, i + 1)
                    evac_fm(i, a.qk2[:, 0:4, i // 2, i % 2, :], a.qk2[:, 4, i // 2, i % 2, 0:DSEQ],
                            scale=GDK ** -0.5 if i < 2 else 1.0)
                    if i % 2:
                        split.hi(act, 2 + i // 2)
                for u in range(2):
                    values(u)
                    split.hi(act, 4 + u)
                act.wait_ge(fm_done, 5)
                evac_fm(4, lrT[:, 0:SEQ], lrT[:, SEQ:TOK])
                split.hi(act, 6)
                act.wait_ge(par_here, 176)
                for j in range(2):
                    act.wait_ge(fm_done, 6 + j)
                    evac_fm(5 + j, laz[:, j, 0:SEQ], laz[:, j, SEQ:TOK], ACT.Identity, bias=bal[:, j:j + 1])
                act.wait_ge(gab_done, 1)
                nc.scalar.copy(gab[:, 0:4, :], zs[:, 0:4, :])
                nc.scalar.copy(gab[0:DSEQ, 4, :], zs[0:DSEQ, 4, :]).then_inc(gab_here, 1)
                split.hi(act, 7)
                act.wait_ge(la_abs, 1)
                ch(nc.scalar.activation(lae[:], lae[:], ACT.Exp, scale=-1.0))
                nc.scalar.activation(lae[:], lae[:], ACT.Ln, bias=1.0).then_inc(la_ln, 1)
                act.wait_ge(gab_abs, 2)
                ch(nc.scalar.activation(ge[:], ge[:], ACT.Exp, scale=-1.0))
                ch(nc.scalar.activation(gp[:, 1, :], gp[:, 1, :], ACT.Exp))
                nc.scalar.activation(ge[:, :, 0:NH], ge[:, :, 0:NH], ACT.Ln, bias=1.0).then_inc(gab_exp, 1)
                for u in range(2, 4):
                    for j in range(u * NT, u * NT + NT):
                        gate(j)
                    split.hi(act, 6 + u)
                for f in range(12):
                    act.wait_ge(fm_done, 8 + f)
                    if f >= 2:
                        act.wait_ge(hist_done, f - 1)
                        act.wait_ge(conv_done, f - 1)
                    evac_fm(7 + f, xc[:, f % 2, 3:3 + SEQ], xc[:, f % 2, SEQ + 6:TOK + 6])
                    if f % 2:
                        split.hi(act, 10 + f // 2)
                    if f:
                        conv_silu(f - 1)
                conv_silu(11)
                for j in range(4 * NT, 6 * NT):
                    gate(j)
                act.wait_ge(conv_used, 12)
                for f in range(8):
                    if f >= 2:
                        act.wait_ge(fm_done, N_FM + f - 1)
                    nc.scalar.activation(sq[:, f % 2, :], a.qkvT[:, f, 0:TOK], ACT.Square).then_inc(sq_ready, 1)
                    if f:
                        l2(f - 1)
                l2(7)
                for b in range(2):
                    act.wait_ge(silu_used[b], 16 * 2 * NT)
                g.done(ch, "act")

            @block.gpsimd
            def _(pool):
                for ap in (a.qk2[:, 4, :, :, DSEQ:P], a.v[:, 4, :], a.b2[:, 4, :, :], a.qkvT[:, :, TOK:NT * P], gab[:]):
                    nc.gpsimd.memset(ap, 0.0).then_inc(pads_set, 1)
                nc.gpsimd.memset(xc[:, :, 0:3], 0.0).then_inc(pads_set, 1)
                pool.wait_ge(par_here, 176)
                for f in range(12):
                    if f >= 2:
                        pool.wait_ge(conv_done, f - 1)
                    nc.gpsimd.tensor_copy(xc[:, f % 2, SEQ + 3:SEQ + 6], hist0[:, f, :]).then_inc(xc_ready, 1)
                    pool.wait_ge(fm_free, 8 + f)
                    nc.gpsimd.tensor_copy(hist[:, 0, f, :], xc[:, f % 2, SEQ:SEQ + 3])
                    nc.gpsimd.tensor_copy(hist[:, 1, f, :], xc[:, f % 2, TOK + 3:TOK + 6]).then_inc(hist_done, 1)

            @block.vector
            def _(dve):
                ch = g.chain(dve, "dve")
                for u in range(6):
                    split.lo(dve, u)
                dve.wait_ge(fm_free, 7)
                nc.vector.scalar_tensor_tensor(lae[:], laz[:], -1.0, laz[:], ALU.mult, ALU.max).then_inc(la_abs, 1)
                split.lo(dve, 6)
                dve.wait_ge(gab_here, 1)
                dve.wait_ge(par_here, 176)
                ch(nc.vector.tensor_tensor(gab[:, :, 0:NH], gab[:, :, 0:NH], gp[:, 0:1, :].to_broadcast([P, NT, NH]), ALU.add))
                nc.vector.scalar_tensor_tensor(ge[:, :, 0:NH], gab[:, :, 0:NH], -1.0, gab[:, :, 0:NH], ALU.mult, ALU.max).then_inc(gab_abs, 1)
                nc.vector.tensor_copy(ge[:, :, NH:], gab[:, :, NH:]).then_inc(gab_abs, 1)
                split.lo(dve, 7)
                dve.wait_ge(la_ln, 1)
                ch(nc.vector.scalar_tensor_tensor(laz[:], laz[:], 0.0, lae[:], ALU.min, ALU.subtract))
                for j in range(2):
                    nc.vector.tensor_scalar(a.b2[:, 0:4, j, :], laz[:, j, 0:SEQ].rearrange("p (t n) -> p t n", n=P), 1.0 / 16.0, None, ALU.mult)
                    ch(nc.vector.tensor_scalar(a.b2[:, 4, j, 0:DSEQ], laz[:, j, SEQ:TOK], 1.0 / 16.0, None, ALU.mult))
                for t in range(NT):
                    for j in range(2):
                        ch(nc.vector.tensor_tensor_scan(lae[:, 0, 0:P], g.c(K_ONE, P), a.b2[:, t, j, :], 0.0, ALU.mult, ALU.add))
                        ch(nc.vector.tensor_copy(a.b2[:, t, j, :], lae[:, 0, 0:P]))
                dve.wait_ge(gab_exp, 1)
                ch(nc.vector.scalar_tensor_tensor(gab[:, :, 0:NH], gab[:, :, 0:NH], 0.0, ge[:, :, 0:NH], ALU.max, ALU.add))
                ch(nc.vector.scalar_tensor_tensor(a.gb[:, :, 0:NH], gab[:, :, 0:NH], -1.0, gp[:, 1:2, :].to_broadcast([P, NT, NH]), ALU.mult, ALU.mult))
                ch(nc.vector.memset(a.gb[32:64, NT - 1, 0:NH], 0.0))
                ch(nc.vector.memset(a.gb[64:P, NT - 1, 0:NH], 0.0))
                ch(nc.vector.tensor_scalar(ge[:, :, NH:], ge[:, :, NH:], 1.0, None, ALU.add))
                ch(nc.vector.reciprocal(a.gb[:, :, NH:], ge[:, :, NH:]))
                split.lo(dve, 8)
                split.lo(dve, 9)
                n = TOK + 3
                for f in range(12):
                    dve.wait_ge(fm_free, 8 + f)
                    dve.wait_ge(xc_ready, f + 1)
                    if f >= 2:
                        dve.wait_ge(conv_used, f - 1)
                    x, o = xc[:, f % 2, :], cv[:, f % 2, 0:n]
                    ch(nc.vector.tensor_scalar(o, x[:, 0:n], cw[:, f, 0:1], None, ALU.mult))
                    for i in range(1, CW):
                        ins = nc.vector.scalar_tensor_tensor(o, x[:, i:i + n], cw[:, f, i:i + 1], o, ALU.mult, ALU.add)
                        if i < CW - 1:
                            ch(ins)
                    ins.then_inc(conv_done, 1)
                    if f % 2:
                        split.lo(dve, 10 + f // 2)
                for f in range(8):
                    dve.wait_ge(rn_ready, f + 1)
                    q = a.qkvT[:, f, 0:TOK]
                    nc.vector.scalar_tensor_tensor(q, q, DK ** -0.5 if f < 4 else 1.0, cv[:, f % 2, 0:TOK],
                                                   ALU.mult, ALU.mult).then_inc(l2_done, 1)
                g.done(ch, "dve")


@phase
def phase_gla(g, a, o):
    nc, io = g.nc, g.io
    with ExitStack() as ctx:
        sb = lambda n, sh: ctx.enter_context(nc.sbuf_tensor("gla_" + n, sh, F32))
        sem = lambda n: g.semaphore("gla_" + n)
        em = sb("em", [P, 2, LEV, 2 * P])
        qe = sb("qe", [P, 2, 2, P])
        ke = sb("ke", [P, 2, 2, P])
        ket = sb("ket", [P, 2, P])
        mk = o[:, 0:2, GH * P:].rearrange("p a (l n) -> p a l n", n=P)
        at = sb("at", [P, GH, P])
        st = sb("st", [P, 3, 2, P])
        el = sb("el", [P, 2, 2, 1])
        ps = ctx.enter_context(nc.psum_tensor("gla_ps", [P, 2, LEV + 1, P], F32))
        pk = ctx.enter_context(nc.psum_tensor("gla_pk", [P, 2, P], F32))
        po = ctx.enter_context(nc.psum_tensor("gla_po", [P, 2, 4, P], F32))
        pst = ctx.enter_context(nc.psum_tensor("gla_pst", [P, 2, P], F32))
        (st_here, x_ready, e_ready, m_ready, s_done, at_ready, kt_done, kt_ready, o_done, o_used, st_done,
         st_ready, out_done) = map(sem, ("st_here", "x_ready", "e_ready", "m_ready", "s_done", "at_ready", "kt_done",
                                         "kt_ready", "o_done", "o_used", "st_done", "st_ready", "out_done"))
        s_in = lambda t: t % 2 if t < NT - 1 else 2
        s_out = lambda t: (t + 1) % 2

        with nc.Block() as block:
            @block.sync
            def _(sp):
                sp.dma_start(st[:, 2, :, :], io["state_gla"][0, 0].rearrange("(j h) d v -> (h d) j v", j=2)).then_inc(st_here, 16)
                g.stream(sp, N_ABO)
                for t, name in ((NT - 2, "gla_prompt"), (NT - 1, "gla_sample")):
                    sp.wait_ge(st_ready, t + 1)
                    sp.dma_start(io[name][0, 0].rearrange("(j h) d v -> (h d) j v", j=2), st[:, s_out(t), :, :]).then_inc(out_done, 16)
                sp.wait_ge(out_done, 32)

            @block.vector
            def _(dve):
                ch = g.chain(dve, "dve")

                def exponents(t):
                    if t >= 2:
                        dve.wait_ge(s_done, GH * (t - 1))
                    for l in range(LEV):
                        m = 1 << l
                        b = a.b2[:, t].rearrange("p j (n x m) -> p (j n) x m", x=2, m=m)
                        e = em[:, t % 2, l].rearrange("p (n x m) -> p n x m", x=2, m=m)
                        mid = b[:, :, 0, m - 1:m].to_broadcast([P, P // m, m])
                        nc.vector.tensor_tensor(e[:, :, 1, :], b[:, :, 1, :], mid, ALU.subtract)
                        nc.vector.tensor_tensor(e[:, :, 0, :], mid, b[:, :, 0, :], ALU.subtract)
                    if t >= 2:
                        dve.wait_ge(kt_done, t - 1)
                    last = a.b2[:, t, :, P - 1:P]
                    nc.vector.tensor_tensor(ke[:, t % 2], last.to_broadcast([P, 2, P]), a.b2[:, t], ALU.subtract).then_inc(x_ready, 1)

                def decayed(t):
                    dve.wait_ge(e_ready, t + 1)
                    for l in range(LEV):
                        m = 1 << l
                        q = a.qk2[:, t, 0].rearrange("p j (n x m) -> p (j n) x m", x=2, m=m)
                        k = a.qk2[:, t, 1].rearrange("p j (n x m) -> p (j n) x m", x=2, m=m)
                        e = em[:, t % 2, l].rearrange("p (n x m) -> p n x m", x=2, m=m)
                        nc.vector.tensor_tensor(e[:, :, 1, :], e[:, :, 1, :], q[:, :, 1, :], ALU.mult)
                        nc.vector.tensor_tensor(e[:, :, 0, :], e[:, :, 0, :], k[:, :, 0, :], ALU.mult)
                    nc.vector.tensor_tensor(qe[:, t % 2], qe[:, t % 2], a.qk2[:, t, 0], ALU.mult)
                    nc.vector.tensor_tensor(ke[:, t % 2], ke[:, t % 2], a.qk2[:, t, 1], ALU.mult).then_inc(m_ready, 1)

                ch(nc.vector.memset(st[:, 0, :, :], 0.0))
                exponents(0)
                decayed(0)
                for t in range(NT):
                    if t + 1 < NT:
                        exponents(t + 1)
                    for h in range(GH):
                        if h == 2 and t + 1 < NT:
                            decayed(t + 1)
                        u = GH * t + h
                        dve.wait_ge(s_done, u + 1)
                        if u:
                            dve.wait_ge(at_ready, u)
                        ch(nc.vector.tensor_tensor(mk, ps[:, u % 2].rearrange("p (a l) n -> p a l n", a=2),
                                                   g.c(K_MT, (LEV + 1) * P).rearrange("p (a l n) -> p a l n", a=2, n=P), ALU.mult))
                        if t:
                            dve.wait_ge(o_done, t)
                        nc.vector.tensor_reduce(at[:, h, :], mk.rearrange("p a l n -> p n a l"), AX.XY, ALU.add).then_inc(at_ready, 1)
                    dve.wait_ge(st_done, t + 1)
                    if t == NT - 1:
                        dve.wait_ge(st_here, 16)
                    for j in range(2):
                        ins = nc.vector.scalar_tensor_tensor(st[:, s_out(t), j, :], st[:, s_in(t), j, :], el[:, t % 2, j, :],
                                                             pst[:, j, :], ALU.mult, ALU.add)
                    ins.then_inc(st_ready, 1)
                g.done(ch, "dve")

            @block.scalar
            def _(act):
                def exps(t):
                    act.wait_ge(x_ready, t + 1)
                    nc.scalar.activation(em[:, t % 2], em[:, t % 2], ACT.Exp)
                    if t >= 2:
                        act.wait_ge(o_done, t - 1)
                        act.wait_ge(st_ready, t - 1)
                    nc.scalar.activation(qe[:, t % 2], a.b2[:, t], ACT.Exp)
                    nc.scalar.activation(el[:, t % 2], a.b2[:, t, :, P - 1:P], ACT.Exp)
                    nc.scalar.activation(ke[:, t % 2], ke[:, t % 2], ACT.Exp).then_inc(e_ready, 1)

                exps(0)
                for t in range(NT):
                    act.wait_ge(kt_done, t + 1)
                    if t:
                        act.wait_ge(st_done, t)
                    nc.scalar.copy(ket[:], pk[:]).then_inc(kt_ready, 1)
                    if t + 1 < NT:
                        exps(t + 1)
                    act.wait_ge(o_done, t + 1)
                    nc.scalar.copy(o[:, t, 0:GH * P].rearrange("p (j b n) -> p b j n", b=2, n=P), po[:, :, 0:2, :]).then_inc(o_used, 1)

            @block.tensor
            def _(pe):
                for t in range(NT):
                    pe.wait_ge(m_ready, t + 1)
                    if t:
                        pe.wait_ge(kt_ready, t)
                    for j in range(2):
                        last = nc.tensor.transpose(pk[:, j, :], ke[:, t % 2, j, :], g.c(K_ID, P))
                    last.then_inc(kt_done, 1)
                    for h in range(GH):
                        u = GH * t + h
                        r, j = slice(64 * (h % 2), 64 * (h % 2) + 64), h // 2
                        if u >= 2:
                            pe.wait_ge(at_ready, u - 1)
                        for l in range(LEV):
                            m = em[r, t % 2, l, j * P:(j + 1) * P]
                            nc.tensor.matmul(ps[:, u % 2, l, :], m, m, start=True, stop=True)
                        nc.tensor.matmul(ps[:, u % 2, LEV, :], a.qk2[r, t, 1, j, :], a.qk2[r, t, 0, j, :],
                                         start=True, stop=True).then_inc(s_done, 1)
                    pe.wait_ge(kt_ready, t + 1)
                    if t:
                        pe.wait_ge(st_ready, t)
                        pe.wait_ge(o_used, t)
                    for h in range(GH):
                        r = slice(64 * (h % 2), 64 * (h % 2) + 64)
                        last = nc.tensor.matmul(pst[r, h // 2, :], ket[:, h // 2, r], a.v[:, t, h * P:(h + 1) * P], start=True, stop=True)
                    last.then_inc(st_done, 1)
                    if t == NT - 1:
                        pe.wait_ge(st_here, 16)
                    if t == 0:
                        pe.wait_ge(at_ready, 1)
                    for h in range(GH):
                        r = slice(64 * (h % 2), 64 * (h % 2) + 64)
                        pe.wait_ge(at_ready, GH * t + h + 1)
                        nc.tensor.matmul(po[:, h % 2, h // 2, :], at[:, h, :], a.v[:, t, h * P:(h + 1) * P], start=True, stop=False)
                        last = nc.tensor.matmul(po[:, h % 2, h // 2, :], qe[r, t % 2, h // 2, :], st[r, s_in(t), h // 2, :], start=False, stop=True)
                    last.then_inc(o_done, 1)


@phase
def phase_gdn_inverse(g, a):
    nc, io = g.nc, g.io
    kT = a.qkvT[:, NH:2 * NH, :]
    with ExitStack() as ctx:
        sb = lambda n, sh: ctx.enter_context(nc.sbuf_tensor("inv_" + n, sh, F32))
        sem = lambda n: g.semaphore("inv_" + n)
        lm = sb("lm", [P, NT, NH, P])
        x = sb("x", [P, NT, NH, P])
        ll = sb("ll", [P, 2, NH, P])
        tt = sb("tt", [P, 2, NH, P])
        lr_done, gam_ready, dl_ready, dl_exp, lm_ready = map(sem, ("lr_done", "gam_ready", "dl_ready", "dl_exp", "lm_ready"))
        with ExitStack() as c2:
            pr = c2.enter_context(nc.psum_tensor("inv_pr", [P, 2, NH, P], F32))
            pkk = c2.enter_context(nc.psum_tensor("inv_pkk", [P, 2, NH, P], F32))
            pg = c2.enter_context(nc.psum_tensor("inv_pg", [P, 2, 512], F32))
            with nc.Block() as block:
                @block.tensor
                def _(pe):
                    for t in range(NT):
                        b = t % 2
                        if t >= 2:
                            pe.wait_ge(lm_ready, t - 1)
                        nc.tensor.matmul(pg[:, b, 0:NH], g.c(K_U, P), a.gb[:, t, 0:NH], start=True, stop=True)
                        for h in range(NH):
                            tok = slice(t * P, t * P + P)
                            nc.tensor.matmul(pr[:, b, h, :], a.gb[:, t, h:h + 1].to_broadcast([P, P]), g.c(K_U, P), start=True, stop=True)
                            last = nc.tensor.matmul(pkk[:, b, h, :], kT[:, h, tok], kT[:, h, tok], start=True, stop=True)
                        last.then_inc(lr_done, 1)

                @block.scalar
                def _(act):
                    for t in range(NT):
                        act.wait_ge(lr_done, t + 1)
                        nc.scalar.copy(a.gam[:, t, :], pg[:, t % 2, 0:NH]).then_inc(gam_ready, 1)
                        act.wait_ge(dl_ready, t + 1)
                        nc.scalar.activation(lm[:, t], lm[:, t], ACT.Exp, scale=-1.0).then_inc(dl_exp, 1)

                @block.vector
                def _(dve):
                    for t in range(NT):
                        dve.wait_ge(gam_ready, t + 1)
                        for h in range(NH):
                            ins = nc.vector.tensor_scalar(lm[:, t, h, :], pr[:, t % 2, h, :], a.gam[:, t, h:h + 1], 0.0, ALU.subtract, ALU.max)
                        ins.then_inc(dl_ready, 1)
                        dve.wait_ge(dl_exp, t + 1)
                        for h in range(NH):
                            ins = nc.vector.scalar_tensor_tensor(lm[:, t, h, :], pkk[:, t % 2, h, :], a.gb[:, t, NH + h:NH + h + 1],
                                                                 lm[:, t, h, :], ALU.mult, ALU.mult)
                        ins.then_inc(lm_ready, 1)
        ptt = ctx.enter_context(nc.psum_tensor("inv_ptt", [P, 2, NH, P], F32))
        pp = ctx.enter_context(nc.psum_tensor("inv_pp", [P, 2, NH, P], F32))
        ppt = ctx.enter_context(nc.psum_tensor("inv_ppt", [P, 2, NH, P], F32))
        ll_ready, tt_done, tt_ready, p_done, x_ready = map(sem, ("ll_ready", "tt_done", "tt_ready", "p_done", "x_ready"))
        steps = LEV * NT
        ident = g.c(K_ID, P)
        with nc.Block() as block:
            @block.gpsimd
            def _(pool):
                for i in range(steps):
                    l, t = divmod(i, NT)
                    if i >= 2:
                        pool.wait_ge(tt_done, i - 1)
                    mask = g.c(K_ML + l * P, P).unsqueeze(1).to_broadcast([P, NH, P])
                    nc.gpsimd.tensor_tensor(ll[:, i % 2], lm[:, t], mask, ALU.mult).then_inc(ll_ready, 1)

            @block.tensor
            def _(pe):
                def product_t(i):
                    l, t = divmod(i, NT)
                    pe.wait_ge(ll_ready, i + 1)
                    if l:
                        pe.wait_ge(x_ready, i - NT + 1)
                    if i >= 2:
                        pe.wait_ge(tt_ready, i - 1)
                    for h in range(NH):
                        last = nc.tensor.matmul(ptt[:, i % 2, h, :], ll[:, i % 2, h, :], a.xt[:, t, h, :] if l else ident, start=True, stop=True)
                    last.then_inc(tt_done, 1)

                def correction(i):
                    l, t = divmod(i, NT)
                    pe.wait_ge(tt_ready, i + 1)
                    if i >= 2:
                        pe.wait_ge(x_ready, i - 1)
                    for h in range(NH):
                        if l < LEV - 1:
                            nc.tensor.matmul(pp[:, i % 2, h, :], tt[:, i % 2, h, :], x[:, t, h, :] if l else ident, start=True, stop=True)
                        last = nc.tensor.matmul(ppt[:, i % 2, h, :], x[:, t, h, :] if l else ident, tt[:, i % 2, h, :], start=True, stop=True)
                    last.then_inc(p_done, 1)

                for i in range(steps):
                    product_t(i)
                    if i:
                        correction(i - 1)
                correction(steps - 1)

            @block.scalar
            def _(act):
                for i in range(steps):
                    act.wait_ge(tt_done, i + 1)
                    if i >= 2:
                        act.wait_ge(p_done, i - 1)
                    nc.scalar.copy(tt[:, i % 2], ptt[:, i % 2]).then_inc(tt_ready, 1)

            @block.vector
            def _(dve):
                eye = ident.unsqueeze(1).to_broadcast([P, NH, P])
                for i in range(steps):
                    l, t = divmod(i, NT)
                    dve.wait_ge(p_done, i + 1)
                    if l < LEV - 1:
                        nc.vector.tensor_tensor(x[:, t], x[:, t] if l else eye, pp[:, i % 2], ALU.subtract)
                    nc.vector.tensor_tensor(a.xt[:, t], a.xt[:, t] if l else eye, ppt[:, i % 2], ALU.subtract).then_inc(x_ready, 1)


@phase
def phase_gdn(g, a, o):
    nc, io = g.nc, g.io
    qT, kT, vT = (a.qkvT[:, NH * i:NH * i + NH, :] for i in range(3))
    with ExitStack() as ctx:
        sb = lambda n, sh: ctx.enter_context(nc.sbuf_tensor("gdn_" + n, sh, F32))
        sem = lambda n: g.semaphore("gdn_" + n)
        eg = sb("eg", [P, 2, 2, NH])
        ge = sb("ge", [P, 2, NH, P])
        du = sb("du", [P, NH, P])
        kn = sb("kn", [P, NH, P])
        vb = sb("vb", [P, NH, P])
        kb = sb("kb", [P, NH, P])
        kd = sb("kd", [P, 2, NH, P])
        u = sb("u", [P, 2, NH, P])
        wT = sb("wT", [P, 2, NH, P])
        qk = sb("qk", [P, 2, NH, P])
        qg = sb("qg", [P, 2, NH, P])
        st = sb("st", [P, 3, NH, P])
        pr, pu, pw, pqk, pws, po, pst = (ctx.enter_context(nc.psum_tensor(f"gdn_p{i}", [P, NH, P], F32)) for i in range(7))
        (st_here, a_done, ad_act, prep_done, b_done, uw_ready, ws_done, d_ready, o_done, o_used, st_ready, du_min, du_exp,
         out_done, kn_ready) = map(sem, ("st_here", "a_done", "ad_act", "prep_done", "b_done", "uw_ready", "ws_done", "d_ready",
                                         "o_done", "o_used", "st_ready", "du_min", "du_exp", "out_done", "kn_ready"))
        s_in = lambda t: t % 2 if t < NT - 1 else 2
        s_out = lambda t: (t + 1) % 2
        with nc.Block() as block:
            @block.sync
            def _(sp):
                sp.dma_start(st[:, 2], io["state_gdn"][0, 0].rearrange("h d v -> d h v")).then_inc(st_here, 16)
                for t, name in ((NT - 2, "gdn_prompt"), (NT - 1, "gdn_sample")):
                    sp.wait_ge(st_ready, t + 2)
                    sp.dma_start(io[name][0, 0].rearrange("h d v -> d h v"), st[:, s_out(t)]).then_inc(out_done, 16)
                sp.wait_ge(out_done, 32)

            @block.tensor
            def _(pe):
                def prepare_a(t):
                    tok = slice(t * P, t * P + P)
                    if t:
                        pe.wait_ge(uw_ready, t)
                        pe.wait_ge(prep_done, t)
                    for h in range(NH):
                        nc.tensor.matmul(pr[:, h, :], a.gb[:, t, h:h + 1].to_broadcast([P, P]), g.c(K_U, P), start=True, stop=True)
                        nc.tensor.transpose(pu[:, h, :], kT[:, h, tok], g.c(K_ID, P))
                        nc.tensor.transpose(pw[:, h, :], vT[:, h, tok], g.c(K_ID, P))
                        last = nc.tensor.matmul(pqk[:, h, :], kT[:, h, tok], qT[:, h, tok], start=True, stop=True)
                    last.then_inc(a_done, 1)

                def prepare_b(t):
                    pe.wait_ge(prep_done, t + 1)
                    for h in range(NH):
                        nc.tensor.matmul(pu[:, h, :], a.xt[:, t, h, :], vb[:, h, :], start=True, stop=True)
                        last = nc.tensor.matmul(pw[:, h, :], kb[:, h, :], a.xt[:, t, h, :], start=True, stop=True)
                    last.then_inc(b_done, 1)

                prepare_a(0)
                prepare_b(0)
                for t in range(NT):
                    if t + 1 < NT:
                        prepare_a(t + 1)
                    pe.wait_ge(uw_ready, t + 1)
                    pe.wait_ge(st_ready, t + 1)
                    if t == NT - 1:
                        pe.wait_ge(st_here, 16)
                    for h in range(NH):
                        last = nc.tensor.matmul(pws[:, h, :], wT[:, t % 2, h, :], st[:, s_in(t), h, :], start=True, stop=True)
                    last.then_inc(ws_done, 1)
                    if t + 1 < NT:
                        prepare_b(t + 1)
                    pe.wait_ge(d_ready, t + 1)
                    if t:
                        pe.wait_ge(o_used, t)
                    for h in range(NH):
                        nc.tensor.matmul(pst[:, h, :], kd[:, t % 2, h, :], u[:, t % 2, h, :], start=True, stop=True)
                    for h in range(NH):
                        nc.tensor.matmul(po[:, h, :], qk[:, t % 2, h, :], u[:, t % 2, h, :], start=True, stop=False)
                        last = nc.tensor.matmul(po[:, h, :], qg[:, t % 2, h, :], st[:, s_in(t), h, :], start=False, stop=True)
                    last.then_inc(o_done, 1)

            @block.scalar
            def _(act):
                def prepare_a(t):
                    b = t % 2
                    act.wait_ge(a_done, t + 1)
                    if t:
                        act.wait_ge(prep_done, t)
                    if t >= 2:
                        act.wait_ge(st_ready, t)
                    nc.scalar.activation(eg[:, b, 0, :], a.gam[:, t, :], ACT.Exp)
                    nc.scalar.copy(kn[:], pu[:]).then_inc(kn_ready, 1)
                    act.wait_ge(du_min, t + 1)
                    nc.scalar.activation(ge[:, b], pr[:], ACT.Exp)
                    nc.scalar.activation(du[:], du[:], ACT.Exp).then_inc(du_exp, 1)

                def prepare_b(t):
                    act.wait_ge(b_done, t + 1)
                    nc.scalar.copy(u[:, t % 2], pu[:])
                    nc.scalar.copy(wT[:, t % 2], pw[:]).then_inc(uw_ready, 1)

                prepare_a(0)
                prepare_b(0)
                for t in range(NT):
                    if t + 1 < NT:
                        prepare_a(t + 1)
                        if t:
                            act.wait_ge(o_done, t)
                        prepare_b(t + 1)
                    act.wait_ge(o_done, t + 1)
                    nc.scalar.copy(o[:, t, NH * P:2 * NH * P].rearrange("p (h n) -> p h n", n=P), po[:]).then_inc(o_used, 1)

            @block.vector
            def _(dve):
                ch = g.chain(dve, "dve")

                def prepare(t):
                    b = t % 2
                    dve.wait_ge(a_done, t + 1)
                    for h in range(NH):
                        ins = nc.vector.tensor_scalar(du[:, h, :], pr[:, h, :], a.gam[:, t, h:h + 1], 0.0, ALU.subtract, ALU.min)
                    ins.then_inc(du_min, 1)
                    beta = a.gb[:, t, NH:2 * NH]
                    if t:
                        dve.wait_ge(b_done, t)
                    for h in range(NH):
                        nc.vector.tensor_scalar(vb[:, h, :], pw[:, h, :], beta[:, h:h + 1], None, ALU.mult)
                    dve.wait_ge(kn_ready, t + 1)
                    ch(nc.vector.tensor_tensor(eg[:, b, 1, :], eg[:, b, 0, :], beta, ALU.mult))
                    for h in range(NH):
                        nc.vector.tensor_scalar(kb[:, h, :], kn[:, h, :], eg[:, b, 1, h:h + 1], None, ALU.mult)
                    dve.wait_ge(du_exp, t + 1)
                    if t >= 2:
                        dve.wait_ge(o_done, t - 1)
                    for h in range(NH):
                        nc.vector.tensor_scalar(kd[:, b, h, :], kn[:, h, :], du[:, h, P - 1:P], None, ALU.mult)
                    nc.vector.tensor_tensor(qg[:, b], qT[:, :, t * P:t * P + P], ge[:, b], ALU.mult)
                    ch(nc.vector.tensor_tensor(qk[:, b], du[:], pqk[:], ALU.mult))
                    nc.vector.tensor_tensor(qk[:, b], qk[:, b], g.c(K_U, P).unsqueeze(1).to_broadcast([P, NH, P]), ALU.mult).then_inc(prep_done, 1)

                nc.vector.memset(st[:, 0], 0.0).then_inc(st_ready, 1)
                prepare(0)
                for t in range(NT):
                    if t + 1 < NT:
                        prepare(t + 1)
                    dve.wait_ge(ws_done, t + 1)
                    nc.vector.tensor_tensor(u[:, t % 2], u[:, t % 2], pws[:], ALU.subtract).then_inc(d_ready, 1)
                    dve.wait_ge(o_done, t + 1)
                    if t == NT - 1:
                        dve.wait_ge(st_here, 16)
                    for h in range(NH):
                        ins = nc.vector.scalar_tensor_tensor(st[:, s_out(t), h, :], st[:, s_in(t), h, :], ge[:, t % 2, h, P - 1:P],
                                                             pst[:, h, :], ALU.mult, ALU.add)
                    ins.then_inc(st_ready, 1)
                g.done(ch, "dve")


@phase
def phase_out(g, s, o, xt, base, gated):
    nc, io = g.nc, g.io
    UNITS = D // 256
    batches = ((0, 1), (2, 3, 4))
    with ExitStack() as ctx:
        sb = lambda n, sh, dt=F32: ctx.enter_context(nc.sbuf_tensor(f"out{s}_{n}", sh, dt))
        sem = lambda n: g.semaphore(f"out{s}_{n}")
        gate = sb("gate", [P, 2, D])
        oh, ol = sb("oh", [P, KT, TOK], F32R), sb("ol", [P, KT, TOK], F32R)
        y = sb("y", [P, 2, 256])
        if gated:
            gr = sb("gr", [P, 2, D])
            nw = sb("nw", [P, 2, P])
            sq = sb("sq", [P, 2, D])
            ms = sb("ms", [P, NT, KT])
        tp = ctx.enter_context(nc.psum_tensor(f"out{s}_tp", [P, 2, KT, P], F32))
        py = ctx.enter_context(nc.psum_tensor(f"out{s}_py", [P, 4, 512], F32))
        (par_here, o_ready, tp_done, oh_ready, ol_ready, y_done, y_ready, x_out, sq_done, ms_ready, rs_ready) = map(sem, (
            "par_here", "o_ready", "tp_done", "oh_ready", "ol_ready", "y_done", "y_ready", "x_out", "sq_done", "ms_ready",
            "rs_ready"))
        x_here = [sem(f"x_here{t}") for t in range(NT)]
        gr_here = [sem(f"gr_here{b}") for b in range(2)]
        split = Splits(g, ctx, f"out{s}", [(base + u // 2, 256 * (u % 2), 256 * (u % 2) + 256, (y_done, NT * (u + 1))) for u in range(UNITS)])
        with nc.Block() as block:
            @block.sync
            def _(sp):
                if gated:
                    for i, name in enumerate(("gla_norm_w", "gdn_norm_w")):
                        sp.dma_start(nw[:, i, :], bcast_rows(io[name][0])).then_inc(par_here, 16)
                    for t in range(2):
                        sp.dma_start(gr[:, t, :], io["gates"][t * P:t * P + P, :]).then_inc(gr_here[t], 16)
                for c in range(2):
                    sp.dma_start(gate[:, c, :], bcast_rows(io["mod"][s, c, 2 * D:3 * D])).then_inc(par_here, 16)
                for t in range(NT):
                    sp.dma_start(xt[0:width(t), t, :], x_source(g, s, t)).then_inc(x_here[t], 16)
                if gated:
                    for t in range(2, NT):
                        sp.wait_ge(o_ready, t - 1)
                        w = width(t)
                        sp.dma_start(gr[0:w, t % 2, :], io["gates"][t * P:t * P + w, :]).then_inc(gr_here[t % 2], 16)
                g.stream(sp, base + 2)
                for t in range(NT):
                    sp.wait_ge(y_ready, (UNITS - 1) * NT + t + 1)
                    sp.dma_start(io["xres"][s][t * P:t * P + width(t), :], xt[0:width(t), t, :]).then_inc(x_out, 16)
                sp.wait_ge(x_out, 16 * NT)

            @block.vector
            def _(dve):
                ch = g.chain(dve, "dve")
                heads = lambda ap: ap.rearrange("p (h n) -> p h n", n=P)

                def normalise(t):
                    w = width(t)
                    ot = o[0:w, t, :]
                    ch(nc.vector.tensor_tensor(heads(ot), heads(ot), ms[0:w, t, :].unsqueeze(2).to_broadcast([w, KT, P]), ALU.mult))
                    o4 = ot.rearrange("p (a h n) -> p a h n", a=2, n=P)
                    ch(nc.vector.tensor_tensor(o4, o4, nw[0:w].unsqueeze(2).to_broadcast([w, 2, 4, P]), ALU.mult))
                    dve.wait_ge(gr_here[t % 2], 16 * (t // 2 + 1))
                    nc.vector.tensor_tensor(ot, ot, gr[0:w, t % 2, :], ALU.mult).then_inc(o_ready, 1)

                def take_lo(t):
                    tok = slice(t * P, t * P + width(t))
                    dve.wait_ge(oh_ready, t + 1)
                    nc.vector.tensor_tensor(ol[:, :, tok], tp[:, t % 2, :, 0:width(t)], oh[:, :, tok].bitcast(F32), ALU.subtract).then_inc(ol_ready, 1)

                def add(u, t):
                    w, c, n = width(t), int(t == NT - 1), u * NT + t
                    cols = slice(256 * u, 256 * u + 256)
                    dve.wait_ge(y_done, n + 1)
                    dve.wait_ge(x_here[t], 16)
                    ch(nc.vector.tensor_tensor(y[0:w, n % 2, :], py[0:w, n % 4, 0:256], gate[0:w, c, cols], ALU.mult))
                    nc.vector.tensor_tensor(xt[0:w, t, cols], xt[0:w, t, cols], y[0:w, n % 2, :], ALU.add).then_inc(y_ready, 1)

                def sums(tiles):
                    for t in tiles:
                        w = width(t)
                        dve.wait_ge(sq_done, t + 1)
                        nc.vector.tensor_reduce(ms[0:w, t, :], heads(sq[0:w, t % 2, :]), AX.X, ALU.add).then_inc(ms_ready, 1)

                if gated:
                    ch(nc.vector.memset(ms[:], 1.0))
                    sums(batches[0])
                split.lo(dve, 0)
                split.lo(dve, 1)
                dve.wait_ge(par_here, 64 if gated else 32)
                for t in range(NT):
                    if gated:
                        if t == 1:
                            sums(batches[1])
                        dve.wait_ge(rs_ready, 1 if t in batches[0] else 2)
                        normalise(t)
                    if t:
                        take_lo(t - 1)
                    if t >= 2:
                        add(0, t - 2)
                take_lo(NT - 1)
                add(0, NT - 2)
                add(0, NT - 1)
                split.lo(dve, 2)
                for u in range(1, UNITS):
                    for t in range(NT):
                        add(u, t)
                    if u + 2 < UNITS:
                        split.lo(dve, u + 2)
                g.done(ch, "dve")

            @block.scalar
            def _(act):
                ch = g.chain(act, "act")
                def factors(tiles):
                    for t in tiles:
                        w = width(t)
                        if t >= 2:
                            act.wait_ge(ms_ready, t - 1)
                        nc.scalar.activation(sq[0:w, t % 2, :], o[0:w, t, :], ACT.Square).then_inc(sq_done, 1)
                    m = ms[:, tiles[0]:tiles[-1] + 1, :]
                    act.wait_ge(ms_ready, tiles[-1] + 1)
                    ch(nc.scalar.activation(m, m, ACT.Ln, scale=1.0 / P, bias=g.eps[:]))
                    nc.scalar.activation(m, m, ACT.Exp, scale=-0.5).then_inc(rs_ready, 1)

                if gated:
                    factors(batches[0])
                split.hi(act, 0)
                split.hi(act, 1)
                if gated:
                    factors(batches[1])
                for t in range(NT):
                    w = width(t)
                    act.wait_ge(tp_done, t + 1)
                    nc.scalar.copy(oh[:, :, t * P:t * P + w], tp[:, t % 2, :, 0:w]).then_inc(oh_ready, 1)
                for u in range(2, UNITS):
                    split.hi(act, u)
                g.done(ch, "act")

            @block.tensor
            def _(pe):
                def transposes(t):
                    w = width(t)
                    if gated:
                        pe.wait_ge(o_ready, t + 1)
                    if t >= 2:
                        pe.wait_ge(ol_ready, t - 1)
                    for k in range(KT):
                        last = nc.tensor.transpose(tp[:, t % 2, k, 0:w], o[0:w, t, k * P:(k + 1) * P], g.c(K_ID, w, w))
                    last.then_inc(tp_done, 1)

                transposes(0)
                for u in range(UNITS):
                    wh, wl = split.get(pe, u)
                    for t in range(NT):
                        w, n = width(t), u * NT + t
                        tok = slice(t * P, t * P + w)
                        if u == 0:
                            if t + 1 < NT:
                                transposes(t + 1)
                            pe.wait_ge(ol_ready, t + 1)
                        if n >= 4:
                            pe.wait_ge(y_ready, n - 3)
                        product(nc, py[0:w, n % 4, 0:256], [(oh[:, k, tok], ol[:, k, tok], wh[:, k, :], wl[:, k, :])
                                                            for k in range(KT)]).then_inc(y_done, 1)


class Routes:

    def __init__(self, nc, ctx, l):
        sb = lambda n, sh, dt=F32: ctx.enter_context(nc.sbuf_tensor(f"{n}_{l}", sh, dt))
        self.logits = sb("logits", [P, NT, NL])
        self.take = sb("take", [P, NB], I32)
        self.put = sb("put", [P, NB], I32)
        self.w = sb("route_w", [P, 2, NT])
        self.more = sb("more", [P, NOV + 1], I32)


@phase
def phase_route(g, l, rt):
    nc, io = g.nc, g.io
    with ExitStack() as ctx:
        sb = lambda n, sh: ctx.enter_context(nc.sbuf_tensor(f"rt{l}_{n}", sh, F32))
        sem = lambda n: g.semaphore(f"rt{l}_{n}")
        lg = rt.logits
        pre = sb("pre", [P, NT + 1, NE])
        g1, g2 = sb("g1", [P, NT, NG]), sb("g2", [P, NT, NG])
        e1, e2, e3, e4 = (sb(f"e{i}", [P, NT, EG]) for i in range(1, 5))
        a1, a2, a3, a4, a5 = (sb(f"a{i}", [P, NT, 1]) for i in range(1, 6))
        o1, o2, o3, t1 = (sb(f"o{i}", [P, NT, NE]) for i in range(1, 5))
        c1, c2, c3, c4 = (sb(f"c{i}", [P, NE]) for i in range(1, 5))
        sl, sb1 = sb("sl", [P, 2 * NT]), sb("sb1", [P, 2 * NT, 1])
        blk = sb("blk", [P, 2 * NT, NB])
        pos = sb("pos", [P, 2 * NT, P])
        who, gap = sb("who", [P, NB]), sb("gap", [P, NB])
        pw = ctx.enter_context(nc.psum_tensor(f"rt{l}_pw", [P, NB], F32))
        bk = sb("bk", [P, NOV, NE])
        bk2 = sb("bk2", [P, NOV + 1])
        pc = ctx.enter_context(nc.psum_tensor(f"rt{l}_pc", [P, NT + 1, NE], F32))
        ex_in, ex_out, oh_ready, pc_done, slots_ready, who_done = map(sem, (
            "ex_in", "ex_out", "oh_ready", "pc_done", "slots_ready", "who_done"))
        with nc.Block() as block:
            @block.tensor
            def _(pe):
                pe.wait_ge(oh_ready, 1)
                nc.tensor.matmul(pc[:], g.c(K_ONE, P), pre[:], start=True, stop=False)
                nc.tensor.matmul(pc[:, 0:NT, :], g.c(K_SU, P), o3[:], start=False, stop=True).then_inc(pc_done, 1)
                pe.wait_ge(slots_ready, 1)
                for i in range(2 * NT):
                    last = nc.tensor.matmul(pw[:], pos[:, i, :], blk[:, i, :], start=i == 0, stop=i == 2 * NT - 1)
                last.then_inc(who_done, 1)

            @block.scalar
            def _(act):
                for i, buf in enumerate((g2, a4)):
                    act.wait_ge(ex_in, i + 1)
                    nc.scalar.activation(buf[:], buf[:], ACT.Exp).then_inc(ex_out, 1)

            @block.vector
            def _(dve):
                ch = g.chain(dve, "dve")
                v = nc.vector
                bc = lambda ap, n: ap[:].to_broadcast([P, NT, n])
                const = lambda at, n: g.c(at, n).unsqueeze(1).to_broadcast([P, NT, n])

                def first_max(out, x, tmp, mx, order, n):
                    ch(v.tensor_reduce(mx[:], x, AX.X, ALU.max))
                    ch(v.tensor_tensor(tmp[:], x, bc(mx, n), ALU.is_equal))
                    ch(v.tensor_tensor(tmp[:], tmp[:], const(order, n), ALU.mult))
                    ch(v.tensor_reduce(a5[:], tmp[:], AX.X, ALU.max))
                    ch(v.tensor_tensor(out[:], tmp[:], bc(a5, n), ALU.is_equal))

                G, E = lg[:, :, 0:NG], lg[:, :, NG:NL].rearrange("p t (a b) -> p t a b", a=NG)
                first_max(g1, G, g2, a1, K_DG, NG)
                v.tensor_tensor(g2[:], G, bc(a1, NG), ALU.subtract).then_inc(ex_in, 1)
                dve.wait_ge(ex_out, 1)
                ch(v.tensor_reduce(a2[:], g2[:], AX.X, ALU.add))
                oh4 = g1[:].unsqueeze(3).to_broadcast([P, NT, NG, EG])
                T1 = t1[:].rearrange("p t (a b) -> p t a b", a=NG)
                ch(v.tensor_tensor(T1, E, oh4, ALU.mult))
                ch(v.tensor_reduce(e1[:], T1.rearrange("p t a b -> p t b a"), AX.X, ALU.add))
                first_max(e2, e1[:], e4, a1, K_DE, EG)
                ch(v.scalar_tensor_tensor(e1[:], e2[:], -1e30, e1[:], ALU.mult, ALU.add))
                first_max(e3, e1[:], e4, a3, K_DE, EG)
                v.tensor_tensor(a4[:], a3[:], a1[:], ALU.subtract).then_inc(ex_in, 1)
                for out, sel in ((o1, e2), (o2, e3)):
                    ch(v.tensor_tensor(out[:].rearrange("p t (a b) -> p t a b", a=NG), oh4,
                                       sel[:].unsqueeze(2).to_broadcast([P, NT, NG, EG]), ALU.mult))
                ch(v.tensor_tensor(o3[:], o1[:], o2[:], ALU.add))
                v.memset(o3[32:64, NT - 1, :], 0.0)
                v.memset(pre[:, 0, :], 0.0)
                ch(v.memset(o3[64:P, NT - 1, :], 0.0))
                for t in range(NT):
                    ins = v.tensor_tensor(pre[:, t + 1, :], pre[:, t, :], o3[:, t, :], ALU.add)
                    if t < NT - 1:
                        ch(ins)
                ins.then_inc(oh_ready, 1)
                dve.wait_ge(ex_out, 2)
                ch(v.scalar_tensor_tensor(a3[:], a4[:], 1.0, a2[:], ALU.add, ALU.mult))
                W = lambda i: rt.w[:, i, :].unsqueeze(2)
                ch(v.reciprocal(W(0), a3[:]))
                ch(v.tensor_tensor(W(1), W(0), a4[:], ALU.mult))
                dve.wait_ge(pc_done, 1)
                ch(v.tensor_copy(c1[:], pc[:, NT, :]))
                ch(v.tensor_scalar(c2[:], c1[:], float(CAP), None, ALU.is_gt))
                for m in range(2, -(-TOK // CAP)):
                    ch(v.scalar_tensor_tensor(c2[:], c1[:], float(m * CAP), c2[:], ALU.is_gt, ALU.add))
                ch(v.tensor_tensor_scan(c3[:], g.c(K_ONE, NE), c2[:], 0.0, ALU.mult, ALU.add))
                ch(v.tensor_tensor(c4[:], c3[:], c2[:], ALU.subtract))
                ch(v.tensor_scalar(c4[:], c4[:], float(NE - 1), float(CAP), ALU.add, ALU.mult))
                ch(v.tensor_tensor(c1[:], g.c(K_EC, NE), c4[:], ALU.subtract))
                row = lambda c: c[:].unsqueeze(1).to_broadcast([P, NT, NE])
                rank = pc[:, 0:NT, :]
                ch(v.tensor_scalar(t1[:], rank, float(CAP), None, ALU.is_lt))
                ch(v.tensor_tensor(t1[:], t1[:], row(c1), ALU.mult))
                ch(v.tensor_tensor(t1[:], t1[:], rank, ALU.add))
                ch(v.tensor_tensor(t1[:], t1[:], row(c4), ALU.add))
                for i, oh in enumerate((o1, o2)):
                    ch(v.tensor_tensor(oh[:], oh[:], t1[:], ALU.mult))
                    ch(v.tensor_reduce(sl[:, i * NT:(i + 1) * NT].unsqueeze(2), oh[:], AX.X, ALU.add))
                every = lambda ap, n: ap.to_broadcast([P, 2 * NT, n])
                starts, places = g.c(K_IB, NB).unsqueeze(1), g.c(K_IO, P).unsqueeze(1)
                ch(v.tensor_tensor(blk[:], every(sl[:].unsqueeze(2), NB), every(starts, NB), ALU.is_ge))
                ch(v.tensor_reduce(sb1[:], blk[:], AX.X, ALU.add))
                ch(v.tensor_scalar(sb1[:], sb1[:], -1.0, float(CAP), ALU.add, ALU.mult))
                ch(v.tensor_tensor(blk[:], every(sb1[:], NB), every(starts, NB), ALU.is_equal))
                ch(v.tensor_tensor(blk[:], blk[:], every(g.c(K_ID1, 2 * NT).unsqueeze(2), NB), ALU.mult))
                ch(v.tensor_tensor(sl[:], sl[:], sb1[:].rearrange("p t o -> p (t o)"), ALU.subtract))
                v.tensor_tensor(pos[:], every(sl[:].unsqueeze(2), P), every(places, P), ALU.is_equal).then_inc(slots_ready, 1)
                ch(v.tensor_tensor(bk[:], c3[:].unsqueeze(1).to_broadcast([P, NOV, NE]),
                                   g.c(K_B, NOV).unsqueeze(2).to_broadcast([P, NOV, NE]), ALU.is_le))
                ch(v.tensor_reduce(bk2[:, 0:NOV].unsqueeze(2), bk[:], AX.X, ALU.add))
                ch(v.tensor_scalar(bk2[:, 0:NOV], bk2[:, 0:NOV], float(NE - 1), None, ALU.min))
                ch(v.tensor_copy(bk2[:, NOV:], c3[:, NE - 1:NE]))
                ch(v.tensor_copy(rt.more[:], bk2[:]))
                dve.wait_ge(who_done, 1)
                ch(v.tensor_scalar(gap[:], pw[:], 0.0, float(NOBODY), ALU.is_equal, ALU.mult))
                ch(v.scalar_tensor_tensor(who[:], pw[:], -1.0, gap[:], ALU.add, ALU.add))
                ch(v.tensor_copy(rt.put[:], who[:]))
                ch(v.tensor_scalar(gap[:], who[:], float(TOK), float(-TOK), ALU.is_ge, ALU.mult))
                ch(v.tensor_tensor(who[:], who[:], gap[:], ALU.add))
                ch(v.tensor_copy(rt.take[:], who[:]))
                g.done(ch, "dve")


@phase
def phase_experts(g, l, rt):
    nc, io = g.nc, g.io
    base = N_MOE[l]
    TURNS = NE // 2 - 1
    weights = (io["moe_w1"][l], io["moe_w3"][l], io["moe_w2"][l])
    with ExitStack() as ctx:
        sb = lambda n, sh, dt=F32: ctx.enter_context(nc.sbuf_tensor(f"ex{l}_{n}", sh, dt))
        ps = lambda n, sh: ctx.enter_context(nc.psum_tensor(f"ex{l}_{n}", sh, F32))
        sem = lambda n: g.semaphore(f"ex{l}_{n}")
        x, y = sb("x", [P, 2, D]), sb("y", [P, 2, D])
        xh, xl = sb("xh", [P, KT, P], F32R), sb("xl", [P, KT, P], F32R)
        wh, wl = sb("wh", [P, 3, CH], F32R), sb("wl", [P, 3, CH], F32R)
        s, gm = sb("s", [P, DE]), sb("gm", [P, DE])
        gh, gl = sb("gh", [P, DE // P, P], F32R), sb("gl", [P, DE // P, P], F32R)
        px, p1, p3, pg, py = ps("px", [P, KT, P]), ps("p1", [P, DE]), ps("p3", [P, 2, 512]), ps("pg", [P, 4, P]), ps("py", [P, 2, 512])
        x_here, y_out = ([sem(f"{n}{b}") for b in range(2)] for n in ("x_here", "y_out"))
        col = sb("col", [P, 3], I32)
        (x_zero, pool_turn, y_free, take_col, put_col, tx_done, xh_ready, xl_ready, h1_done, h3_done, tg_done, y_done, s_ready, gm_ready, gh_ready, gl_ready, y_ready,
         pe_turn) = map(sem, ("x_zero", "pool_turn", "y_free", "take_col", "put_col", "tx_done", "xh_ready", "xl_ready", "h1_done", "h3_done", "tg_done", "y_done", "s_ready",
                              "gm_ready", "gh_ready", "gl_ready", "y_ready", "pe_turn"))
        hi_ready, lo_ready = ([sem(f"{n}{k}") for k in range(3)] for n in ("hi_ready", "lo_ready"))
        g.free_when.update({base + 3 * e + k: None for e in range(NE) for k in range(3)})
        slot = lambda k: (base + k) % RING

        def half(ap, k, a):
            v = ap.rearrange("p (k n) -> p k n", k=KT if k < 2 else DE // P)
            return v[:, :, 256 * a:256 * a + 256] if k < 2 else v[:, 2 * a:2 * a + 2, :]

        w_of = lambda k, a: half(g.ring[:, slot(k), :], k, a)
        hi_of, lo_of = (lambda k, a: half(wh[:, k, :], k, a)), (lambda k, a: half(wl[:, k, :], k, a))

        def experts(eng, body):
            with eng.Fori(0, TURNS) as i:
                for j in range(2):
                    body(i, j, 2 * i + j, 2)
            for j in range(2):
                body(TURNS, j, 2 * TURNS + j, 1 - j)

        with nc.Block() as block:
            @block.sync
            def _(sp):
                with sp.Fori(1, NE) as e:
                    for k, w in enumerate(weights):
                        sp.wait_ge(lo_ready[k], 2 * e)
                        src = w[bass.ds(e, 1)].rearrange("o a n -> (o a) n")
                        src = src.rearrange("(p k) n -> p (k n)", k=KT) if k < 2 else src.rearrange("(k p) n -> p k n", p=P)
                        dst = g.ring[:, slot(k), :]
                        sp.dma_start(dst if k < 2 else dst.rearrange("p (k n) -> p k n", n=D), src).then_inc(g.arrived[slot(k)], 16)
                g.n_load = base + 3 * NE

            @block.gpsimd
            def _(pool):
                def take(b, e):
                    nc.gpsimd.tensor_copy(col[:, b:b + 1], rt.take[:, bass.ds(e, 1)]).then_inc(take_col, 1)
                    pool.wait_ge(take_col, e + 1)
                    pool.sem_inc(pool_turn, 1)
                    pool.indirect_dma_start(out=x[:, b, :], out_offset=None, in_=io["hrow"],
                                            in_offset=bass.IndirectOffsetOnAxis(ap=col[:, b:b + 1], axis=0),
                                            bounds_check=TOK - 1, oob_is_err=False).then_inc(x_here[b], 16)

                def body(i, j, e, left):
                    b = j
                    if left >= 2:
                        pool.wait_ge(tx_done, e + 1)
                        take(b, e + 2)
                    nc.gpsimd.tensor_copy(col[:, 2:3], rt.put[:, bass.ds(e, 1)]).then_inc(put_col, 1)
                    pool.wait_ge(put_col, e + 1)
                    pool.wait_ge(y_ready, e + 2)
                    pool.sem_inc(pool_turn, 1)
                    pool.indirect_dma_start(out=io["yrow"], out_offset=bass.IndirectOffsetOnAxis(ap=col[:, 2:3], axis=0),
                                            in_=y[:, b, :], in_offset=None,
                                            bounds_check=2 * TOK - 1, oob_is_err=False).then_inc(y_out[b], 16)
                    pool.wait_ge(y_out[b], 16 * i + 16)
                    pool.sem_inc(y_free, 1)

                pool.sem_inc(y_free, 2)
                nc.gpsimd.memset(x[:], 0.0).then_inc(x_zero, 1)
                pool.wait_ge(x_zero, 1)
                take(0, 0)
                take(1, 1)
                experts(pool, body)

            @block.tensor
            def _(pe):
                def take_rows(b, n):
                    pe.wait_ge(x_here[b], n)
                    pe.sem_inc(pe_turn, 1)
                    for k in range(KT):
                        last = nc.tensor.transpose(px[:, k, :], x[:, b, k:D:KT], g.c(K_ID, P))
                    last.then_inc(tx_done, 1)

                def up(out, k, a, first=0, end=KT):
                    h, l = hi_of(k, a), lo_of(k, a)
                    return product(nc, out, [(xh[:, q, :], xl[:, q, :], h[:, q, :], l[:, q, :]) for q in range(first, end)],
                                   first == 0, end == KT)

                def gate_transposes(a, e):
                    pe.wait_ge(gm_ready, 2 * e + a + 3)
                    pe.wait_ge(gl_ready, 2 * e + a + 2)
                    pe.sem_inc(pe_turn, 1)
                    for q in range(2 * a, 2 * a + 2):
                        last = nc.tensor.transpose(pg[:, q, :], gm[:, q * P:(q + 1) * P], g.c(K_ID, P))
                    last.then_inc(tg_done, 1)

                def down(a):
                    h, l = hi_of(2, a), lo_of(2, a)
                    for c in range(2):
                        cols = slice(512 * c, 512 * c + 512)
                        last = product(nc, py[:, c, :], [(gh[:, 2 * a + q, :], gl[:, 2 * a + q, :], h[:, q, cols], l[:, q, cols])
                                                     for q in range(2)], a == 0, a == 1)
                    return last

                def body(i, j, e, left):
                    pe.wait_ge(xl_ready, e + 1)
                    pe.wait_ge(s_ready, e + 1)
                    for a in range(2):
                        pe.wait_ge(lo_ready[0], 2 * e + a + 1)
                        ins = up(p1[:, 256 * a:256 * a + 256], 0, a)
                    ins.then_inc(h1_done, 1)
                    pe.wait_ge(lo_ready[1], 2 * e + 1)
                    pe.wait_ge(gm_ready, 2 * e + 2)
                    up(p3[:, 0, 0:256], 1, 0).then_inc(h3_done, 1)
                    pe.wait_ge(lo_ready[1], 2 * e + 2)
                    up(p3[:, 1, 0:256], 1, 1, 0, KT // 2)
                    gate_transposes(0, e)
                    up(p3[:, 1, 0:256], 1, 1, KT // 2, KT).then_inc(h3_done, 1)
                    pe.wait_ge(lo_ready[2], 2 * e + 1)
                    pe.wait_ge(gl_ready, 2 * e + 3)
                    pe.wait_ge(y_ready, e + 1)
                    down(0)
                    gate_transposes(1, e)
                    if left:
                        take_rows(1 - j, 16 * i + 16 * j + 16)
                    pe.wait_ge(lo_ready[2], 2 * e + 2)
                    pe.wait_ge(gl_ready, 2 * e + 4)
                    down(1).then_inc(y_done, 1)

                take_rows(0, 16)
                experts(pe, body)

            @block.scalar
            def _(act):
                def hi(k, a, e):
                    if a == 0:
                        act.wait_ge(g.arrived[slot(k)], 16 * e + 16 * ((base + k) // RING + 1))
                    nc.scalar.copy(hi_of(k, a), w_of(k, a)).then_inc(hi_ready[k], 1)

                def x_hi(e):
                    act.wait_ge(tx_done, e + 1)
                    nc.scalar.copy(xh[:], px[:]).then_inc(xh_ready, 1)

                def g_hi(a, e):
                    act.wait_ge(tg_done, 2 * e + a + 1)
                    nc.scalar.copy(gh[:, 2 * a:2 * a + 2, :], pg[:, 2 * a:2 * a + 2, :]).then_inc(gh_ready, 1)

                def body(i, j, e, left):
                    act.wait_ge(h1_done, e + 1)
                    act.wait_ge(gm_ready, 2 * e + 2)
                    nc.scalar.activation(s[:], p1[:], ACT.Silu).then_inc(s_ready, 1)
                    hi(2, 0, e)
                    g_hi(0, e)
                    hi(2, 1, e)
                    if left:
                        hi(0, 0, e + 1)
                    g_hi(1, e)
                    if left:
                        x_hi(e + 1)
                        hi(0, 1, e + 1)
                    act.wait_ge(y_done, e + 1)
                    act.wait_ge(y_free, e + 1)
                    nc.scalar.copy(y[:, j, :].rearrange("p (a n) -> p a n", a=2), py[:]).then_inc(y_ready, 1)
                    if left:
                        hi(1, 0, e + 1)
                        hi(1, 1, e + 1)

                nc.scalar.preload_act_table(ACT.Silu)
                act.sem_inc(s_ready, 1)
                act.sem_inc(y_ready, 1)
                for k in range(2):
                    for a in range(2):
                        hi(k, a, 0)
                x_hi(0)
                experts(act, body)

            @block.vector
            def _(dve):
                def lo(k, a, e):
                    dve.wait_ge(hi_ready[k], 2 * e + a + 1)
                    nc.vector.tensor_tensor(lo_of(k, a), w_of(k, a), hi_of(k, a).bitcast(F32), ALU.subtract).then_inc(lo_ready[k], 1)

                def x_lo(e):
                    dve.wait_ge(xh_ready, e + 1)
                    nc.vector.tensor_tensor(xl[:], px[:], xh[:].bitcast(F32), ALU.subtract).then_inc(xl_ready, 1)

                def g_lo(a, e):
                    qs = slice(2 * a, 2 * a + 2)
                    dve.wait_ge(gh_ready, 2 * e + a + 1)
                    nc.vector.tensor_tensor(gl[:, qs, :], pg[:, qs, :], gh[:, qs, :].bitcast(F32), ALU.subtract).then_inc(gl_ready, 1)

                def gate(a, e):
                    cols = slice(256 * a, 256 * a + 256)
                    dve.wait_ge(s_ready, e + 2)
                    dve.wait_ge(h3_done, 2 * e + a + 1)
                    nc.vector.tensor_tensor(gm[:, cols], s[:, cols], p3[:, a, 0:256], ALU.mult).then_inc(gm_ready, 1)

                def body(i, j, e, left):
                    lo(2, 0, e)
                    gate(0, e)
                    g_lo(0, e)
                    gate(1, e)
                    lo(2, 1, e)
                    if left:
                        lo(0, 0, e + 1)
                    g_lo(1, e)
                    if left:
                        x_lo(e + 1)
                        lo(0, 1, e + 1)
                        lo(1, 0, e + 1)
                        lo(1, 1, e + 1)

                dve.sem_inc(gm_ready, 2)
                dve.sem_inc(gl_ready, 2)
                for k in range(2):
                    for a in range(2):
                        lo(k, a, 0)
                x_lo(0)
                experts(dve, body)


@phase
def phase_more(g, l, rt):
    nc, io = g.nc, g.io
    weights = (io["moe_w1"][l], io["moe_w3"][l], io["moe_w2"][l])
    with ExitStack() as ctx:
        sb = lambda n, sh, dt=F32: ctx.enter_context(nc.sbuf_tensor(f"mo{l}_{n}", sh, dt))
        ps = lambda n, sh: ctx.enter_context(nc.psum_tensor(f"mo{l}_{n}", sh, F32))
        sem = lambda n: g.semaphore(f"mo{l}_{n}")
        x, y = sb("x", [P, D]), sb("y", [P, D])
        xT, s, gT = sb("xT", [P, KT, CAP]), sb("s", [P, DE // P, CAP]), sb("gT", [P, DE // P, CAP])
        px, p1, p3, py = ps("px", [P, KT, CAP]), ps("p1", [P, DE // P, CAP]), ps("p3", [P, DE // P, CAP]), ps("py", [P, 2, 512])
        col = sb("col", [P, 2], I32)
        (x_zero, pool_turn, cols_ready, x_here, t_done, xT_ready, h1_done, h3_done, s_ready, g_ready, y_done, y_ready, y_out, y_free, pe_turn) = map(sem, (
            "x_zero", "pool_turn", "cols_ready", "x_here", "t_done", "xT_ready", "h1_done", "h3_done", "s_ready", "g_ready", "y_done", "y_ready", "y_out",
            "y_free", "pe_turn"))
        w_here = [sem(f"w_here{k}") for k in range(3)]
        w1, w3 = (g.ring[:, k, :].rearrange("p (k n) -> p k n", k=KT) for k in range(2))
        w2 = g.ring[:, 2, :].rearrange("p (k n) -> p k n", k=DE // P)

        def blocks(eng, body):
            n = eng.value_load(rt.more[0:1, NOV:NOV + 1], min_val=0, max_val=NOV)
            with eng.Fori(0, NOV) as b:
                with eng.If(n > b):
                    body(b)

        with nc.Block() as block:
            @block.sync
            def _(sp):
                def body(b):
                    e = sp.value_load(rt.more[0:1, bass.ds(b, 1)], min_val=0, max_val=NE - 1)
                    for k, (w, done) in enumerate(zip(weights, (h1_done, h3_done, y_done))):
                        sp.wait_ge(done, b + 1)
                        src = w[bass.ds(e, 1)].rearrange("o a n -> (o a) n")
                        src = src.rearrange("(p k) n -> p (k n)", k=KT) if k < 2 else src.rearrange("(k p) n -> p k n", p=P)
                        sp.dma_start(g.ring[:, k, :] if k < 2 else w2, src).then_inc(w_here[k], 16)
                blocks(sp, body)

            @block.gpsimd
            def _(pool):
                def body(b):
                    nc.gpsimd.tensor_copy(col[:, 0:1], rt.take[:, bass.ds(b + NE, 1)])
                    nc.gpsimd.tensor_copy(col[:, 1:2], rt.put[:, bass.ds(b + NE, 1)]).then_inc(cols_ready, 1)
                    pool.wait_ge(cols_ready, b + 1)
                    pool.wait_ge(t_done, b + 1)
                    pool.sem_inc(pool_turn, 1)
                    pool.indirect_dma_start(out=x[:], out_offset=None, in_=io["hrow"],
                                            in_offset=bass.IndirectOffsetOnAxis(ap=col[:, 0:1], axis=0),
                                            bounds_check=TOK - 1, oob_is_err=False).then_inc(x_here, 16)
                    pool.wait_ge(y_ready, b + 2)
                    pool.sem_inc(pool_turn, 1)
                    pool.indirect_dma_start(out=io["yrow"], out_offset=bass.IndirectOffsetOnAxis(ap=col[:, 1:2], axis=0),
                                            in_=y[:], in_offset=None,
                                            bounds_check=2 * TOK - 1, oob_is_err=False).then_inc(y_out, 16)
                    pool.wait_ge(y_out, 16 * b + 16)
                    pool.sem_inc(y_free, 1)

                pool.sem_inc(y_free, 1)
                nc.gpsimd.memset(x[:], 0.0).then_inc(x_zero, 1)
                pool.wait_ge(x_zero, 1)
                blocks(pool, body)

            @block.tensor
            def _(pe):
                def up(w, out, done):
                    for j in range(DE // P):
                        for k in range(KT):
                            last = nc.tensor.matmul(out[:, j, :], w[:, k, j * P:(j + 1) * P], xT[:, k, :], start=k == 0, stop=k == KT - 1)
                    last.then_inc(done, 1)

                def body(b):
                    pe.wait_ge(x_here, 16 * b + 16)
                    pe.sem_inc(pe_turn, 1)
                    for k in range(KT):
                        last = nc.tensor.transpose(px[:, k, :], x[:, k:D:KT], g.c(K_ID, P))
                    last.then_inc(t_done, 1)
                    pe.wait_ge(xT_ready, b + 2)
                    pe.wait_ge(w_here[0], 16 * b + 16)
                    pe.wait_ge(s_ready, b + 1)
                    up(w1, p1, h1_done)
                    pe.wait_ge(w_here[1], 16 * b + 16)
                    pe.wait_ge(g_ready, b + 1)
                    up(w3, p3, h3_done)
                    pe.wait_ge(w_here[2], 16 * b + 16)
                    pe.wait_ge(g_ready, b + 2)
                    pe.wait_ge(y_ready, b + 1)
                    for i in range(2):
                        for j in range(DE // P):
                            last = nc.tensor.matmul(py[:, i, :], gT[:, j, :], w2[:, j, 512 * i:512 * i + 512], start=j == 0, stop=j == DE // P - 1)
                    last.then_inc(y_done, 1)

                for free in (t_done, h1_done, h3_done, y_done):
                    pe.sem_inc(free, 1)
                blocks(pe, body)

            @block.scalar
            def _(act):
                def body(b):
                    act.wait_ge(h1_done, b + 2)
                    act.wait_ge(g_ready, b + 1)
                    nc.scalar.activation(s[:], p1[:], ACT.Silu).then_inc(s_ready, 1)
                    act.wait_ge(y_done, b + 2)
                    act.wait_ge(y_free, b + 1)
                    nc.scalar.copy(y[:].rearrange("p (a n) -> p a n", a=2), py[:]).then_inc(y_ready, 1)

                nc.scalar.preload_act_table(ACT.Silu)
                act.sem_inc(s_ready, 1)
                act.sem_inc(y_ready, 1)
                blocks(act, body)

            @block.vector
            def _(dve):
                def body(b):
                    dve.wait_ge(t_done, b + 2)
                    nc.vector.tensor_copy(xT[:], px[:]).then_inc(xT_ready, 1)
                    dve.wait_ge(s_ready, b + 2)
                    dve.wait_ge(h3_done, b + 2)
                    nc.vector.tensor_tensor(gT[:], s[:], p3[:], ALU.mult).then_inc(g_ready, 1)

                dve.sem_inc(xT_ready, 1)
                dve.sem_inc(g_ready, 1)
                blocks(dve, body)


@phase
def phase_combine(g, s, rt, xt, last):
    nc, io = g.nc, g.io
    with ExitStack() as ctx:
        sb = lambda n, sh: ctx.enter_context(nc.sbuf_tensor(f"cb{s}_{n}", sh, F32))
        sem = lambda n: g.semaphore(f"cb{s}_{n}")
        y = sb("y", [P, NT, 2, D])
        gate = sb("gate", [P, 3, D])
        ss = sb("ss", [P, NT])
        junk = sb("junk", [P, D]) if last else None
        y_here = [[sem(f"y_here{t}{i}") for i in range(2)] for t in range(NT)]
        batches = ((0, 1), (2, 3, 4))
        x_here = [sem(f"x_here{t}") for t in range(NT)]
        nw_here = sem("nw_here") if last else None
        gate_here, y1_ready, y_used, x_ready, x_out, rs_ready, ss_set = map(sem, (
            "gate_here", "y1_ready", "y_used", "x_ready", "x_out", "rs_ready", "ss_set"))
        with nc.Block() as block:
            @block.sync
            def _(sp):
                for c in range(2):
                    sp.dma_start(gate[:, c, :], bcast_rows(io["mod"][s, c, 2 * D:3 * D])).then_inc(gate_here, 16)
                for t in range(NT):
                    for i in range(2):
                        row = i * TOK + t * P
                        sp.dma_start(y[0:width(t), t, i, :], io["yrow"][row:row + width(t), :]).then_inc(y_here[t][i], 16)
                    sp.dma_start(xt[0:width(t), t, :], x_source(g, s, t)).then_inc(x_here[t], 16)
                if last:
                    sp.dma_start(gate[:, 2, :], bcast_rows(io["final_norm_w"])).then_inc(nw_here, 16)
                for t in range(NT):
                    w = width(t)
                    sp.wait_ge(x_ready, t + 1)
                    if not last:
                        dst = io["xres"][s][t * P:t * P + w, :]
                    elif t < NT - 1:
                        dst = io["y_prompt"][0, t * P:t * P + P, :]
                    else:
                        dst = io["y_sample"][0]
                    sp.dma_start(dst, xt[0:w, t, :]).then_inc(x_out, 16)
                sp.wait_ge(x_out, 16 * NT)

            @block.scalar
            def _(act):
                ch = g.chain(act, "act")
                for t in range(NT):
                    w = width(t)
                    act.wait_ge(y_here[t][0], 16)
                    nc.scalar.activation(y[0:w, t, 0, :], y[0:w, t, 0, :], ACT.Identity, scale=rt.w[0:w, 0, t:t + 1]).then_inc(y1_ready, 1)
                if last:
                    act.wait_ge(ss_set, 1)
                    for tiles in batches:
                        cols = slice(tiles[0], tiles[-1] + 1)
                        for t in tiles:
                            w = width(t)
                            act.wait_ge(y_used, t + 1)
                            ch(nc.scalar.activation(junk[0:w, :], xt[0:w, t, :], ACT.Square, accum_out=ss[0:w, t:t + 1]))
                        ch(nc.scalar.activation(ss[:, cols], ss[:, cols], ACT.Ln, scale=1.0 / D, bias=g.eps[:]))
                        nc.scalar.activation(ss[:, cols], ss[:, cols], ACT.Exp, scale=-0.5).then_inc(rs_ready, 1)
                g.done(ch, "act")

            @block.vector
            def _(dve):
                ch = g.chain(dve, "dve")
                if last:
                    nc.vector.memset(ss[:], 1.0).then_inc(ss_set, 1)
                dve.wait_ge(gate_here, 32)
                for t in range(NT):
                    w, c = width(t), int(t == NT - 1)
                    y1, y2 = y[0:w, t, 0, :], y[0:w, t, 1, :]
                    dve.wait_ge(y1_ready, t + 1)
                    dve.wait_ge(y_here[t][1], 16)
                    ch(nc.vector.scalar_tensor_tensor(y1, y2, rt.w[0:w, 1, t:t + 1], y1, ALU.mult, ALU.add))
                    ch(nc.vector.tensor_tensor(y1, y1, gate[0:w, c, :], ALU.mult))
                    dve.wait_ge(x_here[t], 16)
                    nc.vector.tensor_tensor(xt[0:w, t, :], xt[0:w, t, :], y1, ALU.add).then_inc(y_used if last else x_ready, 1)
                if last:
                    dve.wait_ge(nw_here, 16)
                    for t in range(NT):
                        w = width(t)
                        dve.wait_ge(rs_ready, 1 if t in batches[0] else 2)
                        nc.vector.scalar_tensor_tensor(xt[0:w, t, :], xt[0:w, t, :], ss[0:w, t:t + 1], gate[0:w, 2, :],
                                                       ALU.mult, ALU.mult).then_inc(x_ready, 1)
                g.done(ch, "dve")


KEYS = SEQ + PAST + DSEQ
NK = NT + 1
HALF = MH // 2
QW = NOPE + ROPE


def key_cols(j):
    return slice(j * P, j * P + (P if j < NK - 1 else DSEQ))


@phase
def phase_mla_project(g, m, hT):
    nc, io = g.nc, g.io
    base = N_MLA
    with ExitStack() as ctx:
        sb = lambda n, sh: ctx.enter_context(nc.sbuf_tensor("mp_" + n, sh, F32))
        sem = lambda n: g.semaphore("mp_" + n)
        qnw, kvnw = sb("qnw", [P, QR]), sb("kvnw", [P, KVR])
        cq = sb("cq", [P, 2, QR])
        kv = sb("kv", [P, NK, KVR + ROPE])
        junk = sb("junk", [P, QR])
        ss = sb("ss", [P, NT, 2])
        rt = sb("rt", [P, 4, ROPE // 2])
        pq, pk, pv = (ctx.enter_context(nc.psum_tensor(f"mp_p{i}", [P, 2, 512], F32)) for i in range(3))
        tp = ctx.enter_context(nc.psum_tensor("mp_tp", [P, 8, P], F32))
        par_here, cache_here, in_done, rs_ready, lat_ready, tp_done, lat_T, out_done = map(sem, (
            "par_here", "cache_here", "in_done", "rs_ready", "lat_ready", "tp_done", "lat_T", "out_done"))
        v_done, v_used = [sem(f"v_done{i}") for i in range(2)], [sem(f"v_used{i}") for i in range(2)]
        kj = lambda t: t if t < NT - 1 else NK - 1
        g.free_when.update({base: (in_done, NT), base + 1: (in_done, NT)})
        with nc.Block() as block:
            @block.sync
            def _(sp):
                sp.dma_start(qnw[:], bcast_rows(io["mla_q_norm_w"][0])).then_inc(par_here, 16)
                sp.dma_start(kvnw[:], bcast_rows(io["mla_kv_norm_w"][0])).then_inc(par_here, 16)
                sp.dma_start(kv[:, NT - 1, 0:KVR], io["cache_mla_ckv"][0, 0]).then_inc(cache_here, 16)
                sp.dma_start(kv[:, NT - 1, KVR:], io["cache_mla_krope"][0, 0]).then_inc(cache_here, 16)
                g.stream(sp, base + 2)
                for t in range(NT):
                    w = width(t)
                    sp.wait_ge(lat_ready, t + 1)
                    for name, cols in (("ckv", slice(0, KVR)), ("krope", slice(KVR, KVR + ROPE))):
                        dst = io[name + "_prompt"][0, 0, t * P:t * P + P, :] if t < NT - 1 else io[name + "_sample"][0, 0]
                        sp.dma_start(dst, kv[0:w, kj(t), cols]).then_inc(out_done, 16)
                sp.wait_ge(out_done, 32 * NT)

            @block.tensor
            def _(pe):
                wq, wk = g.chunk(pe, base), g.chunk(pe, base + 1)

                def project(t):
                    w = width(t)
                    if t >= 2:
                        pe.wait_ge(lat_ready, t - 1)
                    for out, wx, n in ((pq, wq, QR), (pk, wk, KVR + ROPE)):
                        for k in range(KT):
                            last = nc.tensor.matmul(out[0:w, t % 2, 0:n], hT[:, k, t * P:t * P + w], wx[:, k, :], start=k == 0, stop=k == KT - 1)
                    last.then_inc(in_done, 1)

                def transposes(w, j, b, turn):
                    if turn:
                        pe.wait_ge(lat_T, turn)
                    if b is not None:
                        for k in range(QR // P):
                            nc.tensor.transpose(tp[:, k, 0:w], cq[0:w, b, k * P:(k + 1) * P], g.c(K_ID, w, w))
                    for k in range(KVR // P):
                        nc.tensor.transpose(tp[:, 3 + k, 0:w], kv[0:w, j, k * P:(k + 1) * P], g.c(K_ID, w, w))
                    nc.tensor.transpose(tp[0:QW, 5, 0:w], kv[0:w, j, KVR + ROPE - QW:], g.c(K_ID, w, w)).then_inc(tp_done, 1)

                project(0)
                for t in range(NT):
                    if t + 1 < NT:
                        project(t + 1)
                    pe.wait_ge(lat_ready, t + 1)
                    transposes(width(t), kj(t), t % 2, t)
                pe.wait_ge(cache_here, 32)
                transposes(P, NT - 1, None, NT)
                pe.wait_ge(lat_T, NT + 1)
                wv = g.chunk(pe, base + 4).rearrange("p k (h c) -> p k h c", h=MH)
                for j in range(NK):
                    w = key_cols(j).stop - key_cols(j).start
                    for i in range(2):
                        if j:
                            pe.wait_ge(v_used[i], j)
                        for k in range(KVR // P):
                            last = nc.tensor.matmul(pv[0:w, i, :], m.ckvT[:, k, key_cols(j)], wv[:, k, i * HALF:(i + 1) * HALF, NOPE:],
                                                    start=k == 0, stop=k == KVR // P - 1)
                        last.then_inc(v_done[i], 1)

            @block.scalar
            def _(act):
                ch = g.chain(act, "act")
                def factors(t):
                    w = width(t)
                    act.wait_ge(in_done, t + 1)
                    for i, (src, n) in enumerate(((pq[0:w, t % 2, 0:QR], QR), (pk[0:w, t % 2, 0:KVR], KVR))):
                        ch(nc.scalar.activation(junk[0:w, 0:n], src, ACT.Square, accum_out=ss[0:w, t, i:i + 1]))
                        ch(nc.scalar.activation(ss[0:w, t, i:i + 1], ss[0:w, t, i:i + 1], ACT.Ln, scale=1.0 / n, bias=g.eps[0:w, :]))
                    nc.scalar.activation(ss[0:w, t, :], ss[0:w, t, :], ACT.Exp, scale=-0.5).then_inc(rs_ready, 1)

                def keep(w, t, j, turn):
                    act.wait_ge(tp_done, turn + 1)
                    if t is not None:
                        nc.scalar.copy(m.cqT[:, :, t * P:t * P + w], tp[:, 0:3, 0:w])
                    nc.scalar.copy(m.ckvT[:, :, key_cols(j)], tp[:, 3:5, 0:w])
                    nc.scalar.copy(m.kT[NOPE:QW, 0, key_cols(j)], tp[NOPE:QW, 5, 0:w])
                    nc.scalar.copy(m.kT[NOPE:QW, 1, key_cols(j)], tp[NOPE:QW, 5, 0:w]).then_inc(lat_T, 1)

                factors(0)
                for t in range(NT):
                    if t + 1 < NT:
                        factors(t + 1)
                    keep(width(t), t, kj(t), t)
                keep(P, None, NT - 1, NT)
                for j in range(NK):
                    w = key_cols(j).stop - key_cols(j).start
                    act.wait_ge(v_done[0], j + 1)
                    nc.scalar.copy(m.v[0:w, j, 0:512], pv[0:w, 0, :]).then_inc(v_used[0], 1)
                g.done(ch, "act")

            @block.vector
            def _(dve):
                ch = g.chain(dve, "dve")
                v = nc.vector
                dve.wait_ge(par_here, 32)
                for t in range(NT):
                    w, b, j = width(t), t % 2, kj(t)
                    dve.wait_ge(rs_ready, t + 1)
                    if t >= 2:
                        dve.wait_ge(tp_done, t - 1)
                    v.scalar_tensor_tensor(cq[0:w, b, :], pq[0:w, b, 0:QR], ss[0:w, t, 0:1], qnw[0:w, :], ALU.mult, ALU.mult)
                    v.scalar_tensor_tensor(kv[0:w, j, 0:KVR], pk[0:w, b, 0:KVR], ss[0:w, t, 1:2], kvnw[0:w, :], ALU.mult, ALU.mult)
                    x1, x2 = pk[0:w, b, KVR:KVR + 16], pk[0:w, b, KVR + 16:KVR + 32]
                    cos, sin = g.c(K_CS + t * ROPE, 16, w), g.c(K_CS + t * ROPE + 16, 16, w)
                    for i, (x, y) in enumerate(((x1, cos), (x2, sin), (x1, sin), (x2, cos))):
                        last = v.tensor_tensor(rt[0:w, i, :], x, y, ALU.mult)
                    ch(last)
                    v.tensor_tensor(kv[0:w, j, KVR:KVR + 16], rt[0:w, 0, :], rt[0:w, 1, :], ALU.subtract)
                    ch(v.tensor_tensor(kv[0:w, j, KVR + 16:], rt[0:w, 2, :], rt[0:w, 3, :], ALU.add))
                    dve.sem_inc(lat_ready, 1)
                for j in range(NK):
                    w = key_cols(j).stop - key_cols(j).start
                    dve.wait_ge(v_done[1], j + 1)
                    v.tensor_copy(m.v[0:w, j, 512:1024], pv[0:w, 1, :]).then_inc(v_used[1], 1)
                g.done(ch, "dve")


@phase
def phase_mla_queries(g, m, hf):
    nc = g.nc
    n = N_MLA + 2 + hf
    with ExitStack() as ctx:
        sem = lambda n: g.semaphore(f"mq{hf}_" + n)
        rt = ctx.enter_context(nc.sbuf_tensor(f"mq{hf}_rt", [P, 4, HALF, ROPE // 2], F32))
        ps = ctx.enter_context(nc.psum_tensor(f"mq{hf}_ps", [P, 2, 2, 512], F32))
        q_done, q_here = map(sem, ("q_done", "q_here"))
        hw = HALF // 2 * QW
        g.free_when[n] = (q_done, NT)
        with nc.Block() as block:
            @block.sync
            def _(sp):
                g.stream(sp, n + 1)

            @block.tensor
            def _(pe):
                wq = g.chunk(pe, n)
                for t in range(NT):
                    w = width(t)
                    if t >= 2:
                        pe.wait_ge(q_here, t - 1)
                    for i in range(2):
                        for k in range(QR // P):
                            last = nc.tensor.matmul(ps[0:w, t % 2, i, 0:hw], m.cqT[:, k, t * P:t * P + w], wq[:, k, i * hw:(i + 1) * hw],
                                                    start=k == 0, stop=k == QR // P - 1)
                    last.then_inc(q_done, 1)

            @block.scalar
            def _(act):
                for t in range(NT):
                    w = width(t)
                    act.wait_ge(q_done, t + 1)
                    nc.scalar.copy(m.q[0:w, t, :].rearrange("p (i n) -> p i n", i=2), ps[0:w, t % 2, :, 0:hw]).then_inc(q_here, 1)

            @block.vector
            def _(dve):
                ch = g.chain(dve, "dve")
                for t in range(NT):
                    w = width(t)
                    dve.wait_ge(q_here, t + 1)
                    qh = m.q[0:w, t, :].rearrange("p (h c) -> p h c", h=HALF)
                    x1, x2 = qh[:, :, NOPE:NOPE + 16], qh[:, :, NOPE + 16:]
                    cos, sin = (g.c(K_CS + t * ROPE + i, 16, w).unsqueeze(1).to_broadcast([w, HALF, 16]) for i in (0, 16))
                    for i, (x, y) in enumerate(((x1, cos), (x2, sin), (x1, sin), (x2, cos))):
                        last = nc.vector.tensor_tensor(rt[0:w, i], x, y, ALU.mult)
                    ch(last)
                    nc.vector.tensor_tensor(x1, rt[0:w, 0], rt[0:w, 1], ALU.subtract)
                    ch(nc.vector.tensor_tensor(x2, rt[0:w, 2], rt[0:w, 3], ALU.add))
                g.done(ch, "dve")


@phase
def phase_mla_attend(g, m, hf, o):
    nc = g.nc
    scale = QW ** -0.5
    steps = HALF * NT
    with ExitStack() as ctx:
        sb = lambda n, sh: ctx.enter_context(nc.sbuf_tensor(f"ma{hf}_{n}", sh, F32))
        sem = lambda n: g.semaphore(f"ma{hf}_{n}")
        qT = sb("qT", [QW, 2, TOK])
        p = sb("p", [P, 2, SEQ])
        pT = sb("pT", [P, 2, NT - 1, P])
        mx, nm, sm = sb("mx", [P, steps]), sb("nm", [P, steps]), sb("sm", [P, steps])
        pre = ctx.enter_context(nc.psum_tensor(f"ma{hf}_pre", [P, 2, 512], F32))
        ps = ctx.enter_context(nc.psum_tensor(f"ma{hf}_ps", [P, 2, 512], F32))
        pt = ctx.enter_context(nc.psum_tensor(f"ma{hf}_pt", [P, 2, NT - 1, P], F32))
        po = ctx.enter_context(nc.psum_tensor(f"ma{hf}_po", [P, 2, 512], F32))
        (k_done, k_ready, qT_done, qT_ready, s_done, m_ready, p_ready, t_done, pT_ready, o_done, o_ready) = map(sem, (
            "k_done", "k_ready", "qT_done", "qT_ready", "s_done", "m_ready", "p_ready", "t_done", "pT_ready", "o_done", "o_ready"))
        if hf:
            g.free_when[N_MLA + 4] = (k_done, HALF)
        keys = lambda t: slice(0, (t + 1) * P) if t < NT - 1 else slice(SEQ, KEYS)
        tiles = lambda t: list(range(t + 1)) if t < NT - 1 else [NT - 1, NT]
        cut = lambda j: key_cols(j).stop - key_cols(j).start
        with nc.Block() as block:
            @block.sync
            def _(sp):
                g.stream(sp, N_MLA + 3 + 2 * hf)

            @block.tensor
            def _(pe):
                wk = g.chunk(pe, N_MLA + 4)

                def keys_of(h):
                    if h:
                        pe.wait_ge(qT_ready, h)
                    for k in range(KVR // P):
                        lhsT = wk[:, k, (hf * HALF + h) * P:(hf * HALF + h) * P + NOPE]
                        nc.tensor.matmul(pre[0:NOPE, 0, :], lhsT, m.ckvT[:, k, 0:SEQ], start=k == 0, stop=k == KVR // P - 1)
                        last = nc.tensor.matmul(pre[0:NOPE, 1, 0:KEYS - SEQ], lhsT, m.ckvT[:, k, SEQ:KEYS], start=k == 0, stop=k == KVR // P - 1)
                    last.then_inc(k_done, 1)

                def queries_of(h):
                    pe.wait_ge(k_ready, h + 1)
                    for t in range(NT):
                        w = width(t)
                        out = pre[0:QW, 0, t * P:t * P + P] if t < NT - 1 else pre[0:QW, 1, 0:w]
                        last = nc.tensor.transpose(out, m.q[0:w, t, h * QW:(h + 1) * QW], g.c(K_ID, w, w))
                    last.then_inc(qT_done, 1)

                def scores(i):
                    h, t = divmod(i, NT)
                    w, n = width(t), keys(t).stop - keys(t).start
                    if t == 0:
                        pe.wait_ge(k_ready, h + 1)
                        pe.wait_ge(qT_ready, h + 1)
                    if i >= 2:
                        pe.wait_ge(p_ready, i - 1)
                    last = nc.tensor.matmul(ps[0:w, i % 2, 0:n], qT[:, h % 2, t * P:t * P + w], m.kT[:, h % 2, keys(t)],
                                            start=True, stop=t == NT - 1)
                    if t < NT - 1:
                        last = nc.tensor.matmul(ps[:, i % 2, n - 64:n], g.c(K_AM, P, 1), g.c(K_AM + P, 64, 1), start=False, stop=True)
                    last.then_inc(s_done, 1)

                def transposes(i):
                    t = i % NT
                    w = width(t)
                    pe.wait_ge(p_ready, i + 1)
                    if i >= 2:
                        pe.wait_ge(pT_ready, i - 1)
                    for a, j in enumerate(tiles(t)):
                        last = nc.tensor.transpose(pt[0:cut(j), i % 2, a, 0:w], p[0:w, i % 2, a * P:a * P + cut(j)], g.c(K_ID, w, w))
                    last.then_inc(t_done, 1)

                def values(i):
                    h, t = divmod(i, NT)
                    w, js = width(t), tiles(t)
                    c = (hf * HALF + h) * MV
                    pe.wait_ge(pT_ready, i + 1)
                    if i >= 2:
                        pe.wait_ge(o_ready, i - 1)
                    for a, j in enumerate(js):
                        last = nc.tensor.matmul(po[0:w, i % 2, 0:MV], pT[0:cut(j), i % 2, a, 0:w], m.v[0:cut(j), j, c:c + MV],
                                                start=a == 0, stop=a == len(js) - 1)
                    last.then_inc(o_done, 1)

                keys_of(0)
                queries_of(0)
                scores(0)
                for i in range(steps):
                    h, t = divmod(i, NT)
                    if i + 1 < steps:
                        scores(i + 1)
                    if t == 1 and h + 1 < HALF:
                        keys_of(h + 1)
                    if t == 2 and h + 1 < HALF:
                        queries_of(h + 1)
                    transposes(i)
                    if i:
                        values(i - 1)
                values(steps - 1)

            @block.scalar
            def _(act):
                def exps(i):
                    t = i % NT
                    w, n = width(t), keys(t).stop - keys(t).start
                    act.wait_ge(m_ready, i + 1)
                    if i >= 2:
                        act.wait_ge(t_done, i - 1)
                    nc.scalar.activation(p[0:w, i % 2, 0:n], ps[0:w, i % 2, 0:n], ACT.Exp, scale=scale,
                                         bias=nm[0:w, i:i + 1], accum_out=sm[0:w, i:i + 1]).then_inc(p_ready, 1)

                def keep_queries(h):
                    act.wait_ge(qT_done, h + 1)
                    nc.scalar.copy(qT[:, h % 2, 0:SEQ], pre[0:QW, 0, :])
                    nc.scalar.copy(qT[:, h % 2, SEQ:TOK], pre[0:QW, 1, 0:DSEQ]).then_inc(qT_ready, 1)

                keep_queries(0)
                exps(0)
                for i in range(steps):
                    h, t = divmod(i, NT)
                    if i + 1 < steps:
                        exps(i + 1)
                    if t == 2 and h + 1 < HALF:
                        keep_queries(h + 1)
                    act.wait_ge(t_done, i + 1)
                    if i >= 2:
                        act.wait_ge(o_done, i - 1)
                    if t < NT - 1:
                        nc.scalar.copy(pT[:, i % 2, 0:t + 1, :], pt[:, i % 2, 0:t + 1, :]).then_inc(pT_ready, 1)
                    else:
                        nc.scalar.copy(pT[:, i % 2, 0, 0:DSEQ], pt[:, i % 2, 0, 0:DSEQ])
                        nc.scalar.copy(pT[0:DSEQ, i % 2, 1, 0:DSEQ], pt[0:DSEQ, i % 2, 1, 0:DSEQ]).then_inc(pT_ready, 1)

            @block.vector
            def _(dve):
                ch = g.chain(dve, "dve")

                def maxima(i):
                    t = i % NT
                    w, n = width(t), keys(t).stop - keys(t).start
                    dve.wait_ge(s_done, i + 1)
                    ch(nc.vector.tensor_reduce(mx[0:w, i:i + 1], ps[0:w, i % 2, 0:n], AX.X, ALU.max))
                    nc.vector.tensor_scalar(nm[0:w, i:i + 1], mx[0:w, i:i + 1], -scale, None, ALU.mult).then_inc(m_ready, 1)

                def keep_keys(h):
                    dve.wait_ge(k_done, h + 1)
                    if h >= 2:
                        dve.wait_ge(s_done, NT * (h - 1))
                    nc.vector.tensor_copy(m.kT[0:NOPE, h % 2, 0:SEQ], pre[0:NOPE, 0, :])
                    nc.vector.tensor_copy(m.kT[0:NOPE, h % 2, SEQ:KEYS], pre[0:NOPE, 1, 0:KEYS - SEQ]).then_inc(k_ready, 1)

                def outputs(i):
                    h, t = divmod(i, NT)
                    w, c = width(t), (hf * HALF + h) * MV
                    ch(nc.vector.reciprocal(mx[0:w, i:i + 1], sm[0:w, i:i + 1]))
                    dve.wait_ge(o_done, i + 1)
                    nc.vector.tensor_scalar(o[0:w, t, c:c + MV], po[0:w, i % 2, 0:MV], mx[0:w, i:i + 1], None, ALU.mult).then_inc(o_ready, 1)

                keep_keys(0)
                maxima(0)
                for i in range(steps):
                    h, t = divmod(i, NT)
                    if i + 1 < steps:
                        maxima(i + 1)
                    if t == 1 and h + 1 < HALF:
                        keep_keys(h + 1)
                    if i:
                        outputs(i - 1)
                outputs(steps - 1)
                g.done(ch, "dve")


class Heads:
    pass


def stream_tile(g, name):
    ctx = ExitStack()
    return ctx, ctx.enter_context(g.nc.sbuf_tensor(name, [P, NT, D], F32, side="right"))


def layer_ab(g):
    nc = g.nc
    a = Heads()
    with ExitStack() as c_o:
        with ExitStack() as c_gdn:
            with ExitStack() as c_gla:
                with ExitStack() as c_h:
                    hh, hl = (c_h.enter_context(nc.sbuf_tensor(n, [P, KT, TOK], F32R)) for n in ("ab_hh", "ab_hl"))
                    phase_norm(g, 0, hh, hl, None, None, N_AB)
                    sb = lambda n, sh, c: c.enter_context(nc.sbuf_tensor(n, sh, F32, side="right"))
                    a.gb = sb("gdn_gb", [P, NT, 2 * NH], c_gdn)
                    a.gam = sb("gdn_gam", [P, NT, NH], c_gdn)
                    a.qkvT = sb("gdn_qkvT", [P, 3 * NH, NT * P], c_gdn)
                    a.qk2 = sb("gla_qk", [P, NT, 2, 2, P], c_gla)
                    a.b2 = sb("gla_b", [P, NT, 2, P], c_gla)
                    a.v = sb("gla_v", [P, NT, GH * GDV], c_gla)
                    phase_ab_project(g, a, hh, hl)
                o = c_o.enter_context(nc.sbuf_tensor("ab_o", [P, NT, D], F32))
                phase_gla(g, a, o)
            a.xt = sb("gdn_xt", [P, NT, NH, P], c_gdn)
            phase_gdn_inverse(g, a)
            phase_gdn(g, a, o)
        c_x, x = stream_tile(g, "x_1")
        phase_out(g, 0, o, x, N_ABO, True)
    return c_x, x


def layer_mla(g, c_x, x):
    nc = g.nc
    with ExitStack() as c_o:
        with ExitStack() as c_m:
            sb = lambda n, sh, c: c.enter_context(nc.sbuf_tensor("mla_" + n, sh, F32, side="right"))
            m = Heads()
            with ExitStack() as c_h:
                hT = c_h.enter_context(nc.sbuf_tensor("mla_hT", [P, KT, TOK], F32))
                phase_norm(g, 2, hT, None, None, x, N_MLA)
                c_x.close()
                m.cqT = sb("cqT", [P, QR // P, TOK], c_m)
                m.ckvT = sb("ckvT", [P, KVR // P, KEYS], c_m)
                m.kT = sb("kT", [QW, 2, KEYS], c_m)
                m.v = sb("v", [P, NK, MH * MV], c_m)
                phase_mla_project(g, m, hT)
            o = c_o.enter_context(nc.sbuf_tensor("mla_o", [P, NT, D], F32))
            m.q = sb("q", [P, NT, HALF * QW], c_m)
            for hf in range(2):
                phase_mla_queries(g, m, hf)
                phase_mla_attend(g, m, hf, o)
        c_x, x = stream_tile(g, "x_3")
        phase_out(g, 2, o, x, N_MLA + 5, False)
    return c_x, x


def layer_moe(g, l, c_x, x):
    nc = g.nc
    s = 2 * l + 1
    with ExitStack() as ctx:
        rt = Routes(nc, ctx, l)
        with ExitStack() as c2:
            hT = c2.enter_context(nc.sbuf_tensor(f"hT_{s}", [P, KT, TOK], F32))
            h = c2.enter_context(nc.sbuf_tensor(f"h_{s}", [P, NT, D], F32))
            phase_norm(g, s, hT, None, h, x, N_MOE[l], rt.logits)
            c_x.close()
        phase_route(g, l, rt)
        phase_experts(g, l, rt)
        phase_more(g, l, rt)
        c_x, x = stream_tile(g, f"x_{s + 1}")
        phase_combine(g, s, rt, x, l == 1)
    return c_x, x


OUTS = [("y_prompt", (1, SEQ, D)), ("y_sample", (1, DSEQ, D)),
        ("gla_prompt", (1, 1, GH, GDK, GDV)), ("gdn_prompt", (1, 1, NH, DK, DV)),
        ("conv_prompt", (1, 1, CW - 1, CONV)), ("ckv_prompt", (1, 1, SEQ, KVR)), ("krope_prompt", (1, 1, SEQ, ROPE)),
        ("gla_sample", (1, 1, GH, GDK, GDV)), ("gdn_sample", (1, 1, NH, DK, DV)),
        ("conv_sample", (1, 1, CW - 1, CONV)), ("ckv_sample", (1, 1, DSEQ, KVR)), ("krope_sample", (1, 1, DSEQ, ROPE))]
SCRATCH = [("mod", (4, 2, 3 * D)), ("hrow", (TOK, D)), ("yrow", (2 * TOK, D)), ("gates", (TOK, D)),
           ("xres", (3, TOK, D))]


def build(nc, io):
    with ExitStack() as ctx:
        g = Prog(nc, ctx, io)
        g.plan = make_plan(io)
        phase_modulation(g)
        x = layer_ab(g)
        x = layer_moe(g, 0, *x)
        x = layer_mla(g, *x)
        c_x, _ = layer_moe(g, 1, *x)
        c_x.close()


def kernel(**inputs):
    import concourse.bacc as bacc
    from concourse.bass_utils import run_bass_kernel_spmd

    nc = bacc.Bacc("TRN2", target_bir_lowering=False, num_devices=1)
    data = {name: np.ascontiguousarray(a) for name, a in inputs.items()}
    data["cst"] = constants()
    io = {name: nc.dram_tensor("in_" + name, a.shape, F32, kind="ExternalInput").ap() for name, a in data.items()}
    for names, kind in ((OUTS, "ExternalOutput"), (SCRATCH, "Internal")):
        for name, shape in names:
            io[name] = nc.dram_tensor("out_" + name if kind == "ExternalOutput" else name, shape, F32, kind=kind).ap()
    build(nc, io)
    r = run_bass_kernel_spmd(nc, [{"in_" + name: a for name, a in data.items()}], core_ids=[0])
    return tuple(r.results[0]["out_" + name] for name, _ in OUTS)
```
